# Optimizing a Trainium2 kernel written in Bass

```python
import math
import jax
import jax.numpy as jnp
from jax import lax
import numpy as np

D_MODEL = 2048
BATCH = 1
SEQ = 256
DEPTH = 2
DEC_BATCH = 8
DEC_SEQ = 4
PAST_LEN = 2048
PAGE_SIZE = 128

HEAD_DIM = 128
MIX_WIDTH = D_MODEL
MEM_WIDTH = D_MODEL // 4
MEM_HEADS = MEM_WIDTH // HEAD_DIM
MEM_LEN = 256
TOK_WIDTH = MIX_WIDTH - MEM_WIDTH
NSA_HEADS = TOK_WIDTH // HEAD_DIM
NSA_KV_HEADS = 2
NSA_HPG = NSA_HEADS // NSA_KV_HEADS
NSA_KV = NSA_KV_HEADS * HEAD_DIM
L_CMP = 32
L_SEL = 64
SEL_RATIO = L_SEL // L_CMP
TOP_N = 16
WINDOW = 512
CMP_HIDDEN = 2 * HEAD_DIM
N_BRANCH = 3
SEL_QBLK = 64
WIN_QBLK = 128
FORCED_SCORE = 1e4
GLA_HEADS = 4
GLA_VW = TOK_WIDTH
GLA_KW = TOK_WIDTH // 2
GLA_DV = GLA_VW // GLA_HEADS
GLA_DK = GLA_KW // GLA_HEADS
GATE_RANK = 16
GATE_TAU = 16.0
GLA_CHUNK = 16
D_FF = 4 * D_MODEL
NUM_BUCKETS = 32
MAX_DISTANCE = 128
EPS = 1e-6
N_NSA = (DEPTH + 1) // 2
N_GLA = DEPTH // 2
NSA_IN = TOK_WIDTH + 6 * NSA_KV + N_BRANCH * NSA_HEADS + MEM_WIDTH
GLA_IN = 2 * GLA_KW + 2 * GLA_VW + GATE_RANK + MEM_WIDTH

kernel_name = 'nsa_gla_hybrid_decode_step'

def rms_norm(x, g):
    xf = x.astype(jnp.float32)
    y = xf * lax.rsqrt(jnp.mean(xf * xf, axis=-1, keepdims=True) + EPS)
    return (y * g.astype(jnp.float32)).astype(x.dtype)

def t5_bucket(dist):
    n = jnp.maximum(dist, 0)
    exact = NUM_BUCKETS // 2
    nf = jnp.maximum(n, 1).astype(jnp.float32)
    large = exact + (jnp.log(nf / exact) / math.log(MAX_DISTANCE / exact)
                     * (NUM_BUCKETS - exact)).astype(jnp.int32)
    large = jnp.minimum(large, NUM_BUCKETS - 1)
    return jnp.where(n < exact, n, large)

def masked_softmax(s, valid):
    s = jnp.where(valid, s.astype(jnp.float32), -jnp.inf)
    m = jnp.max(s, axis=-1, keepdims=True)
    m = jnp.where(jnp.isfinite(m), m, 0.0)
    e = jnp.exp(s - m)
    return e / jnp.maximum(jnp.sum(e, axis=-1, keepdims=True), 1e-30)

def group_bias(table, bucket):
    tab = table.reshape(NUM_BUCKETS, NSA_KV_HEADS, NSA_HPG)
    bias = jax.vmap(lambda t, bk: t[bk], in_axes=(1, 1), out_axes=1)(tab, bucket)
    return jnp.moveaxis(bias, -1, 2)

def nsa_compress(rows, pe, w1, b1, w2):
    b, t, g, d = rows.shape
    nc = t // L_CMP
    blk = rows[:, :nc * L_CMP].reshape(b, nc, L_CMP, g, d) + pe[:, None, :].astype(rows.dtype)
    flat = jnp.moveaxis(blk, 3, 2).reshape(b, nc, g, L_CMP * d)
    return jax.nn.silu(flat @ w1 + b1) @ w2

def nsa_attention(q, q_pos, rows, win_k, win_v, win_kpos, gates, table, g_k, pe, w1, b1, w2):
    b, l, _, d = q.shape
    g, hpg = NSA_KV_HEADS, NSA_HPG
    scale = HEAD_DIM ** -0.5
    qg = q.reshape(b, l, g, hpg, d)
    kc = rms_norm(nsa_compress(rows[:, :, 0], pe[0], w1[0], b1[0], w2[0]), g_k[0])
    vc = nsa_compress(rows[:, :, 1], pe[1], w1[1], b1[1], w2[1])
    nc = kc.shape[1]
    dist_c = q_pos[:, None] - ((jnp.arange(nc) + 1) * L_CMP - 1)[None, :]
    bias_c = table[t5_bucket(dist_c)].reshape(l, nc, g, hpg).transpose(2, 3, 0, 1)
    s_c = jnp.einsum('blghd,bcgd->bghlc', qg, kc).astype(jnp.float32) * scale + bias_c
    p_c = masked_softmax(s_c, dist_c >= 0)
    o_cmp = jnp.einsum('bghlc,bcgd->blghd', p_c.astype(vc.dtype), vc)
    t = rows.shape[1]
    nsel = -(-t // L_SEL)
    n_top = min(TOP_N, nsel)
    ps = jnp.pad(jnp.sum(p_c, axis=2), ((0, 0), (0, 0), (0, 0), (0, nsel * SEL_RATIO - nc)))
    ps = ps.reshape(b, g, l, nsel, SEL_RATIO).sum(-1)
    ids = jnp.arange(nsel)[None, :]
    cur = (q_pos // L_SEL)[:, None]
    forced = (ids == 0) | (ids == cur) | (ids == cur - 1)
    score = jnp.where(forced, FORCED_SCORE, ps)
    score = jnp.where(ids * L_SEL <= q_pos[:, None], score, -jnp.inf)
    top_val, top_idx = lax.top_k(score, n_top)
    top_ok = jnp.isfinite(top_val)
    pad = nsel * L_SEL - t
    ks = jnp.pad(rms_norm(rows[:, :, 2], g_k[1]), ((0, 0), (0, pad), (0, 0), (0, 0)))
    vs = jnp.pad(rows[:, :, 3], ((0, 0), (0, pad), (0, 0), (0, 0)))
    kb = jnp.moveaxis(ks.reshape(b, nsel, L_SEL, g, d), 3, 1).reshape(b * g, nsel, L_SEL, d)
    vb = jnp.moveaxis(vs.reshape(b, nsel, L_SEL, g, d), 3, 1).reshape(b * g, nsel, L_SEL, d)
    take = jax.vmap(lambda blocks, i: blocks[i])

    def sel_block(args):
        qb, pb, ib, okb = args
        lq = ib.shape[2]
        flat = ib.reshape(b * g, lq * n_top)
        kg = take(kb, flat).reshape(b, g, lq, n_top * L_SEL, d)
        vg = take(vb, flat).reshape(b, g, lq, n_top * L_SEL, d)
        kpos = (ib[..., None] * L_SEL + jnp.arange(L_SEL)).reshape(b, g, lq, n_top * L_SEL)
        dist = pb[None, None, :, None] - kpos
        valid = (dist >= 0) & jnp.repeat(okb, L_SEL, axis=-1)
        s = (jnp.einsum('bqghd,bgqkd->bghqk', qb, kg).astype(jnp.float32) * scale
             + group_bias(table, t5_bucket(dist)))
        p = masked_softmax(s, valid[:, :, None])
        return jnp.einsum('bghqk,bgqkd->bqghd', p.astype(vg.dtype), vg)

    if l > SEL_QBLK and l % SEL_QBLK == 0:
        nq = l // SEL_QBLK
        o_sel = lax.map(sel_block, (
            jnp.swapaxes(qg.reshape(b, nq, SEL_QBLK, g, hpg, d), 0, 1),
            q_pos.reshape(nq, SEL_QBLK),
            top_idx.reshape(b, g, nq, SEL_QBLK, n_top).transpose(2, 0, 1, 3, 4),
            top_ok.reshape(b, g, nq, SEL_QBLK, n_top).transpose(2, 0, 1, 3, 4)))
        o_sel = jnp.swapaxes(o_sel, 0, 1).reshape(b, l, g, hpg, d)
    else:
        o_sel = sel_block((qg, q_pos, top_idx, top_ok))
    kw = rms_norm(win_k, g_k[2])
    nb, kblk = win_kpos.shape
    qblk = l // nb
    qp = q_pos.reshape(nb, qblk)
    dist_w = qp[:, :, None] - win_kpos[:, None, :]
    valid_w = (dist_w >= 0) & (dist_w < WINDOW) & (win_kpos[:, None, :] >= 0)
    bias_w = table[t5_bucket(dist_w)].reshape(nb, qblk, kblk, g, hpg).transpose(3, 4, 0, 1, 2)
    s_w = (jnp.einsum('bnqghd,bnkgd->bghnqk', qg.reshape(b, nb, qblk, g, hpg, d), kw)
           .astype(jnp.float32) * scale + bias_w)
    p_w = masked_softmax(s_w, valid_w)
    o_win = jnp.einsum('bghnqk,bnkgd->bnqghd', p_w.astype(win_v.dtype), win_v).reshape(b, l, g, hpg, d)
    gt = gates.reshape(b, l, N_BRANCH, g, hpg, 1)
    o = gt[:, :, 0] * o_cmp + gt[:, :, 1] * o_sel + gt[:, :, 2] * o_win
    return o.reshape(b, l, NSA_HEADS * d)

def band_blocks(win):
    l = win.shape[1]
    qb = min(WIN_QBLK, l)
    nb = l // qb
    padded = jnp.pad(win, ((0, 0), (WINDOW, 0), (0, 0), (0, 0), (0, 0)))
    idx = jnp.arange(nb)[:, None] * qb + jnp.arange(WINDOW + qb)[None, :]
    blk = padded[:, idx]
    return blk[:, :, :, 0], blk[:, :, :, 1], idx - WINDOW

def nsa_split(proj, gate_b):
    b, l, _ = proj.shape
    o = 0
    q = proj[..., o:o + TOK_WIDTH].reshape(b, l, NSA_HEADS, HEAD_DIM)
    o += TOK_WIDTH
    rows = proj[..., o:o + 4 * NSA_KV].reshape(b, l, 4, NSA_KV_HEADS, HEAD_DIM)
    o += 4 * NSA_KV
    win = proj[..., o:o + 2 * NSA_KV].reshape(b, l, 2, NSA_KV_HEADS, HEAD_DIM)
    o += 2 * NSA_KV
    gates = jax.nn.sigmoid(proj[..., o:o + N_BRANCH * NSA_HEADS] + gate_b).reshape(b, l, N_BRANCH, NSA_HEADS)
    o += N_BRANCH * NSA_HEADS
    qm = proj[..., o:o + MEM_WIDTH].reshape(b, l, MEM_HEADS, HEAD_DIM)
    return q, rows, win, gates, qm

def gla_split(proj):
    b, l, _ = proj.shape
    o = 0
    q = proj[..., o:o + GLA_KW].reshape(b, l, GLA_HEADS, GLA_DK)
    o += GLA_KW
    k = proj[..., o:o + GLA_KW].reshape(b, l, GLA_HEADS, GLA_DK)
    o += GLA_KW
    v = proj[..., o:o + GLA_VW].reshape(b, l, GLA_HEADS, GLA_DV)
    o += GLA_VW
    a = proj[..., o:o + GATE_RANK]
    o += GATE_RANK
    r = proj[..., o:o + GLA_VW]
    o += GLA_VW
    qm = proj[..., o:o + MEM_WIDTH].reshape(b, l, MEM_HEADS, HEAD_DIM)
    return q, k, v, a, r, qm

def gla_scan(q, k, v, log_a, s0):
    b, l, h, _ = q.shape
    dv = v.shape[-1]
    c = GLA_CHUNK if l % GLA_CHUNK == 0 else l
    n = l // c

    def chunks(t):
        return jnp.swapaxes(jnp.moveaxis(t.astype(jnp.float32).reshape(b, n, c, h, t.shape[-1]), 1, 0), 2, 3)

    tril = jnp.tril(jnp.ones((c, c), bool))

    def step(s, inp):
        qc, kc, vc, ac = inp
        bc = jnp.cumsum(ac, axis=2)
        o_inter = jnp.einsum('bhcd,bhde->bhce', qc * jnp.exp(bc), s)
        diff = bc[:, :, :, None, :] - bc[:, :, None, :, :]
        decay = jnp.exp(jnp.where(tril[:, :, None], diff, -jnp.inf))
        att = jnp.einsum('bhid,bhjd,bhijd->bhij', qc, kc, decay)
        o_intra = jnp.einsum('bhij,bhje->bhie', att, vc)
        last = bc[:, :, -1:, :]
        s_new = (jnp.exp(last[:, :, 0, :, None]) * s
                 + jnp.einsum('bhcd,bhce->bhde', kc * jnp.exp(last - bc), vc))
        return s_new, o_inter + o_intra

    s_fin, o = lax.scan(step, s0.astype(jnp.float32), (chunks(q), chunks(k), chunks(v), chunks(log_a)))
    o = jnp.moveaxis(jnp.swapaxes(o, 2, 3), 0, 1).reshape(b, l, h, dv)
    return o.astype(v.dtype), s_fin.astype(s0.dtype)

def gla_mixer(q, k, v, a_lr, r, s0, w_a2, b_a, g_o):
    b, l = q.shape[:2]
    log_a = jax.nn.log_sigmoid((a_lr @ w_a2 + b_a).astype(jnp.float32)) / GATE_TAU
    log_a = log_a.reshape(b, l, GLA_HEADS, GLA_DK)
    o, s = gla_scan(q * GLA_DK ** -0.5, k, v, log_a, s0)
    o = rms_norm(o, g_o).reshape(b, l, GLA_VW) * jax.nn.silu(r)
    return o, s

def mem_attention(qm, mem_kv, g_q, g_k):
    b, l = qm.shape[:2]
    q = rms_norm(qm, g_q)
    k = rms_norm(mem_kv[:, :, 0], g_k)
    v = mem_kv[:, :, 1]
    s = jnp.einsum('blhd,bmhd->bhlm', q, k).astype(jnp.float32) * HEAD_DIM ** -0.5
    p = jax.nn.softmax(s, axis=-1)
    return jnp.einsum('bhlm,bmhd->blhd', p.astype(v.dtype), v).reshape(b, l, MEM_WIDTH)

def sq_relu_mlp(h, w_up, w_down):
    return jnp.square(jax.nn.relu(h @ w_up)) @ w_down

def setup_inputs(seed: int = 0) -> dict:
    key = jax.random.key(seed)
    keys = iter(jax.random.split(key, 40))

    def nrm(shape, scale):
        return jax.random.normal(next(keys), shape, jnp.float32) * scale

    def gain(shape):
        return 1.0 + nrm(shape, 0.05)

    n_pages = PAST_LEN // PAGE_SIZE
    n_pool = (DEC_BATCH * n_pages * 5) // 4
    perm = jax.random.permutation(next(keys), n_pool)
    page_table = perm[:DEC_BATCH * n_pages].reshape(DEC_BATCH, n_pages).astype(jnp.int32)
    return {
        'x_prompt': nrm((BATCH, SEQ, D_MODEL), 1.0),
        'x_sample': nrm((DEC_BATCH, DEC_SEQ, D_MODEL), 1.0),
        'cache_nsa_kv': nrm((N_NSA, n_pool, PAGE_SIZE, 4, NSA_KV_HEADS, HEAD_DIM), 1.0),
        'state_nsa_win': nrm((N_NSA, DEC_BATCH, min(WINDOW, PAST_LEN), 2, NSA_KV_HEADS, HEAD_DIM), 1.0),
        'state_gla': nrm((N_GLA, DEC_BATCH, GLA_HEADS, GLA_DK, GLA_DV), 0.5),
        'cache_mem_kv': nrm((DEPTH, DEC_BATCH, MEM_LEN, 2, MEM_HEADS, HEAD_DIM), 1.0),
        'page_table': page_table,
        'mem_prompt': nrm((BATCH, MEM_LEN, D_MODEL), 1.0),
        'rel_bias': nrm((NUM_BUCKETS, NSA_HEADS), 0.5),
        'g_mix': gain((DEPTH, D_MODEL)),
        'g_mlp': gain((DEPTH, D_MODEL)),
        'g_mem': gain((DEPTH, D_MODEL)),
        'w_mem_kv': nrm((DEPTH, D_MODEL, 2 * MEM_WIDTH), D_MODEL ** -0.5),
        'g_mem_q': gain((DEPTH, HEAD_DIM)),
        'g_mem_k': gain((DEPTH, HEAD_DIM)),
        'w_out': nrm((DEPTH, MIX_WIDTH, D_MODEL), MIX_WIDTH ** -0.5),
        'w_up': nrm((DEPTH, D_MODEL, D_FF), D_MODEL ** -0.5),
        'w_down': nrm((DEPTH, D_FF, D_MODEL), D_FF ** -0.5),
        'nsa_w_in': nrm((N_NSA, D_MODEL, NSA_IN), D_MODEL ** -0.5),
        'nsa_gate_b': nrm((N_NSA, N_BRANCH * NSA_HEADS), 0.1),
        'nsa_g_q': gain((N_NSA, HEAD_DIM)),
        'nsa_g_k': gain((N_NSA, N_BRANCH, HEAD_DIM)),
        'nsa_cmp_pe': nrm((N_NSA, 2, L_CMP, HEAD_DIM), 0.1),
        'nsa_cmp_w1': nrm((N_NSA, 2, L_CMP * HEAD_DIM, CMP_HIDDEN), (L_CMP * HEAD_DIM) ** -0.5),
        'nsa_cmp_b1': nrm((N_NSA, 2, CMP_HIDDEN), 0.02),
        'nsa_cmp_w2': nrm((N_NSA, 2, CMP_HIDDEN, HEAD_DIM), CMP_HIDDEN ** -0.5),
        'gla_w_in': nrm((N_GLA, D_MODEL, GLA_IN), D_MODEL ** -0.5),
        'gla_w_a2': nrm((N_GLA, GATE_RANK, GLA_KW), GATE_RANK ** -0.5),
        'gla_b_a': nrm((N_GLA, GLA_KW), 0.1),
        'gla_g_o': gain((N_GLA, GLA_DV)),
    }

def reference(x_prompt, x_sample, cache_nsa_kv, state_nsa_win, state_gla, cache_mem_kv, page_table,
              mem_prompt, rel_bias, g_mix, g_mlp, g_mem, w_mem_kv, g_mem_q, g_mem_k, w_out, w_up, w_down,
              nsa_w_in, nsa_gate_b, nsa_g_q, nsa_g_k, nsa_cmp_pe, nsa_cmp_w1, nsa_cmp_b1, nsa_cmp_w2,
              gla_w_in, gla_w_a2, gla_b_a, gla_g_o):
    bp, lp, _ = x_prompt.shape
    bs, ls, _ = x_sample.shape
    past = page_table.shape[1] * PAGE_SIZE
    pos_p = jnp.arange(lp, dtype=jnp.int32)
    pos_s = past + jnp.arange(ls, dtype=jnp.int32)
    yp, ys = x_prompt, x_sample
    nsa_kv_p, nsa_win_p, gla_p, mem_kv_p = [], [], [], []
    nsa_kv_s, nsa_win_s, gla_s = [], [], []
    for i in range(DEPTH):
        j = i // 2
        hp = rms_norm(yp, g_mix[i])
        hs = rms_norm(ys, g_mix[i])
        mkv_p = (rms_norm(mem_prompt, g_mem[i]) @ w_mem_kv[i]).reshape(bp, MEM_LEN, 2, MEM_HEADS, HEAD_DIM)
        mkv_s = cache_mem_kv[i]
        mem_kv_p.append(mkv_p)
        if i % 2 == 0:
            nsa_w = (nsa_g_k[j], nsa_cmp_pe[j], nsa_cmp_w1[j], nsa_cmp_b1[j], nsa_cmp_w2[j])
            q, rows, win, gates, qm_p = nsa_split(hp @ nsa_w_in[j], nsa_gate_b[j])
            wk, wv, wpos = band_blocks(win)
            mix_p = nsa_attention(rms_norm(q, nsa_g_q[j]), pos_p, rows, wk, wv, wpos, gates, rel_bias, *nsa_w)
            nsa_kv_p.append(rows)
            nsa_win_p.append(win[:, -min(WINDOW, lp):])
            q, rows_new, win_new, gates, qm_s = nsa_split(hs @ nsa_w_in[j], nsa_gate_b[j])
            past_rows = cache_nsa_kv[j][page_table].reshape(bs, past, 4, NSA_KV_HEADS, HEAD_DIM)
            rows_all = jnp.concatenate([past_rows, rows_new.astype(past_rows.dtype)], axis=1)
            wcat = jnp.concatenate([state_nsa_win[j], win_new.astype(state_nsa_win.dtype)], axis=1)
            wb = state_nsa_win.shape[2]
            wpos = (past - wb + jnp.arange(wb + ls, dtype=jnp.int32))[None]
            mix_s = nsa_attention(rms_norm(q, nsa_g_q[j]), pos_s, rows_all, wcat[:, None, :, 0],
                                  wcat[:, None, :, 1], wpos, gates, rel_bias, *nsa_w)
            nsa_kv_s.append(rows_new)
            nsa_win_s.append(wcat[:, -min(WINDOW, wb + ls):])
        else:
            gw = (gla_w_a2[j], gla_b_a[j], gla_g_o[j])
            q, k, v, a, r, qm_p = gla_split(hp @ gla_w_in[j])
            s0 = jnp.zeros((bp, GLA_HEADS, GLA_DK, GLA_DV), yp.dtype)
            mix_p, st_p = gla_mixer(q, k, v, a, r, s0, *gw)
            gla_p.append(st_p)
            q, k, v, a, r, qm_s = gla_split(hs @ gla_w_in[j])
            mix_s, st_s = gla_mixer(q, k, v, a, r, state_gla[j], *gw)
            gla_s.append(st_s)
        att_p = jnp.concatenate([mix_p, mem_attention(qm_p, mkv_p, g_mem_q[i], g_mem_k[i])], axis=-1)
        att_s = jnp.concatenate([mix_s, mem_attention(qm_s, mkv_s, g_mem_q[i], g_mem_k[i])], axis=-1)
        yp = yp + att_p @ w_out[i]
        ys = ys + att_s @ w_out[i]
        yp = yp + sq_relu_mlp(rms_norm(yp, g_mlp[i]), w_up[i], w_down[i])
        ys = ys + sq_relu_mlp(rms_norm(ys, g_mlp[i]), w_up[i], w_down[i])
    nsa_kv_prompt = jnp.stack(nsa_kv_p)
    nsa_win_prompt = jnp.stack(nsa_win_p)
    gla_prompt = jnp.stack(gla_p)
    mem_kv_prompt = jnp.stack(mem_kv_p)
    nsa_kv_sample = jnp.stack(nsa_kv_s)
    nsa_win_sample = jnp.stack(nsa_win_s)
    gla_sample = jnp.stack(gla_s)
    return (yp, ys, nsa_kv_prompt, nsa_win_prompt, gla_prompt, mem_kv_prompt, nsa_kv_sample, nsa_win_sample, gla_sample)


_drawn_inputs = setup_inputs


def setup_inputs(seed=0):
    import zlib

    import numpy as np

    out = dict(_drawn_inputs(seed))
    spreads = {}
    factors = {'g_mem_q': 8.0,
     'g_mem_k': 8.0,
     'nsa_gate_b': 4.337,
     'nsa_g_q': 6.344,
     'nsa_g_k': 6.025,
     'nsa_cmp_b1': 4.169,
     'gla_g_o': 3.597}
    for name, (base, spread) in spreads.items():
        noise = np.random.default_rng([zlib.crc32(name.encode()), seed]).standard_normal(out[name].shape)
        drawn = base * np.exp(spread * noise) if base else spread * noise
        out[name] = jnp.asarray(drawn.astype(out[name].dtype))
    for name, factor in factors.items():
        out[name] = (out[name] * factor).astype(out[name].dtype)
    return out
```

```python
from contextlib import ExitStack

import numpy as np

import concourse.bass as bass
from concourse import mybir

F32 = mybir.dt.float32
I32 = mybir.dt.int32
ALU = mybir.AluOpType
ACT = mybir.ActivationFunctionType
AX_X = mybir.AxisListType.X

P = 128
D_MODEL = 2048
KT = D_MODEL // P
SEQ = 256
QT = SEQ // P
BATCH = 8
STEP = 4
SAMPLED = BATCH * STEP
TOKENS = SEQ + SAMPLED
PAST = 2048
PAGE = 128
PAGES = PAST // PAGE
HD = 128
HEADS = 12
GROUPS = 2
HPG = HEADS // GROUPS
MEM_HEADS = 4
MEM_LEN = 256
MEM_WIDTH = MEM_HEADS * HD
WINDOW = 512
CMP_LEN = 32
CMP_PER_PAGE = PAGE // CMP_LEN
CMP_BLOCKS = PAST // CMP_LEN
CMP_PROMPT = SEQ // CMP_LEN
CMP_HIDDEN = 256
SEL_LEN = 64
SEL_BLOCKS = PAST // SEL_LEN + 1
BRANCHES = 3
BUCKETS = 32
D_FF = 8192
FT = D_FF // P
GLA_HEADS = 4
GLA_DK = 192
GLA_DV = 384
GLA_KW = GLA_HEADS * GLA_DK
GLA_KT = GLA_KW // P
GLA_VW = GLA_HEADS * GLA_DV
GATE_RANK = 16
GATE_TAU = 16.0
EPS = 1e-6
MASKED = -1e30
SCALE = HD ** -0.5

RING = 4
WCOLS = 512
WTILES = 4
PAIRS = BATCH // 2

VEC = {}
_at = 0
for _name, _rows in (("g_mix", 2 * KT), ("g_mlp", 2 * KT), ("g_mem", 2 * KT), ("g_mem_q", 2), ("g_mem_k", 2),
                     ("nsa_g_q", 1), ("nsa_g_k", 3), ("cmp_b1", 4), ("gla_b_a", GLA_KT), ("gla_g_o", 3)):
    VEC[_name] = _at
    _at += _rows
VECS = _at

DIST0 = 255
DISTS = 512


def shape_constants():
    dist = DIST0 - np.arange(DISTS)
    n = np.maximum(dist, 0)
    large = 16 + (np.log(np.maximum(n, 1) / 16.0) / np.log(8.0) * 16).astype(np.int64)
    bucket = np.where(n < 16, n, np.minimum(large, BUCKETS - 1))
    onehot = np.zeros((BUCKETS + 1, DISTS), np.float32)
    onehot[bucket[dist >= 0], np.arange(DISTS)[dist >= 0]] = 1.0
    onehot[BUCKETS, dist < 0] = MASKED

    row = np.arange(P)
    block, hh, pos = row // 32, row % 32 // STEP, row % STEP
    same = ((block[:, None] == block[None]) & (pos[:, None] == pos[None])
            & (hh[:, None] < HPG) & (hh[None] < HPG)).astype(np.float32)
    wrong_group = np.where(block[:, None] % 2 == np.arange(P)[None] // CMP_BLOCKS, 0.0, MASKED)
    too_old = np.where(np.arange(32)[None] <= pos[:, None], MASKED, 0.0)
    token_of = np.arange(SAMPLED) // STEP
    other = np.stack([np.where(token_of[None] == 2 * t + (block // 2)[:, None], 0.0, MASKED)
                      for t in range(PAIRS)], 1).reshape(P, -1)
    own = (np.arange(2 * STEP)[None] == (block // 2 * STEP + pos)[:, None]) & (hh < HPG)[:, None]
    at = pos[:, None] == np.arange(STEP)[None]
    flip = np.eye(P)[::-1]
    sparse = np.concatenate([same, wrong_group, too_old, other, own, at, flip], 1).astype(np.float32)
    head = block % 2 * HPG + hh
    gate_rows = np.concatenate([np.arange(BRANCHES * HEADS)[:, None] == (r * HEADS + head)[None]
                                for r in range(BRANCHES)], 1) & np.tile(hh < HPG, BRANCHES)[None]

    i = np.arange(P)
    level = [(i[:, None] == i[None])]
    s = 1
    while s < P:
        level.append((i[:, None] // (2 * s) == i[None] // (2 * s)) & (i[:, None] // s % 2 == 0)
                     & (i[None] // s % 2 == 1))
        s *= 2
    batch_rows = i[:, None] // STEP == np.arange(BATCH)[None]
    batch_tokens = np.repeat(np.eye(BATCH), STEP, 1).reshape(1, -1) * np.ones((P, 1))
    linear = np.concatenate(level + [batch_rows, batch_tokens], 1).astype(np.float32)
    return onehot, sparse, gate_rows.astype(np.float32), linear


LEVELS = 8
SP_SAME, SP_GROUP, SP_OLD, SP_OTHER = 0, P, 2 * P, 2 * P + 32
SP_OWN = SP_OTHER + PAIRS * SAMPLED
SP_AT = SP_OWN + 2 * STEP
SP_FLIP = SP_AT + STEP
SP_COLS = SP_FLIP + P
LIN_ROWS = LEVELS * P
LIN_TOKENS = LIN_ROWS + BATCH
LIN_COLS = LIN_TOKENS + BATCH * SAMPLED


class Names:
    pass


class Chain:

    def __init__(self, eng, sem, base=0):
        self.eng, self.sem, self.base, self.n = eng, sem, base, 0

    def __call__(self, ins):
        self.n += 1
        ins.then_inc(self.sem, 1)
        self.eng.wait_ge(self.sem, self.base + self.n)




def wait(eng, sem, value):
    if not isinstance(value, int) or value > 0:
        eng.wait_ge(sem, value)


HELD = []


def counters(nc, ctx, tag):
    used = []

    def clear():
        numbers = [s.num for s in used]
        nc.clear_and_free_semaphores(used)
        for held in HELD:
            nc.release_semaphore(held)
        HELD[:] = [nc.alloc_semaphore(f"held_{tag}{n}", num=n) for n in numbers]

    ctx.callback(clear)

    def sem(name):
        used.append(nc.alloc_semaphore(tag + name))
        return used[-1]
    return sem



def chunks_of(w, first_col=0):
    tiled = w.rearrange("(c k p) n -> c p k n", k=WTILES, p=P)
    return lambda n, c: tiled[c][:, :, bass.ds(n * WCOLS + first_col, WCOLS)]


def load_first_chunks(sp, g, src, base):
    for b in range(RING):
        if base:
            sp.wait_ge(g.weights_used, base + b - RING + 1)
        sp.dma_start(g.ring[:, b], src(0, b)).then_inc(g.weights_loaded[b], 16)


def load_other_chunks(sp, g, src, base, groups, chunks, late=(0, None)):
    for c in range(RING, chunks):
        sp.wait_ge(g.weights_used, base + c - RING + 1)
        sp.dma_start(g.ring[:, c % RING], src(0, c)).then_inc(g.weights_loaded[c % RING], 16)
    late, late_source = late

    def group(n, source):
        for c in range(chunks):
            sp.wait_ge(g.weights_used, n * chunks + (base + c - RING + 1))
            sp.dma_start(g.ring[:, c % RING], source(n, c)).then_inc(g.weights_loaded[c % RING], 16)

    if groups - late > 1:
        with sp.Fori(1, groups - late) as n:
            group(n, src)
    if late > 1:
        with sp.Fori(groups - late, groups) as n:
            group(n, late_source)
    elif late:
        group(groups - 1, late_source)


def project(nc, g, base, groups, k_tiles, moving, src, then, next_chunks=None, late=(0, None)):
    chunks = k_tiles // WTILES
    loads = chunks // RING
    kind, out = then
    with ExitStack() as ctx:
        banks = ctx.enter_context(nc.psum_tensor(f"project{base}_banks", [P, 2, 4, 512], F32))
        positive = ctx.enter_context(nc.sbuf_tensor(f"project{base}_positive", [P, 2, 4, TOKENS], F32)) \
            if kind == "square relu" else None
        banks_free, squared = map(counters(nc, ctx, f"project{base}_"), ("banks_free", "squared"))
        block = ctx.enter_context(nc.Block())

        @block.sync
        def _(sp):
            load_other_chunks(sp, g, src, base, groups, chunks, late)
            if next_chunks is not None:
                load_first_chunks(sp, g, next_chunks, base + groups * chunks)

        @block.tensor
        def _(pe):
            def group(n, half):
                for c in range(chunks):
                    pe.wait_ge(g.weights_loaded[c % RING],
                               n * (16 * loads) + 16 * (base // RING + c // RING + 1))
                    for k in range(WTILES):
                        kt = c * WTILES + k
                        for o in range(4):
                            mm = nc.tensor.matmul(banks[:, half, o, 0:TOKENS],
                                                  g.ring[:, c % RING, k, o * P:(o + 1) * P], moving[:, kt],
                                                  start=(kt == 0), stop=(kt == k_tiles - 1))
                    mm.then_inc(g.weights_used, 1)

            group(0, 0)
            group(1, 1)
            with pe.Fori(1, groups // 2) as m:
                for half in range(2):
                    pe.wait_ge(banks_free, m * 2 + (half - 1))
                    group(m * 2 + half, half)
            if groups % 2:
                pe.wait_ge(banks_free, groups - 2)
                group(groups - 1, 0)

        @block.scalar
        def _(act):
            if kind == "add":
                return

            def group(n, half):
                act.wait_ge(g.weights_used, n * chunks + (base + chunks))
                if kind == "copy":
                    nc.scalar.activation(out[:, bass.ds(n * 4, 4)], banks[:, half, :, 0:TOKENS],
                                         ACT.Copy).then_inc(banks_free, 1)
                else:
                    wait(act, squared, n - 1)
                    nc.scalar.activation(positive[:, half], banks[:, half, :, 0:TOKENS],
                                         ACT.Relu).then_inc(banks_free, 1)

            group(0, 0)
            group(1, 1)
            with act.Fori(1, groups // 2) as m:
                group(m * 2, 0)
                group(m * 2 + 1, 1)
            if groups % 2:
                group(groups - 1, 0)

        @block.vector
        def _(dve):
            if kind == "copy":
                return

            def group(n, half):
                dst = out[:, bass.ds(n * 4, 4)]
                if kind == "add":
                    dve.wait_ge(g.weights_used, n * chunks + (base + chunks))
                    nc.vector.tensor_tensor(dst, banks[:, half, :, 0:TOKENS], dst, ALU.add).then_inc(banks_free, 1)
                else:
                    dve.wait_ge(banks_free, n + 1)
                    nc.vector.tensor_tensor(dst, positive[:, half], positive[:, half], ALU.mult).then_inc(squared, 1)

            with dve.Fori(0, groups // 2) as m:
                group(m * 2, 0)
                group(m * 2 + 1, 1)
    return base + groups * chunks


def normalize(nc, g, tag, gain, narrow=None):
    with ExitStack() as ctx:
        squares = ctx.enter_context(nc.sbuf_tensor(f"norm{tag}_squares", [P, KT, TOKENS], F32))
        rstd = ctx.enter_context(nc.sbuf_tensor(f"norm{tag}_rstd", [P, TOKENS], F32))
        sums = ctx.enter_context(nc.psum_tensor(f"norm{tag}_sums", [P, TOKENS], F32))
        few = ctx.enter_context(nc.psum_tensor(f"norm{tag}_few", [P, 512], F32))
        columns = narrow[2] if narrow else 1
        w_few = ctx.enter_context(nc.sbuf_tensor(f"norm{tag}_w", [P, KT, columns], F32))
        sem = counters(nc, ctx, f"norm{tag}_")
        squared, summed, mean, root, ready, few_loaded, few_done, few_out = map(sem, (
            "squared", "summed", "mean", "root", "ready", "few_loaded", "few_done", "few_out"))
        block = ctx.enter_context(nc.Block())

        @block.sync
        def _(sp):
            if narrow:
                w, col, n, _ = narrow
                sp.dma_start(w_few[:], w.rearrange("(k p) n -> p k n", p=P)[:, :, col:col + n]
                             ).then_inc(few_loaded, 16)

        @block.gpsimd
        def _(pool):
            for t in range(KT):
                if t % 4 == 3:
                    nc.gpsimd.tensor_tensor(squares[:, t], g.x[:, t], g.x[:, t], ALU.mult).then_inc(squared, 1)

        @block.scalar
        def _(act):
            for t in range(KT):
                if t % 4 in (1, 2):
                    nc.scalar.activation(squares[:, t], g.x[:, t], ACT.Square).then_inc(squared, 1)
            act.wait_ge(mean, 1)
            nc.scalar.activation(rstd[:], rstd[:], ACT.Sqrt).then_inc(root, 1)
            if narrow:
                act.wait_ge(few_done, 1)
                nc.scalar.activation(narrow[3][0:narrow[2]], few[0:narrow[2], 0:TOKENS], ACT.Copy).then_inc(few_out, 1)

        @block.tensor
        def _(pe):
            pe.wait_ge(squared, KT)
            for t in range(KT):
                mm = nc.tensor.matmul(sums[:], g.ones[:], squares[:, t], start=(t == 0), stop=(t == KT - 1))
            mm.then_inc(summed, 1)
            if narrow:
                pe.wait_ge(few_loaded, 16)
                for t in range(KT):
                    pe.wait_ge(ready, t + 1)
                    mm = nc.tensor.matmul(few[0:columns, 0:TOKENS], w_few[:, t], g.h[:, t],
                                          start=(t == 0), stop=(t == KT - 1))
                mm.then_inc(few_done, 1)

        @block.vector
        def _(dve):
            for t in range(0, KT, 4):
                nc.vector.tensor_tensor(squares[:, t], g.x[:, t], g.x[:, t], ALU.mult).then_inc(squared, 1)
            dve.wait_ge(summed, 1)
            nc.vector.tensor_scalar(rstd[:], sums[:], 1.0 / D_MODEL, EPS, ALU.mult, ALU.add).then_inc(mean, 1)
            dve.wait_ge(root, 1)
            nc.vector.reciprocal(rstd[:], rstd[:]).then_inc(root, 1)
            dve.wait_ge(root, 2)
            for t in range(KT):
                nc.vector.scalar_tensor_tensor(g.h[:, t], g.x[:, t], g.vec[:, gain + t:gain + t + 1], rstd[:],
                                               ALU.mult, ALU.mult).then_inc(ready, 1)


def load_tokens(nc, g, a):
    with ExitStack() as ctx:
        sb = lambda n, s: ctx.enter_context(nc.sbuf_tensor(n, s, F32))
        sem = counters(nc, ctx, "start_")
        rows = sb("token_rows", [P, QT, D_MODEL])
        sampled = sb("sampled_rows", [SAMPLED, D_MODEL])
        memory = sb("memory_rows", [P, QT, D_MODEL])
        vec_rows = sb("vec_rows", [VECS, P])
        pe_rows = sb("pe_rows", [2 * CMP_LEN, P])
        table = sb("bias_table", [BUCKETS + 1, HEADS])
        onehot = sb("bucket_onehot", [BUCKETS + 1, DISTS])
        bias = sb("bias_by_distance", [HEADS, DISTS])
        scratch = sb("memory_squares", [P, D_MODEL])
        ss = sb("memory_sums", [P, QT])
        banks = ctx.enter_context(nc.psum_tensor("turn_banks", [P, 8, 512], F32))
        ident_cleared, consts, params_loaded, tokens_loaded, memory_loaded, row_ones, turned, copied, mem_copied, \
            mem_squared, mem_mean, mem_root, mem_scaled, bias_stored = map(sem, (
                "ident_cleared", "consts", "params_loaded", "tokens_loaded", "memory_loaded", "row_ones", "turned",
                "copied", "mem_copied", "mem_squared", "mem_mean", "mem_root", "mem_scaled", "bias_stored"))
        block = ctx.enter_context(nc.Block())
        params = [(a.g_mix, "g_mix"), (a.g_mlp, "g_mlp"), (a.g_mem, "g_mem"), (a.g_mem_q, "g_mem_q"),
                  (a.g_mem_k, "g_mem_k"), (a.nsa_g_q, "nsa_g_q"), (a.nsa_g_k, "nsa_g_k"), (a.nsa_cmp_b1, "cmp_b1"),
                  (a.gla_b_a, "gla_b_a"), (a.gla_g_o, "gla_g_o")]

        @block.sync
        def _(sp):
            for ap, name in params:
                names = "abc"[:len(ap.shape)]
                flat = ap.rearrange(f"{' '.join(names)} -> ({' '.join(names)})").rearrange("(r p) -> r p", p=P)
                sp.dma_start(vec_rows[VEC[name]:VEC[name] + flat.shape[0]], flat).then_inc(params_loaded, 16)
            sp.dma_start(pe_rows[:], a.nsa_cmp_pe[0].rearrange("k l d -> (k l) d")).then_inc(params_loaded, 16)
            sp.dma_start(table[0:BUCKETS], a.rel_bias).then_inc(params_loaded, 16)
            sp.dma_start(onehot[:], a.bucket_onehot).then_inc(params_loaded, 16)
            sp.dma_start(g.gate_bias[:], a.nsa_gate_b.rearrange("a n -> n a")).then_inc(params_loaded, 16)
            sp.dma_start(g.pages[:], a.page_table.rearrange("b n -> (b n)").unsqueeze(0)).then_inc(params_loaded, 16)
            load_first_chunks(sp, g, chunks_of(a.w_mem_kv[0]), 0)
            sp.wait_ge(copied, 3)
            sp.dma_start(g.bias_dram, bias[:]).then_inc(bias_stored, 16)
            sp.wait_ge(bias_stored, 16)

        @block.scalar
        def _(act):
            for t in range(QT):
                act.dma_start(memory[:, t], a.mem_prompt[0, t * P:(t + 1) * P]).then_inc(memory_loaded, 16)
            for t in range(QT):
                act.dma_start(rows[:, t], a.x_prompt[0, t * P:(t + 1) * P]).then_inc(tokens_loaded, 16)
            act.dma_start(sampled[:], a.x_sample.rearrange("b l d -> (b l) d")).then_inc(tokens_loaded, 16)
            act.wait_ge(memory_loaded, 16 * QT)
            for t in range(QT):
                nc.scalar.activation(scratch[:], memory[:, t], ACT.Square,
                                     accum_out=ss[:, t:t + 1]).then_inc(mem_squared, 1)
                act.wait_ge(mem_squared, t + 1)
            act.wait_ge(mem_mean, 1)
            nc.scalar.activation(ss[:], ss[:], ACT.Sqrt).then_inc(mem_root, 1)
            for s in range(KT // 4):
                act.wait_ge(turned, 3 + KT // 4 + s + 1)
                nc.scalar.activation(g.mem[:, 4 * s:4 * s + 4], banks[:, 4 * (s % 2):4 * (s % 2) + 4, 0:MEM_LEN],
                                     ACT.Copy).then_inc(mem_copied, 1)

        @block.gpsimd
        def _(pool):
            nc.gpsimd.memset(g.ident[:], 0.0).then_inc(ident_cleared, 1)
            nc.gpsimd.memset(g.ones[:], 1.0).then_inc(consts, 1)
            pool.wait_ge(ident_cleared, 1)
            nc.gpsimd.affine_select(out=g.ident[:], in_=g.ident[:], compare_op=ALU.not_equal, fill=1.0, base=0,
                                    pattern=[[-1, P]], channel_multiplier=1).then_inc(consts, 1)

        @block.tensor
        def _(pe):
            pe.wait_ge(consts, 2)
            pe.wait_ge(params_loaded, 16 * (len(params) + 5))
            nc.tensor.transpose(banks[:, 0, 0:VECS], vec_rows[:], g.ident[0:VECS, 0:VECS]).then_inc(turned, 1)
            nc.tensor.transpose(banks[:, 1, 0:2 * CMP_LEN], pe_rows[:],
                                g.ident[0:2 * CMP_LEN, 0:2 * CMP_LEN]).then_inc(turned, 1)
            pe.wait_ge(row_ones, 1)
            nc.tensor.matmul(banks[0:HEADS, 2, :], table[:], onehot[:], start=True, stop=True).then_inc(turned, 1)
            pe.wait_ge(tokens_loaded, 16 * (QT + 1))
            pe.wait_ge(copied, 3)
            for s in range(KT // 4):
                if s >= 2:
                    pe.wait_ge(copied, 3 + s - 1)
                for o in range(4):
                    t = 4 * s + o
                    bank = banks[:, 4 * (s % 2) + o]
                    for q in range(QT):
                        nc.tensor.transpose(bank[:, q * P:(q + 1) * P], rows[:, q, t * P:(t + 1) * P], g.ident[:])
                    mm = nc.tensor.transpose(bank[:, SEQ:TOKENS], sampled[:, t * P:(t + 1) * P],
                                             g.ident[0:SAMPLED, 0:SAMPLED])
                mm.then_inc(turned, 1)
            pe.wait_ge(mem_scaled, QT)
            for s in range(KT // 4):
                if s < 2:
                    pe.wait_ge(copied, 3 + KT // 4 + s - 1)
                else:
                    pe.wait_ge(mem_copied, s - 1)
                for o in range(4):
                    t = 4 * s + o
                    for q in range(QT):
                        mm = nc.tensor.transpose(banks[:, 4 * (s % 2) + o, q * P:(q + 1) * P],
                                                 memory[:, q, t * P:(t + 1) * P], g.ident[:])
                mm.then_inc(turned, 1)

        @block.vector
        def _(dve):
            nc.vector.memset(table[BUCKETS:BUCKETS + 1], 1.0).then_inc(row_ones, 1)
            for n, (dst, src) in enumerate(((g.vec[:], banks[:, 0, 0:VECS]), (g.cmp_pe[:], banks[:, 1, 0:2 * CMP_LEN]),
                                            (bias[:], banks[0:HEADS, 2, :]))):
                dve.wait_ge(turned, n + 1)
                nc.vector.tensor_copy(dst, src).then_inc(copied, 1)
            dve.wait_ge(mem_squared, QT)
            nc.vector.tensor_scalar(ss[:], ss[:], 1.0 / D_MODEL, EPS, ALU.mult, ALU.add).then_inc(mem_mean, 1)
            dve.wait_ge(mem_root, 1)
            nc.vector.reciprocal(ss[:], ss[:]).then_inc(mem_root, 1)
            dve.wait_ge(mem_root, 2)
            for t in range(QT):
                nc.vector.tensor_scalar(memory[:, t], memory[:, t], ss[:, t:t + 1], None,
                                        ALU.mult).then_inc(mem_scaled, 1)
            for s in range(KT // 4):
                dve.wait_ge(turned, 3 + s + 1)
                nc.vector.tensor_copy(g.x[:, 4 * s:4 * s + 4], banks[:, 4 * (s % 2):4 * (s % 2) + 4, 0:TOKENS]
                                      ).then_inc(copied, 1)


def store_tokens(nc, g, a):
    with ExitStack() as ctx:
        rows = ctx.enter_context(nc.sbuf_tensor("out_rows", [P, QT + 1, D_MODEL], F32))
        banks = ctx.enter_context(nc.psum_tensor("out_banks", [P, 8, 512], F32))
        turned, copied, stored = map(counters(nc, ctx, "out_"), ("turned", "copied", "stored"))
        block = ctx.enter_context(nc.Block())
        steps = [(q, s) for q in range(QT + 1) for s in range(KT // 4)]
        width = lambda q: P if q < QT else SAMPLED

        @block.tensor
        def _(pe):
            for n, (q, s) in enumerate(steps):
                if n >= 8:
                    pe.wait_ge(copied, n - 7)
                for o in range(4):
                    mm = nc.tensor.transpose(banks[0:width(q), n % 8, o * P:(o + 1) * P],
                                             g.x[:, 4 * s + o, q * P:q * P + width(q)], g.ident[:])
                mm.then_inc(turned, 1)

        @block.vector
        def _(dve):
            for n, (q, s) in enumerate(steps):
                dve.wait_ge(turned, n + 1)
                nc.vector.tensor_copy(rows[0:width(q), q, s * 512:(s + 1) * 512], banks[0:width(q), n % 8, :]
                                      ).then_inc(copied, 1)

        @block.sync
        def _(sp):
            for q in range(QT + 1):
                sp.wait_ge(copied, (q + 1) * (KT // 4))
                dst = a.y_prompt[0, q * P:(q + 1) * P] if q < QT else a.y_sample.rearrange("b l d -> (b l) d")
                sp.dma_start(dst, rows[0:width(q), q]).then_inc(stored, 16)
            sp.wait_ge(stored, 16 * (QT + 1))


def memory_keys_values(nc, g, a, base, layer, next_chunks):
    chunks = KT // WTILES
    with ExitStack() as ctx:
        sb = lambda n, s: ctx.enter_context(nc.sbuf_tensor(f"memkv{layer}_{n}", s, F32))
        sem = counters(nc, ctx, f"memkv{layer}_")
        scaled = sb("scaled", [P, KT, MEM_LEN])
        keys = sb("keys", [P, QT, MEM_WIDTH])
        squares = sb("squares", [P, QT, MEM_WIDTH])
        ss = sb("sums", [P, QT, MEM_HEADS])
        banks = ctx.enter_context(nc.psum_tensor(f"memkv{layer}_banks", [P, 8, 512], F32))
        scaled_done, copied, link, mean, root, keys_scaled, turned, stored = map(sem, (
            "scaled_done", "copied", "link", "mean", "root", "keys_scaled", "turned", "stored"))
        block = ctx.enter_context(nc.Block())
        gain = VEC["g_mem"] + layer * KT
        out = a.mem_kv_prompt[layer, 0].rearrange("m s h d -> m s (h d)")

        @block.sync
        def _(sp):
            load_other_chunks(sp, g, chunks_of(a.w_mem_kv[layer]), base, 2, chunks)
            for part, src in enumerate((keys, g.mem_v[:, layer])):
                sp.wait_ge(copied, 2 * part + 2)
                for t in range(QT):
                    sp.dma_start(out[t * P:(t + 1) * P, part], src[:, t]).then_inc(stored, 16)
            sp.wait_ge(stored, 16 * 2 * QT)
            load_first_chunks(sp, g, next_chunks, base + 2 * chunks)

        @block.tensor
        def _(pe):
            for part in range(2):
                for c in range(chunks):
                    pe.wait_ge(g.weights_loaded[c % RING], 16 * (base // RING + part * chunks // RING + c // RING + 1))
                    for k in range(WTILES):
                        kt = c * WTILES + k
                        if part == 0:
                            pe.wait_ge(scaled_done, kt + 1)
                        for t in range(QT):
                            mm = nc.tensor.matmul(banks[:, 2 * part + t, :], scaled[:, kt, t * P:(t + 1) * P],
                                                  g.ring[:, c % RING, k, :], start=(kt == 0), stop=(kt == KT - 1))
                    mm.then_inc(g.weights_used, 1)
            pe.wait_ge(keys_scaled, 1)
            for h in range(MEM_HEADS):
                for t in range(QT):
                    mm = nc.tensor.transpose(banks[:, 4 + h, t * P:(t + 1) * P], squares[:, t, h * HD:(h + 1) * HD],
                                             g.ident[:])
            mm.then_inc(turned, 1)

        @block.scalar
        def _(act):
            for part in range(2):
                act.wait_ge(g.weights_used, base + (part + 1) * chunks)
                for t in range(QT):
                    dst = (keys if part == 0 else g.mem_v[:, layer])[:, t]
                    nc.scalar.activation(dst, banks[:, 2 * part + t, :], ACT.Copy).then_inc(copied, 1)
                if part == 0:
                    act.wait_ge(mean, 1)
                    nc.scalar.activation(ss[:], ss[:], ACT.Sqrt).then_inc(root, 1)

        @block.vector
        def _(dve):
            for t in range(KT):
                nc.vector.tensor_scalar(scaled[:, t], g.mem[:, t], g.vec[:, gain + t:gain + t + 1], None,
                                        ALU.mult).then_inc(scaled_done, 1)
            dve.wait_ge(copied, 2)
            nc.vector.tensor_tensor(squares[:], keys[:], keys[:], ALU.mult).then_inc(link, 1)
            dve.wait_ge(link, 1)
            nc.vector.tensor_reduce(ss[:], squares[:].rearrange("p t (h d) -> p t h d", d=HD), AX_X, ALU.add
                                    ).then_inc(link, 1)
            dve.wait_ge(link, 2)
            nc.vector.tensor_scalar(ss[:], ss[:], 1.0 / HD, EPS, ALU.mult, ALU.add).then_inc(mean, 1)
            dve.wait_ge(root, 1)
            nc.vector.reciprocal(ss[:], ss[:]).then_inc(link, 1)
            dve.wait_ge(link, 3)
            for t in range(QT):
                mm = nc.vector.tensor_tensor(squares[:, t].rearrange("p (h d) -> p h d", d=HD),
                                             keys[:, t].rearrange("p (h d) -> p h d", d=HD),
                                             ss[:, t].unsqueeze(2).to_broadcast([P, MEM_HEADS, HD]), ALU.mult)
            mm.then_inc(keys_scaled, 1)
            dve.wait_ge(turned, 1)
            gk = VEC["g_mem_k"] + layer
            nc.vector.tensor_scalar(g.mem_k[:, layer], banks[:, 4:8, 0:MEM_LEN], g.vec[:, gk:gk + 1], None, ALU.mult)
    return base + 2 * chunks
CHUNK_PAGES = 4
CHUNKS = PAGES // CHUNK_PAGES
PAIR_COLS = 2 * GROUPS * CMP_BLOCKS
OWN_COLS = GROUPS * CMP_PROMPT // PAIRS
CMP_COLS = PAIR_COLS + OWN_COLS


def compress(nc, g, a, kind):
    with ExitStack() as ctx:
        tag = "cmp_kv"[4 + kind]
        sb = lambda n, s: ctx.enter_context(nc.sbuf_tensor(f"cmp_{tag}_{n}", s, F32))
        ps = lambda n, s: ctx.enter_context(nc.psum_tensor(f"cmp_{tag}_{n}", s, F32))
        sem = counters(nc, ctx, f"cmp_{tag}_")
        stage = g.h[:].rearrange("p k n -> p (k n)")[:, 0:4 * CHUNK_PAGES * GROUPS * HD].rearrange(
            "p (b q n) -> p b q n", b=4, q=CHUNK_PAGES)
        blocks = sb("blocks", [P, 2, CMP_LEN, CMP_COLS])
        w1 = g.ring[:].rearrange("p b k n -> p (b k n)").rearrange("p (j m) -> p j m", m=CMP_HIDDEN)
        w2 = sb("w2", [P, 2, HD])
        neg_b1 = sb("neg_b1", [P, 2])
        e = sb("exp", [P, 2, CMP_COLS])
        hidden = sb("hidden", [P, 2, CMP_COLS])
        own_hidden = sb("own_hidden", [P, 2, GROUPS, CMP_PROMPT])
        squares = blocks[:, 0].rearrange("p j n -> p (j n)")[:, 0:PAIRS * CMP_COLS]
        rows_ps = ps("rows_ps", [P, 2, GROUPS, 512])
        hid_ps = ps("hid_ps", [P, 2, 512])
        out_ps = ps("out_ps", [P, 2, 512])
        stage_loaded = [sem(f"stage_loaded{b}") for b in range(4)]
        w1_loaded, w2_loaded, chunk_turned, chunk_placed, own_placed, hid_done, exp_done, link, hidden_done, \
            out_done, out_copied, b1_neg, squared, summed, mean, root, scaled = map(sem, (
                "w1_loaded", "w2_loaded", "chunk_turned", "chunk_placed", "own_placed", "hid_done", "exp_done",
                "link", "hidden_done", "out_done", "out_copied", "b1_neg", "squared", "summed", "mean", "root",
                "scaled"))
        block = ctx.enter_context(nc.Block())
        per_pair = 2 * CHUNKS
        total = PAIRS * per_pair
        pages = a.cache_nsa_kv[0].rearrange("n r k g d -> n r k (g d)")
        b1 = VEC["cmp_b1"] + 2 * kind
        thirds = [(s, min(512, PAIRS * CMP_COLS - s)) for s in range(0, PAIRS * CMP_COLS, 512)]

        @block.sync
        def _(sp):
            def chunk(n, b, turned=0):
                numbers = [sp.value_load(g.pages[0:1, bass.ds(n * CHUNK_PAGES + q, 1)], min_val=0,
                                         max_val=pages.shape[0] - 1) for q in range(CHUNK_PAGES)]
                wait(sp, chunk_turned, turned)
                for q, page in enumerate(numbers):
                    sp.dma_start(stage[:, b, q], pages[bass.ds(page, 1), :, kind].squeeze(0)
                                 ).then_inc(stage_loaded[b], 16)

            sp.dma_start(w2[:], a.nsa_cmp_w2[0, kind].rearrange("(k p) n -> p k n", p=P)).then_inc(w2_loaded, 16)
            for b in range(4):
                chunk(b, b)
            with sp.Fori(1, total // 4) as m:
                for b in range(4):
                    chunk(m * 4 + b, b, m * 4 + (b - 3))

        @block.gpsimd
        def _(pool):
            nc.gpsimd.tensor_scalar(neg_b1[:], g.vec[:, b1:b1 + 2], -1.0, None, ALU.mult).then_inc(b1_neg, 1)

        @block.scalar
        def _(act):
            for q in range(2):
                half = CMP_LEN // 2
                act.dma_start(w1[:, q * half:(q + 1) * half],
                              a.nsa_cmp_w1[0, kind].rearrange("(j p) m -> p j m", p=P)[:, q * half:(q + 1) * half]
                              ).then_inc(w1_loaded, 16)
            act.wait_ge(b1_neg, 1)
            for t in range(PAIRS):
                act.wait_ge(hid_done, t + 1)
                if t:
                    act.wait_ge(hidden_done, 2 * t)
                for m in range(2):
                    nc.scalar.activation(e[:, m], hid_ps[:, m, 0:CMP_COLS], ACT.Exp, bias=neg_b1[:, m:m + 1],
                                         scale=-1.0).then_inc(exp_done, 1)
                act.wait_ge(out_done, t + 1)
                if kind == 0:
                    nc.scalar.activation(g.cmp_k[:, t], out_ps[:, 0, 0:CMP_COLS], ACT.Copy).then_inc(out_copied, 1)
                else:
                    nc.scalar.activation(g.cmp_v[:, 2 * t:2 * t + 2], out_ps[:, 0, 0:2 * HD].rearrange(
                        "p (b d) -> p b d", b=2), ACT.Copy).then_inc(out_copied, 1)
            if kind == 0:
                act.wait_ge(mean, 1)
                nc.scalar.activation(squares, squares, ACT.Sqrt).then_inc(root, 1)
            else:
                act.wait_ge(out_done, PAIRS + 1)
                nc.scalar.activation(g.cmp_v_prompt[0:CMP_PROMPT], out_ps[0:CMP_PROMPT, 1, 0:GROUPS * HD].rearrange(
                    "p (g d) -> p g d", g=GROUPS), ACT.Copy)

        @block.tensor
        def _(pe):
            def turn_chunk(n):
                b = n % 4
                pe.wait_ge(stage_loaded[b], 16 * CHUNK_PAGES * (n // 4 + 1))
                if n >= 2:
                    pe.wait_ge(chunk_placed, n - 1)
                for h in range(GROUPS):
                    for q in range(CHUNK_PAGES):
                        mm = nc.tensor.transpose(rows_ps[:, n % 2, h, q * PAGE:(q + 1) * PAGE],
                                                 stage[:, b, q, h * HD:(h + 1) * HD], g.ident[:])
                mm.then_inc(chunk_turned, 1)

            def hide(t):
                pe.wait_ge(chunk_placed, per_pair * (t + 1))
                pe.wait_ge(own_placed, t + 1)
                if t == 0:
                    pe.wait_ge(w1_loaded, 32)
                else:
                    pe.wait_ge(hidden_done, 2 * t)
                for m in range(2):
                    for j in range(CMP_LEN):
                        mm = nc.tensor.matmul(hid_ps[:, m, 0:CMP_COLS], w1[:, j, m * P:(m + 1) * P],
                                              blocks[:, t % 2, j], start=(j == 0), stop=(j == CMP_LEN - 1))
                mm.then_inc(hid_done, 1)

            def second_layer(t):
                pe.wait_ge(hidden_done, 2 * t + 2)
                if t == 0:
                    pe.wait_ge(w2_loaded, 16)
                else:
                    pe.wait_ge(out_copied, t)
                if kind == 0:
                    for m in range(2):
                        mm = nc.tensor.matmul(out_ps[:, 0, 0:CMP_COLS], w2[:, m], hidden[:, m], start=(m == 0),
                                              stop=(m == 1))
                else:
                    for b in range(2):
                        for m in range(2):
                            mm = nc.tensor.matmul(out_ps[:, 0, b * HD:(b + 1) * HD], hidden[:, m, b * P:(b + 1) * P],
                                                  w2[:, m], start=(m == 0), stop=(m == 1))
                mm.then_inc(out_done, 1)

            for n in range(2 * per_pair):
                turn_chunk(n)
            for t in range(PAIRS):
                hide(t)
                if t + 2 < PAIRS:
                    for n in range((t + 2) * per_pair, (t + 3) * per_pair):
                        turn_chunk(n)
                second_layer(t)
            if kind == 0:
                pe.wait_ge(squared, 1)
                for n, (s, w) in enumerate(thirds):
                    mm = nc.tensor.matmul((hid_ps[:, n % 2] if n < 2 else out_ps[:, 1])[:, 0:w], g.ones[:],
                                          squares[:, s:s + w], start=True, stop=True)
                mm.then_inc(summed, 1)
            else:
                pe.wait_ge(own_placed, 2 * PAIRS)
                for h in range(GROUPS):
                    for m in range(2):
                        mm = nc.tensor.matmul(out_ps[0:CMP_PROMPT, 1, h * HD:(h + 1) * HD], own_hidden[:, m, h],
                                              w2[:, m], start=(m == 0), stop=(m == 1))
                mm.then_inc(out_done, 1)

        @block.vector
        def _(dve):
            pe_cols = g.cmp_pe[:, kind * CMP_LEN:(kind + 1) * CMP_LEN]
            linked = Chain(dve, link)

            def place(n):
                t, c = divmod(n, per_pair)
                b, c = divmod(c, CHUNKS)
                dve.wait_ge(chunk_turned, n + 1)
                if t >= 2 and n % per_pair == 0:
                    dve.wait_ge(hid_done, t - 1)
                for h in range(GROUPS):
                    col = b * P + h * CMP_BLOCKS + c * CHUNK_PAGES * CMP_PER_PAGE
                    width = CHUNK_PAGES * CMP_PER_PAGE
                    last = nc.vector.tensor_tensor(
                        blocks[:, t % 2, :, col:col + width].rearrange("p j n -> p n j"),
                        rows_ps[:, n % 2, h].rearrange("p (n j) -> p n j", j=CMP_LEN),
                        pe_cols.unsqueeze(1).to_broadcast([P, width, CMP_LEN]), ALU.add)
                last.then_inc(chunk_placed, 1)

            def place_own(t):
                for h in range(GROUPS):
                    col = PAIR_COLS + 2 * h
                    own = g.p[:, HEADS + kind * GROUPS + h, 2 * t * CMP_LEN:2 * (t + 1) * CMP_LEN]
                    last = nc.vector.tensor_tensor(
                        blocks[:, t % 2, :, col:col + 2].rearrange("p j n -> p n j"),
                        own.rearrange("p (n j) -> p n j", j=CMP_LEN),
                        pe_cols.unsqueeze(1).to_broadcast([P, 2, CMP_LEN]), ALU.add)
                last.then_inc(own_placed, 1)

            def silu(t):
                dve.wait_ge(exp_done, 2 * t + 2)
                linked(nc.vector.tensor_scalar(e[:], e[:], 1.0, None, ALU.add))
                linked(nc.vector.reciprocal(e[:], e[:]))
                if t:
                    dve.wait_ge(out_done, t)
                for m in range(2):
                    nc.vector.scalar_tensor_tensor(hidden[:, m], hid_ps[:, m, 0:CMP_COLS],
                                                   g.vec[:, b1 + m:b1 + m + 1], e[:, m], ALU.add,
                                                   ALU.mult).then_inc(hidden_done, 1)
                if kind == 1:
                    dve.wait_ge(hidden_done, 2 * t + 2)
                    nc.vector.tensor_copy(
                        own_hidden[:, :, :, 2 * t:2 * t + 2],
                        hidden[:, :, PAIR_COLS:CMP_COLS].rearrange("p m (h c) -> p m h c", h=GROUPS)
                    ).then_inc(own_placed, 1)

            for t in range(2):
                for n in range(t * per_pair, (t + 1) * per_pair):
                    place(n)
                place_own(t)
            for t in range(PAIRS):
                silu(t)
                if t + 2 < PAIRS:
                    for n in range((t + 2) * per_pair, (t + 3) * per_pair):
                        place(n)
                    place_own(t + 2)
            if kind == 0:
                flat = g.cmp_k[:].rearrange("p t n -> p (t n)")
                dve.wait_ge(out_copied, PAIRS)
                nc.vector.tensor_tensor(squares, flat, flat, ALU.mult).then_inc(squared, 1)
                dve.wait_ge(summed, 1)
                for n, (s, w) in enumerate(thirds):
                    last = nc.vector.tensor_scalar(squares[:, s:s + w],
                                                   (hid_ps[:, n % 2] if n < 2 else out_ps[:, 1])[:, 0:w],
                                                   1.0 / HD, EPS, ALU.mult, ALU.add)
                last.then_inc(mean, 1)
                dve.wait_ge(root, 1)
                linked(nc.vector.reciprocal(squares, squares))
                gk = VEC["nsa_g_k"]
                linked(nc.vector.scalar_tensor_tensor(flat, flat, g.vec[:, gk:gk + 1], squares, ALU.mult, ALU.mult))
                nc.vector.tensor_copy(g.cmp_k_prompt[:].rearrange("p h (t c) -> p h t c", c=2),
                                      g.cmp_k[:, :, PAIR_COLS:CMP_COLS].rearrange("p t (h c) -> p h t c", c=2))


SEL_K, SEL_V, WIN_K, WIN_V = HEADS + 4, HEADS + 6, HEADS + 8, HEADS + 10
MEM_Q = HEADS + 12
ROW_TILES = 12
T_COLS = 384


def prepare_sparse(nc, g, a):
    with ExitStack() as ctx:
        sb = lambda n, s: ctx.enter_context(nc.sbuf_tensor(f"prep_{n}", s, F32))
        sem = counters(nc, ctx, f"prep_")
        gq, gk, gm = VEC["nsa_g_q"], VEC["nsa_g_k"], VEC["g_mem_q"]
        normed = [(t, gq, SCALE) for t in range(HEADS)] \
            + [(t, gk + 1, 1.0) for t in (SEL_K, SEL_K + 1)] + [(t, gk + 2, 1.0) for t in (WIN_K, WIN_K + 1)] \
            + [(t, gm, SCALE) for t in range(MEM_Q, MEM_Q + MEM_HEADS)]
        BATCHED = 4
        squares = sb("squares", [P, 2, BATCHED, TOKENS])
        scaled_gain = sb("scaled_gain", [P, 2])
        neg_bias = sb("neg_bias", [BRANCHES * HEADS, 1])
        gate_rows = sb("gate_rows", [BRANCHES * HEADS, BRANCHES * P])
        own_gates = sb("own_gates", [P, BRANCHES * SAMPLED])
        bias = sb("bias", [HEADS, DISTS])
        rows_ps = ctx.enter_context(nc.psum_tensor("prep_rows_ps", [P, 4, 512], F32))
        sums_ps = ctx.enter_context(nc.psum_tensor("prep_sums_ps", [P, BATCHED, 512], F32))
        turned, rows_copied, squared, summed, mean, root, inverse, scaled, link, neg_done, gate_exp, gates_done, \
            loaded, stored, blank = map(sem, (
                "turned", "rows_copied", "squared", "summed", "mean", "root", "inverse", "scaled", "link",
                "neg_done", "gate_exp", "gates_done", "loaded", "stored", "blank"))
        flipped, flip_copied = sem("flipped"), sem("flip_copied")
        FLIP_BANKS = 3
        FLIPS = HEADS * T_COLS // (512 * FLIP_BANKS)
        block = ctx.enter_context(nc.Block())
        sets = [(s, tok) for tok in range(QT + 1) for s in range(ROW_TILES // 4)]
        width = lambda tok: P if tok < QT else SAMPLED
        rounds = len(normed) // BATCHED
        u = g.bias_dram.tensor

        @block.sync
        def _(sp):
            sp.dma_start(g.near[:], bass.AP(u, 0, [[1, P], [DISTS, HEADS], [1, T_COLS]])).then_inc(loaded, 16)
            sp.dma_start(bias[:], g.bias_dram).then_inc(loaded, 16)
            sp.dma_start(g.sparse_masks[:], a.sparse_masks).then_inc(loaded, 16)
            sp.dma_start(gate_rows[:], a.gate_rows).then_inc(loaded, 16)
            kv, win = 4 * GROUPS * HD, 2 * GROUPS * HD
            for tok in range(QT + 1):
                sp.wait_ge(rows_copied, 3 * (tok + 1))
                src = g.rows[:, tok] if tok < QT else g.rows_sampled[:]
                if tok < QT:
                    dst = a.nsa_kv_prompt[0, 0, tok * P:(tok + 1) * P].rearrange("r k g d -> r (k g d)")
                    dst_win = a.nsa_win_prompt[0, 0, tok * P:(tok + 1) * P].rearrange("r k g d -> r (k g d)")
                    sp.dma_start(dst_win, src[:, kv:kv + win]).then_inc(stored, 16)
                else:
                    dst = a.nsa_kv_sample[0].rearrange("b l k g d -> (b l) (k g d)")
                    for b in range(BATCH):
                        sp.dma_start(a.nsa_win_sample[0, b, WINDOW - STEP:WINDOW].rearrange("r k g d -> r (k g d)"),
                                     src[b * STEP:(b + 1) * STEP, kv:kv + win]).then_inc(stored, 16)
                sp.dma_start(dst, src[:, 0:kv]).then_inc(stored, 16)
            for b in range(BATCH):
                sp.dma_start(a.nsa_win_sample[0, b, 0:WINDOW - STEP], a.state_nsa_win[0, b, STEP:WINDOW]
                             ).then_inc(stored, 16)
            sp.wait_ge(stored, 16 * (QT * 2 + 1 + 2 * BATCH))
            sp.wait_ge(loaded, 16 * 4)

        @block.gpsimd
        def _(pool):
            nc.gpsimd.memset(g.q_sampled[:], 0.0).then_inc(blank, 1)

        @block.tensor
        def _(pe):
            for n, (s, tok) in enumerate(sets):
                if n >= 4:
                    pe.wait_ge(rows_copied, n - 3)
                for o in range(4):
                    mm = nc.tensor.transpose(rows_ps[0:width(tok), n % 4, o * P:(o + 1) * P],
                                             g.p[:, HEADS + 4 * s + o, tok * P:tok * P + width(tok)], g.ident[:])
                mm.then_inc(turned, 1)
            pe.wait_ge(gates_done, 1)
            pe.wait_ge(rows_copied, len(sets))
            for tok in range(QT):
                mm = nc.tensor.transpose(rows_ps[:, tok, 0:BRANCHES * HEADS], g.gates[:, tok * P:(tok + 1) * P],
                                         g.ident[0:BRANCHES * HEADS, 0:BRANCHES * HEADS])
            pe.wait_ge(loaded, 16 * 4)
            for r in range(BRANCHES):
                mm = nc.tensor.matmul(rows_ps[:, 2, r * SAMPLED:(r + 1) * SAMPLED], gate_rows[:, r * P:(r + 1) * P],
                                      g.gates[:, SEQ:TOKENS], start=True, stop=True)
            mm.then_inc(turned, 1)
            nc.tensor.matmul(rows_ps[:, 3, :], gate_rows[0:HEADS, 0:P], bias[:], start=True, stop=True
                             ).then_inc(turned, 1)
            flat = g.near[:].rearrange("p h c -> p (h c)")
            for n in range(FLIPS):
                wait(pe, flip_copied, n)
                for o in range(FLIP_BANKS):
                    at = (n * FLIP_BANKS + o) * 512
                    mm = nc.tensor.matmul(sums_ps[:, o], g.sparse_masks[:, SP_FLIP:SP_FLIP + P], flat[:, at:at + 512],
                                          start=True, stop=True)
                mm.then_inc(flipped, 1)
            pe.wait_ge(flip_copied, FLIPS)
            for r in range(rounds):
                pe.wait_ge(squared, r + 1)
                if r:
                    pe.wait_ge(mean, r)
                for o in range(BATCHED):
                    mm = nc.tensor.matmul(sums_ps[:, o, 0:TOKENS], g.ones[:], squares[:, r % 2, o], start=True,
                                          stop=True)
                mm.then_inc(summed, 1)

        @block.scalar
        def _(act):
            act.wait_ge(neg_done, 1)
            nc.scalar.activation(g.gates[:], g.gates[:], ACT.Exp, bias=neg_bias[:], scale=-1.0
                                 ).then_inc(gate_exp, 1)
            for n, (s, tok) in enumerate(sets):
                act.wait_ge(turned, n + 1)
                dst = g.rows[:, tok, s * 512:(s + 1) * 512] if tok < QT else g.rows_sampled[:, s * 512:(s + 1) * 512]
                nc.scalar.activation(dst, rows_ps[0:width(tok), n % 4, :], ACT.Copy).then_inc(rows_copied, 1)
            for n in range(FLIPS):
                act.wait_ge(flipped, n + 1)
                nc.scalar.activation(
                    g.near[:].rearrange("p h c -> p (h c)").rearrange("p (n b c) -> p n b c", b=FLIP_BANKS, c=512)[:, n],
                    sums_ps[:, 0:FLIP_BANKS], ACT.Copy).then_inc(flip_copied, 1)
            for r in range(rounds):
                act.wait_ge(mean, r + 1)
                nc.scalar.activation(squares[:, r % 2], squares[:, r % 2], ACT.Sqrt).then_inc(root, 1)

        @block.vector
        def _(dve):
            linked = Chain(dve, link)
            nc.vector.tensor_scalar(neg_bias[:], g.gate_bias[:], -1.0, None, ALU.mult).then_inc(neg_done, 1)
            linked(nc.vector.tensor_scalar(scaled_gain[:, 0:1], g.vec[:, gq:gq + 1], SCALE, None, ALU.mult))
            linked(nc.vector.tensor_scalar(scaled_gain[:, 1:2], g.vec[:, gm:gm + 1], SCALE, None, ALU.mult))
            dve.wait_ge(gate_exp, 1)
            linked(nc.vector.tensor_scalar(g.gates[:], g.gates[:], 1.0, None, ALU.add))
            nc.vector.reciprocal(g.gates[:], g.gates[:]).then_inc(gates_done, 1)
            dve.wait_ge(turned, len(sets) + 1)
            nc.vector.tensor_copy(g.gates_prompt[:], rows_ps[:, 0:QT, 0:BRANCHES * HEADS])
            own = g.sparse_masks[:, SP_OWN:SP_OWN + 2 * STEP]
            linked(nc.vector.tensor_tensor(
                own_gates[:].rearrange("p (n c) -> p n c", c=2 * STEP),
                rows_ps[:, 2, 0:BRANCHES * SAMPLED].rearrange("p (n c) -> p n c", c=2 * STEP),
                own.unsqueeze(1).to_broadcast([P, BRANCHES * PAIRS, 2 * STEP]), ALU.mult))
            nc.vector.tensor_reduce(g.gates_sampled[:], own_gates[:].rearrange(
                "p (r t c) -> p t r c", t=PAIRS, c=2 * STEP), AX_X, ALU.add)

            dve.wait_ge(turned, len(sets) + 2)
            nc.vector.tensor_copy(g.bias_far[:], rows_ps[:, 3, 0:1])
            for l in range(STEP):
                near = rows_ps[:, 3, P - 1 - l:P - 1 - l + 132]
                at = g.sparse_masks[:, SP_AT + l:SP_AT + l + 1]
                if l == 0:
                    linked(nc.vector.tensor_scalar(g.bias_near[:], near, at, None, ALU.mult))
                else:
                    linked(nc.vector.scalar_tensor_tensor(g.bias_near[:], near, at, g.bias_near[:], ALU.mult, ALU.add))

            def square(r):
                for o in range(BATCHED):
                    t = normed[r * BATCHED + o][0]
                    last = nc.vector.tensor_tensor(squares[:, r % 2, o], g.p[:, t], g.p[:, t], ALU.mult)
                last.then_inc(squared, 1)

            square(0)
            for r in range(rounds):
                if r + 1 < rounds:
                    if r >= 1:
                        dve.wait_ge(scaled, r)
                    square(r + 1)
                dve.wait_ge(summed, r + 1)
                nc.vector.tensor_scalar(squares[:, r % 2], sums_ps[:, :, 0:TOKENS], 1.0 / HD, EPS, ALU.mult, ALU.add
                                        ).then_inc(mean, 1)
                dve.wait_ge(root, r + 1)
                linked(nc.vector.reciprocal(squares[:, r % 2], squares[:, r % 2]))
                for o in range(BATCHED):
                    t, gain, scale = normed[r * BATCHED + o]
                    col = g.vec[:, gain:gain + 1] if scale == 1.0 else scaled_gain[:, int(gain == gm):int(gain == gm) + 1]
                    if o == 0:
                        dve.wait_ge(turned, len(sets))
                    last = nc.vector.scalar_tensor_tensor(g.p[:, t], g.p[:, t], col, squares[:, r % 2, o], ALU.mult,
                                                          ALU.mult)
                last.then_inc(scaled, 1)
            dve.wait_ge(scaled, rounds)
            dve.wait_ge(blank, 1)
            for j in range(4):
                h0, b = (j % 2) * HPG, j // 2
                src = g.p[:, h0:h0 + HPG, SEQ:TOKENS].rearrange("p h (t b l) -> p b t h l", b=2, l=STEP)[:, b]
                for t in range(PAIRS):
                    nc.vector.tensor_copy(g.q_sampled[:, t, 32 * j:32 * j + HPG * STEP].rearrange(
                        "p (h l) -> p h l", l=STEP), src[:, t])
            nc.vector.tensor_copy(g.new_k[:, 0:2], g.p[:, SEL_K:SEL_K + 2, SEQ:TOKENS])
            nc.vector.tensor_copy(g.new_k[:, 2:4], g.p[:, WIN_K:WIN_K + 2, SEQ:TOKENS])


def attend_prompt(nc, g, tag, bodies, heads, query, branches, gate, out):
    units = [(k, i) for k in range(heads) for i in range(QT)]
    NB = len(branches)
    biased = gate is not None
    widest = [b["width"](QT - 1) for b in branches]
    starts = [sum(widest[:n]) for n in range(NB)]
    cols = sum(widest)
    with ExitStack() as ctx:
        sb = lambda n, s: ctx.enter_context(nc.sbuf_tensor(f"{tag}_{n}", s, F32))
        sem = counters(nc, ctx, f"{tag}_")
        q = sb("q", [P, 2, SEQ])
        s = sb("scores", [P, 2, cols])
        probs = sb("probs", [P, 2, cols])
        maxima = sb("maxima", [P, 2, NB])
        sums = sb("sums", [P, 2, NB])
        coef = sb("coef", [P, 2, NB])
        turned = sb("turned", [P, 5, P])
        s_ps = ctx.enter_context(nc.psum_tensor(f"{tag}_s_ps", [P, 2, 2, 512], F32))
        t_ps = ctx.enter_context(nc.psum_tensor(f"{tag}_t_ps", [P, 2, 512], F32))
        o_ps = ctx.enter_context(nc.psum_tensor(f"{tag}_o_ps", [P, 2, 512], F32))
        q_ready, scored, biased_done, negated, exped, scaled, turns_done, turns_copied, out_done, \
            out_copied, link = map(sem, (
                "q_ready", "scored", "biased_done", "negated", "exped", "scaled",
                "turns_done", "turns_copied", "out_done", "out_copied", "link"))
        block = ctx.enter_context(nc.Block())

        def place(n):
            return (0, starts[n] - (starts[1] if NB == 3 else 0)) if (NB == 1 or n > 0) else (1, 0)

        def pieces(i):
            return [(n, c, min(P, b["width"](i) - c * P)) for n, b in enumerate(branches)
                    for c in range(-(-b["width"](i) // P))]

        U = len(units)

        def score_psum(n, unit):
            bank, col = place(n)
            return s_ps[:, unit % 2, bank, col:col + branches[n]["width"](units[unit][1])]

        def loop(eng, body):
            body(0)
            if bodies > 1:
                with eng.Fori(1, bodies) as m:
                    body(m)

        @block.gpsimd
        def _(pool):
            def body(m):
                for k in range(heads):
                    wait(pool, scored, m * U + QT * (k - 1))
                    nc.gpsimd.tensor_copy(q[:, k % 2], query(m, k)).then_inc(q_ready, 1)
            loop(pool, body)

        @block.tensor
        def _(pe):
            def scores(m, u):
                k, i = units[u]
                if i == 0:
                    pe.wait_ge(q_ready, m * heads + (k + 1))
                wait(pe, biased_done if biased else exped, m * U + (u - 1))
                for n, b in enumerate(branches):
                    mm = nc.tensor.matmul(score_psum(n, u), q[:, k % 2, i * P:(i + 1) * P],
                                          b["keys"](m, k)[:, 0:b["width"](i)], start=True, stop=True,
                                          skip_group_check=True)
                mm.then_inc(scored, 1)

            def outputs(m, u):
                k, i = units[u]
                pe.wait_ge(scaled, m * U + (u + 1))
                wait(pe, turns_copied, m * U + u)
                for e, (n, c, w) in enumerate(pieces(i)):
                    mm = nc.tensor.transpose(t_ps[0:w, e // 4, (e % 4) * P:(e % 4 + 1) * P],
                                             probs[:, u % 2, starts[n] + c * P:starts[n] + c * P + w], g.ident[:])
                mm.then_inc(turns_done, 1)
                pe.wait_ge(turns_copied, m * U + (u + 1))
                wait(pe, out_copied, m * U + (u - 1))
                for e, (n, c, w) in enumerate(pieces(i)):
                    mm = nc.tensor.matmul(o_ps[:, u % 2, 0:P], branches[n]["values"](k, c)[0:w], turned[0:w, e],
                                          start=(e == 0), stop=(e == len(pieces(i)) - 1))
                mm.then_inc(out_done, 1)

            def body(m):
                scores(m, 0)
                for u in range(U):
                    if u + 1 < U:
                        scores(m, u + 1)
                    outputs(m, u)
            loop(pe, body)

        @block.vector
        def _(dve):
            def front(m, u, linked):
                k, i = units[u]
                dve.wait_ge(scored, m * U + (u + 1))
                for n, b in enumerate(branches):
                    w = b["width"](i)
                    if biased:
                        last = nc.vector.tensor_tensor(s[:, u % 2, starts[n]:starts[n] + w], score_psum(n, u), b["bias"](m, k, i), ALU.add)
                if biased:
                    last.then_inc(biased_done, 1)
                    dve.wait_ge(biased_done, m * U + (u + 1))
                for n, b in enumerate(branches):
                    w = b["width"](i)
                    src = s[:, u % 2, starts[n]:starts[n] + w] if biased else score_psum(n, u)
                    last = nc.vector.tensor_reduce(maxima[:, u % 2, n:n + 1], src, AX_X, ALU.max)
                linked(last)
                nc.vector.tensor_scalar(maxima[:, u % 2], maxima[:, u % 2], 0.1 * MASKED, -1.0, ALU.max, ALU.mult
                                        ).then_inc(negated, 1)

            def back(m, u, linked):
                k, i = units[u]
                dve.wait_ge(exped, m * U + (u + 1))
                linked(nc.vector.tensor_scalar(sums[:, u % 2], sums[:, u % 2], 1e-30, None, ALU.max))
                linked(nc.vector.reciprocal(coef[:, u % 2], sums[:, u % 2]))
                if biased:
                    linked(nc.vector.tensor_tensor(coef[:, u % 2], coef[:, u % 2], gate(m, k, i), ALU.mult))
                for n, b in enumerate(branches):
                    at = slice(starts[n], starts[n] + b["width"](i))
                    last = nc.vector.tensor_scalar(probs[:, u % 2, at], probs[:, u % 2, at],
                                                   coef[:, u % 2, n:n + 1], None, ALU.mult)
                last.then_inc(scaled, 1)

            def take(m, u):
                dve.wait_ge(out_done, m * U + (u + 1))
                k, i = units[u]
                nc.vector.tensor_copy(out(m, k, i), o_ps[:, u % 2, 0:P]).then_inc(out_copied, 1)

            def body(m):
                links = U * (4 if biased else 3)
                linked = Chain(dve, link, m * links)
                front(m, 0, linked)
                for u in range(U):
                    if u + 1 < U:
                        front(m, u + 1, linked)
                    back(m, u, linked)
                    if u >= 1:
                        take(m, u - 1)
                take(m, U - 1)
                assert linked.n == links
            loop(dve, body)

        @block.scalar
        def _(act):
            def exps(m, u):
                k, i = units[u]
                act.wait_ge(negated, m * U + (u + 1))
                for n, b in enumerate(branches):
                    at = slice(starts[n], starts[n] + b["width"](i))
                    src = s[:, u % 2, at] if biased else score_psum(n, u)
                    last = nc.scalar.activation(probs[:, u % 2, at], src, ACT.Exp, bias=maxima[:, u % 2, n:n + 1],
                                                accum_out=sums[:, u % 2, n:n + 1])
                last.then_inc(exped, 1)

            def copies(m, u):
                k, i = units[u]
                act.wait_ge(turns_done, m * U + (u + 1))
                wait(act, out_done, m * U + u)
                e = pieces(i)
                for b in range(-(-len(e) // 4)):
                    part = e[4 * b:4 * b + 4]
                    full = [x for x in part if x[2] == P]
                    few = [(x, y) for x, y in enumerate(part) if y[2] < P]
                    first = 1 if few else 0
                    if few:
                        w = few[0][1][2]
                        nc.scalar.activation(turned[0:w, 4 * b], t_ps[0:w, b, 0:P], ACT.Copy)
                    last = nc.scalar.activation(turned[:, 4 * b + first:4 * b + len(part)],
                                                t_ps[:, b, first * P:len(part) * P].rearrange("p (c q) -> p c q", q=P),
                                                ACT.Copy)
                last.then_inc(turns_copied, 1)

            def body(m):
                exps(m, 0)
                for u in range(U):
                    if u + 1 < U:
                        exps(m, u + 1)
                    copies(m, u)
            loop(act, body)


NEW = SAMPLED
S_CMP, S_SEL = 0, 2 * CMP_BLOCKS
S_SEL_NEW = S_SEL + PAST
S_WIN = S_SEL_NEW + NEW
S_WIN_NEW = S_WIN + WINDOW
S_COLS = S_WIN_NEW + NEW
HALVES = 2 * (CHUNKS + 1)
TOP_ROUNDS = 2
FORCED = 1e4
P_CHUNKS = [(S_CMP, P)] + [(S_SEL + c * P, P) for c in range(PAGES)] + [(S_SEL_NEW, NEW)] \
    + [(S_WIN + c * P, P) for c in range(WINDOW // P)] + [(S_WIN_NEW, NEW)]


def attend_sampled(nc, g, a, base, next_chunks):
    with ExitStack() as ctx:
        sb = lambda n, s: ctx.enter_context(nc.sbuf_tensor(f"sp_{n}", s, F32))
        ps = lambda n, s: ctx.enter_context(nc.psum_tensor(f"sp_{n}", s, F32))
        sem = counters(nc, ctx, "sp_")
        q = sb("q", [P, P])
        cmp_k = sb("cmp_k", [P, 2, GROUPS * CMP_BLOCKS])
        cmp_v = sb("cmp_v", [P, 2, HD])
        stage = sb("stage", [P, 4, CHUNK_PAGES, GROUPS * HD])
        squares = [g.mem_k[:, 0].rearrange("p h k -> p (h k)"), g.mem_v[:, 0].rearrange("p t n -> p (t n)")]
        ss = sb("ss", [P, 2, CHUNK_PAGES * GROUPS])
        turned_k = sb("turned_k", [P, 2, GROUPS, 512])
        values = sb("values", [P, HALVES, CHUNK_PAGES, GROUPS * HD])
        s = sb("s", [P, S_COLS])
        probs = sb("probs", [P, len(P_CHUNKS), P])
        cmp_bias = sb("cmp_bias", [P, 2 * CMP_BLOCKS])
        win_bias = sb("win_bias", [P, WINDOW])
        new_bias = sb("new_bias", [P, NEW])
        near_bias = sb("near_bias", [P, P])
        block_score = sb("block_score", [P, SEL_BLOCKS])
        pair_score = sb("pair_score", [P, 2 * GROUPS * CMP_BLOCKS // 4])
        unselected = sb("unselected", [P, SEL_BLOCKS])
        sel_bias = sb("sel_bias", [P, SEL_BLOCKS])
        top = sb("top", [P, TOP_ROUNDS, 8])
        spare = sb("spare", [P, 1])
        neg_max = sb("neg_max", [P, BRANCHES])
        sums = sb("sums", [P, BRANCHES])
        coef = sb("coef", [P, BRANCHES])
        o = sb("o", [P, HD])
        k_ps = ps("k_ps", [P, 2, GROUPS, 512])
        s_ps = ps("s_ps", [P, 2, 512])
        small_ps = ps("small_ps", [P, 512])
        o_ps = ps("o_ps", [P, 512])
        stage_loaded = [sem(f"stage_loaded{b}") for b in range(4)]
        values_loaded = sem("values_loaded")
        q_ready, small_scored, cmp_negated, cmp_exped, cmp_ready, group_summed, k_squared, k_mean, k_root, k_inverse, \
            k_scaled, k_turned, k_copied, half_scored, s_taken, negated, exped, scaled, p_turned, p_copied, multiplied, \
            o_taken, o_turned, o_stored, link = map(sem, (
                "q_ready", "small_scored", "cmp_negated", "cmp_exped", "cmp_ready", "group_summed", "k_squared",
                "k_mean", "k_root", "k_inverse", "k_scaled", "k_turned", "k_copied", "half_scored", "s_taken",
                "negated", "exped", "scaled", "p_turned", "p_copied", "multiplied", "o_taken", "o_turned",
                "o_stored", "link"))
        block = ctx.enter_context(nc.Block())
        pages = a.cache_nsa_kv[0].rearrange("n r k g d -> n r k (g d)")
        window = a.state_nsa_win[0].rearrange("b (c p) k g d -> b p c k (g d)", p=P)
        CH = CHUNKS + 1
        sets = [list(range(n, min(n + 8, len(P_CHUNKS)))) for n in range(0, len(P_CHUNKS), 8)]

        def turns(eng, body):
            body(0)
            with eng.Fori(1, PAIRS) as t:
                body(t)

        @block.sync
        def _(sp):
            def sources(t, n):
                c, b = divmod(n, 2)
                if c == CHUNKS:
                    return lambda part: [window[bass.ds(t * 2 + b, 1), :, quarter, part].squeeze(0)
                                         for quarter in range(WINDOW // P)]
                first = t * (2 * PAGES) + (b * PAGES + c * CHUNK_PAGES)
                numbers = [sp.value_load(g.pages[0:1, bass.ds(first + quarter, 1)], min_val=0,
                                         max_val=pages.shape[0] - 1) for quarter in range(CHUNK_PAGES)]
                return lambda part: [pages[bass.ds(page, 1), :, 2 + part].squeeze(0) for page in numbers]

            def body(t):
                for n in range(HALVES):
                    source = sources(t, n)
                    last_here = n - 4 if n >= 4 else (HALVES - 1 - (HALVES - 1 - n) % 4) - HALVES
                    wait(sp, k_turned, t * HALVES + (last_here + 1))
                    for quarter, src in enumerate(source(0)):
                        sp.dma_start(stage[:, n % 4, quarter], src).then_inc(stage_loaded[n % 4], 16)
                    if n == 0:
                        wait(sp, multiplied, t)
                    for quarter, src in enumerate(source(1)):
                        sp.dma_start(values[:, n, quarter], src).then_inc(values_loaded, 16)

            load_first_chunks(sp, g, next_chunks, base)
            body(0)
            with sp.Fori(1, PAIRS) as t:
                body(t)

        @block.gpsimd
        def _(pool):
            def body(t):
                for n in range(HALVES):
                    pool.wait_ge(k_inverse, t * HALVES + (n + 1))
                    k = stage[:, n % 4].rearrange("p q (g d) -> p (q g) d", g=GROUPS)
                    nc.gpsimd.tensor_tensor(k, k, ss[:, n % 2].unsqueeze(2).to_broadcast(
                        [P, CHUNK_PAGES * GROUPS, HD]), ALU.mult).then_inc(k_scaled, 1)
            turns(pool, body)

        @block.tensor
        def _(pe):
            def turn_keys(t, n):
                pe.wait_ge(k_scaled, t * HALVES + (n + 1))
                wait(pe, k_copied, t * HALVES + (n - 1))
                if n < 2:
                    wait(pe, p_copied, t * len(sets))
                for h in range(GROUPS):
                    for q_ in range(CHUNK_PAGES):
                        mm = nc.tensor.transpose(k_ps[:, n % 2, h, q_ * P:(q_ + 1) * P],
                                                 stage[:, n % 4, q_, h * HD:(h + 1) * HD], g.ident[:])
                mm.then_inc(k_turned, 1)

            def score(t, n):
                c, b = divmod(n, 2)
                pe.wait_ge(k_copied, t * HALVES + (n + 1))
                wait(pe, s_taken, t * CH + (c - 1 if c else 0))
                for h in range(GROUPS):
                    j = 2 * b + h
                    mm = nc.tensor.matmul(s_ps[32 * j:32 * j + 32, c % 2], q[:, 32 * j:32 * j + 32],
                                          turned_k[:, n % 2, h], start=True, stop=True)
                mm.then_inc(half_scored, 1)

            def body(t):
                pe.wait_ge(q_ready, t + 1)
                for j in range(4):
                    rows = slice(32 * j, 32 * j + 32)
                    nc.tensor.matmul(small_ps[rows, 0:P], q[:, rows], cmp_k[:, j // 2], start=True, stop=True, skip_group_check=True)
                for j in range(4):
                    rows = slice(32 * j, 32 * j + 32)
                    for w in range(2):
                        mm = nc.tensor.matmul(small_ps[rows, P + w * NEW:P + (w + 1) * NEW], q[:, rows],
                                              g.new_k[:, 2 * w + j % 2], start=True, stop=True,
                                              skip_group_check=True)
                mm.then_inc(small_scored, 1)
                turn_keys(t, 0)
                turn_keys(t, 1)
                pe.wait_ge(cmp_ready, t + 1)
                nc.tensor.matmul(small_ps[:, 256:256 + P], g.sparse_masks[:, SP_SAME:SP_SAME + P], s[:, 0:P],
                                 start=True, stop=True, skip_group_check=True).then_inc(group_summed, 1)
                for n in range(HALVES):
                    score(t, n)
                    if n + 2 < HALVES:
                        turn_keys(t, n + 2)
                pe.wait_ge(scaled, t + 1)
                for i, chunks in enumerate(sets):
                    pe.wait_ge(k_copied, (t + 1) * HALVES)
                    if i >= 2:
                        pe.wait_ge(p_copied, t * len(sets) + (i - 1))
                    for e, x in enumerate(chunks):
                        col, w = P_CHUNKS[x]
                        mm = nc.tensor.transpose(k_ps[0:w, i % 2, e // 4, e % 4 * P:(e % 4 + 1) * P], s[:, col:col + w],
                                                 g.ident[:])
                    mm.then_inc(p_turned, 1)
                pe.wait_ge(values_loaded, t * (64 * HALVES) + 64 * HALVES)
                wait(pe, o_taken, t)
                done = 0
                for i, chunks in enumerate(sets):
                    pe.wait_ge(p_copied, t * len(sets) + (i + 1))
                    for x in chunks:
                        col, w = P_CHUNKS[x]
                        for j in range(4):
                            b, h = divmod(j, 2)
                            if x == 0:
                                v = cmp_v[:, b]
                            elif w == NEW:
                                tile = (SEL_V if col == S_SEL_NEW else WIN_V) - HEADS + h
                                v = g.rows_sampled[:, tile * HD:(tile + 1) * HD]
                            else:
                                c = (col - S_SEL) // P if col < S_WIN else PAGES + (col - S_WIN) // P
                                v = values[:, 2 * (c // CHUNK_PAGES) + b, c % CHUNK_PAGES, h * HD:(h + 1) * HD]
                            mm = nc.tensor.matmul(o_ps[32 * j:32 * j + 32, 0:HD], probs[0:w, x, 32 * j:32 * j + 32], v,
                                                  start=(x == 0), stop=(x == len(P_CHUNKS) - 1))
                mm.then_inc(multiplied, 1)
                pe.wait_ge(o_taken, t + 1)
                nc.tensor.transpose(small_ps[:, 384:512], o[:], g.ident[:]).then_inc(o_turned, 1)
            turns(pe, body)

        @block.scalar
        def _(act):
            def body(t):
                act.wait_ge(cmp_negated, t + 1)
                nc.scalar.activation(s[:, 0:P], s[:, 0:P], ACT.Exp, bias=neg_max[:, 0:1],
                                     accum_out=sums[:, 0:1]).then_inc(cmp_exped, 1)

                def square(n):
                    act.wait_ge(stage_loaded[n % 4], square_loads(t, n))
                    wait(act, k_mean, t * HALVES + (n - 1))
                    nc.scalar.activation(squares[n % 2], stage[:, n % 4].rearrange("p q n -> p (q n)"), ACT.Square
                                         ).then_inc(k_squared, 1)

                square(0)
                square(1)
                for n in range(HALVES):
                    act.wait_ge(k_mean, t * HALVES + (n + 1))
                    nc.scalar.activation(ss[:, n % 2], ss[:, n % 2], ACT.Sqrt).then_inc(k_root, 1)
                    if n + 2 < HALVES:
                        square(n + 2)
                    act.wait_ge(k_turned, t * HALVES + (n + 1))
                    wait(act, half_scored, t * HALVES + (n - 1))
                    gk = VEC["nsa_g_k"] + (1 if n < 2 * CHUNKS else 2)
                    nc.scalar.activation(turned_k[:, n % 2], k_ps[:, n % 2], ACT.Copy, scale=g.vec[:, gk:gk + 1]
                                         ).then_inc(k_copied, 1)
                act.wait_ge(negated, t + 1)
                for r, (c0, c1) in ((1, (S_SEL, S_WIN)), (2, (S_WIN, S_COLS))):
                    nc.scalar.activation(s[:, c0:c1], s[:, c0:c1], ACT.Exp, bias=neg_max[:, r:r + 1],
                                         accum_out=sums[:, r:r + 1]).then_inc(exped, 1)
                for i, chunks in enumerate(sets):
                    act.wait_ge(p_turned, t * len(sets) + (i + 1))
                    wait(act, multiplied, t)
                    for h in range(2):
                        part = chunks[4 * h:4 * h + 4]
                        whole = [x for x in part if P_CHUNKS[x][1] == P]
                        runs = []
                        for x in whole:
                            if runs and runs[-1][-1] == x - 1:
                                runs[-1].append(x)
                            else:
                                runs.append([x])
                        for x in part:
                            if x not in whole:
                                e = x - part[0]
                                last = nc.scalar.activation(probs[0:NEW, x], k_ps[0:NEW, i % 2, h, e * P:(e + 1) * P],
                                                            ACT.Copy)
                        for run in runs:
                            e = run[0] - part[0]
                            last = nc.scalar.activation(
                                probs[:, run[0]:run[-1] + 1],
                                k_ps[:, i % 2, h, e * P:(e + len(run)) * P].rearrange("p (c n) -> p c n", n=P), ACT.Copy)
                    last.then_inc(p_copied, 1)
            per = [len(range(b, HALVES, 4)) for b in range(4)]

            def square_loads(t, n):
                return t * (64 * per[n % 4]) + 64 * (n // 4 + 1)
            turns(act, body)

        @block.vector
        def _(dve):
            mask = g.sparse_masks
            far = g.bias_far[:, 0:1]
            linked = Chain(dve, link)
            linked(nc.vector.tensor_scalar(cmp_bias[:], mask[:, SP_GROUP:SP_GROUP + P], far, None, ALU.add))
            late = slice(CMP_BLOCKS - 4, CMP_BLOCKS)
            for h in range(GROUPS):
                cols = slice(h * CMP_BLOCKS + CMP_BLOCKS - 4, (h + 1) * CMP_BLOCKS)
                linked(nc.vector.tensor_tensor(
                    cmp_bias[:, cols], mask[:, SP_GROUP + cols.start:SP_GROUP + cols.stop],
                    g.bias_near[:, CMP_LEN - 1:P:CMP_LEN], ALU.add))
            linked(nc.vector.memset(win_bias[:], 0.0))
            linked(nc.vector.tensor_scalar(win_bias[:], win_bias[:], far, None, ALU.add))
            linked(nc.vector.tensor_tensor(win_bias[:, 0:32], win_bias[:, 0:32], mask[:, SP_OLD:SP_OLD + 32], ALU.add))
            linked(nc.vector.tensor_copy(win_bias[:, WINDOW - P:WINDOW], g.bias_near[:, 0:P]))
            setup = linked.n

            def keys(t, n, linked):
                dve.wait_ge(k_squared, t * HALVES + (n + 1))
                wait(dve, k_scaled, t * HALVES + (n - 1))
                linked(nc.vector.tensor_reduce(ss[:, n % 2], squares[n % 2].rearrange("p (c d) -> p c d", d=HD),
                                               AX_X, ALU.add))
                nc.vector.tensor_scalar(ss[:, n % 2], ss[:, n % 2], 1.0 / HD, EPS, ALU.mult, ALU.add
                                        ).then_inc(k_mean, 1)
                dve.wait_ge(k_root, t * HALVES + (n + 1))
                nc.vector.reciprocal(ss[:, n % 2], ss[:, n % 2]).then_inc(k_inverse, 1)

            def take_scores(t, c):
                dve.wait_ge(half_scored, t * HALVES + (2 * c + 2))
                if c == CHUNKS:
                    last = nc.vector.tensor_tensor(s[:, S_WIN:S_WIN + 512], s_ps[:, c % 2], win_bias[:], ALU.add)
                else:
                    wide = 8 if c < CHUNKS - 1 else 6
                    last = nc.vector.tensor_tensor(
                        s[:, S_SEL + c * 512:S_SEL + c * 512 + wide * SEL_LEN].rearrange("p (n k) -> p n k", k=SEL_LEN),
                        s_ps[:, c % 2, 0:wide * SEL_LEN].rearrange("p (n k) -> p n k", k=SEL_LEN),
                        sel_bias[:, c * 8:c * 8 + wide].unsqueeze(2).to_broadcast([P, wide, SEL_LEN]), ALU.add)
                    if wide < 8:
                        last = nc.vector.tensor_tensor(s[:, S_SEL_NEW - P:S_SEL_NEW], s_ps[:, c % 2, 512 - P:512],
                                                       near_bias[:], ALU.add)
                last.then_inc(s_taken, 1)

            def body(t, base):
                linked = Chain(dve, link, base)
                wait(dve, multiplied, t)
                nc.vector.tensor_copy(cmp_v[:], g.cmp_v[:, bass.ds(t * 2, 2)])
                nc.vector.tensor_copy(cmp_k[:].rearrange("p b n -> p (b n)"),
                                      g.cmp_k[:, bass.ds(t, 1), 0:PAIR_COLS].squeeze(1))
                nc.vector.tensor_copy(q[:], g.q_sampled[:, bass.ds(t, 1)].squeeze(1)).then_inc(q_ready, 1)
                linked(nc.vector.tensor_tensor(
                    new_bias[:].rearrange("p (b l) -> p b l", l=STEP),
                    mask[:, bass.ds(t * SAMPLED + SP_OTHER, SAMPLED)].rearrange("p (b l) -> p b l", l=STEP),
                    g.bias_near[:, P:P + STEP].unsqueeze(1).to_broadcast([P, BATCH, STEP]), ALU.add))
                dve.wait_ge(small_scored, t + 1)
                wait(dve, p_turned, t * len(sets))
                nc.vector.tensor_tensor(s[:, S_SEL_NEW:S_WIN], small_ps[:, P:P + NEW], new_bias[:], ALU.add)
                nc.vector.tensor_tensor(s[:, S_WIN_NEW:S_COLS], small_ps[:, P + NEW:P + 2 * NEW], new_bias[:], ALU.add)
                linked(nc.vector.tensor_tensor(s[:, 0:P], small_ps[:, 0:P], cmp_bias[:], ALU.add))
                linked(nc.vector.tensor_reduce(neg_max[:, 0:1], s[:, 0:P], AX_X, ALU.max))
                nc.vector.tensor_scalar(neg_max[:, 0:1], neg_max[:, 0:1], 0.1 * MASKED, -1.0, ALU.max, ALU.mult
                                        ).then_inc(cmp_negated, 1)
                dve.wait_ge(cmp_exped, t + 1)
                linked(nc.vector.tensor_scalar(sums[:, 0:1], sums[:, 0:1], 1e-30, None, ALU.max))
                linked(nc.vector.reciprocal(coef[:, 0:1], sums[:, 0:1]))
                nc.vector.tensor_scalar(s[:, 0:P], s[:, 0:P], coef[:, 0:1], None, ALU.mult).then_inc(cmp_ready, 1)
                keys(t, 0, linked)
                keys(t, 1, linked)
                dve.wait_ge(group_summed, t + 1)
                linked(nc.vector.tensor_reduce(pair_score[:], small_ps[:, 256:256 + P].rearrange(
                    "p (n c) -> p n c", c=2), AX_X, ALU.add))
                half = SEL_BLOCKS - 1
                nc.vector.tensor_tensor(block_score[:, 0:half], pair_score[:, 0:half], pair_score[:, half:2 * half],
                                        ALU.add).then_inc(link, 1)
                linked.n += 1
                dve.wait_ge(link, linked.base + linked.n)
                linked(nc.vector.memset(block_score[:, 0:1], FORCED))
                linked(nc.vector.memset(block_score[:, half - 1:half + 1], FORCED))
                for r in range(TOP_ROUNDS):
                    nc.vector.memset(spare[:], 0.0)
                    linked(nc.vector.max(top[:, r], block_score[:]))
                    nc.vector.memset(spare[:], 0.0)
                    linked(nc.vector.match_replace(block_score[:], top[:, r], block_score[:], MASKED))
                linked(nc.vector.tensor_scalar(unselected[:], block_score[:], 0.0, MASKED, ALU.is_ge, ALU.mult))
                linked(nc.vector.tensor_scalar(sel_bias[:], unselected[:], far, None, ALU.add))
                linked(nc.vector.tensor_tensor(
                    near_bias[:].rearrange("p (n k) -> p n k", k=SEL_LEN),
                    g.bias_near[:, 0:P].rearrange("p (n k) -> p n k", k=SEL_LEN),
                    unselected[:, half - 2:half].unsqueeze(2).to_broadcast([P, 2, SEL_LEN]), ALU.add))
                for n in range(2, HALVES):
                    keys(t, n, linked)
                    if n % 2 == 1:
                        take_scores(t, n // 2 - 1)
                take_scores(t, CHUNKS)
                dve.wait_ge(s_taken, t * CH + CH)
                nc.vector.tensor_reduce(neg_max[:, 1:2], s[:, S_SEL:S_WIN], AX_X, ALU.max)
                linked(nc.vector.tensor_reduce(neg_max[:, 2:3], s[:, S_WIN:S_COLS], AX_X, ALU.max))
                nc.vector.tensor_scalar(neg_max[:, 1:3], neg_max[:, 1:3], 0.1 * MASKED, -1.0, ALU.max, ALU.mult
                                        ).then_inc(negated, 1)
                dve.wait_ge(exped, t * 2 + 2)
                linked(nc.vector.tensor_scalar(sums[:, 1:3], sums[:, 1:3], 1e-30, None, ALU.max))
                linked(nc.vector.reciprocal(coef[:, 1:3], sums[:, 1:3]))
                gates = g.gates_sampled[:, bass.ds(t, 1)].squeeze(1)
                linked(nc.vector.tensor_tensor(coef[:, 1:3], coef[:, 1:3], gates[:, 1:3], ALU.mult))
                nc.vector.tensor_scalar(s[:, 0:P], s[:, 0:P], gates[:, 0:1], None, ALU.mult)
                nc.vector.tensor_scalar(s[:, S_SEL:S_WIN], s[:, S_SEL:S_WIN], coef[:, 1:2], None, ALU.mult)
                nc.vector.tensor_scalar(s[:, S_WIN:S_COLS], s[:, S_WIN:S_COLS], coef[:, 2:3], None, ALU.mult
                                        ).then_inc(scaled, 1)
                dve.wait_ge(multiplied, t + 1)
                nc.vector.tensor_copy(o[:], o_ps[:, 0:HD]).then_inc(o_taken, 1)
                dve.wait_ge(o_turned, t + 1)
                for j in range(4):
                    b, h = divmod(j, 2)
                    nc.vector.tensor_copy(
                        g.h[:, h * HPG:(h + 1) * HPG, bass.ds(t * (2 * STEP) + (SEQ + b * STEP), STEP)],
                        small_ps[:, 384 + 32 * j:384 + 32 * j + HPG * STEP].rearrange("p (h l) -> p h l", l=STEP))
                return linked.n

            per_turn = body(0, setup)
            with dve.Fori(1, PAIRS) as t:
                assert body(t, t * per_turn + setup) == per_turn


def attend_memory_sampled(nc, g, a, layer, query, out):
    with ExitStack() as ctx:
        sb = lambda n, s: ctx.enter_context(nc.sbuf_tensor(f"mem{layer}_{n}", s, F32))
        ps = lambda n, s: ctx.enter_context(nc.psum_tensor(f"mem{layer}_{n}", s, F32))
        sem = counters(nc, ctx, f"mem{layer}_")
        q = sb("q", [P, MEM_HEADS, BATCH, SAMPLED])
        stage = sb("stage", [P, 2, QT, MEM_WIDTH])
        squares = sb("squares", [P, 2, QT * MEM_WIDTH])
        ss = sb("ss", [P, 2, QT * MEM_HEADS])
        turned_k = sb("turned_k", [P, 2, MEM_HEADS, MEM_LEN])
        values = g.ring[:].rearrange("p b k n -> p (b k) n").rearrange("p (b t) n -> p b t n", t=QT)
        s = sb("s", [P, MEM_LEN])
        probs = sb("probs", [P, QT, MEM_HEADS, BATCH, SAMPLED])
        stat = sb("stat", [P, 3])
        o = sb("o", [P, HD])
        k_ps = ps("k_ps", [P, 2, 2, 512])
        s_ps = ps("s_ps", [P, 512])
        t_ps = ps("t_ps", [P, 512])
        o_ps = ps("o_ps", [P, 512])
        blank, q_placed, k_squared, k_mean, k_root, k_inverse, k_scaled, k_turned, k_copied, scored, negated, exped, \
            scaled, turned, placed, multiplied, o_taken, o_turned, values_loaded, link = map(sem, (
                "blank", "q_placed", "k_squared", "k_mean", "k_root", "k_inverse", "k_scaled", "k_turned", "k_copied",
                "scored", "negated", "exped", "scaled", "turned", "placed", "multiplied", "o_taken", "o_turned",
                "values_loaded", "link"))
        loaded = [sem(f"loaded{b}") for b in range(2)]
        block = ctx.enter_context(nc.Block())
        rows = a.cache_mem_kv[layer].rearrange("b (t p) k h d -> b p t k (h d)", p=P)

        @block.sync
        def _(sp):
            for b in range(BATCH):
                wait(sp, k_turned, b - 1)
                sp.dma_start(stage[:, b % 2], rows[b, :, :, 0]).then_inc(loaded[b % 2], 16)
                sp.dma_start(values[:, b], rows[b, :, :, 1]).then_inc(values_loaded, 16)

        @block.gpsimd
        def _(pool):
            nc.gpsimd.memset(q[:], 0.0).then_inc(blank, 1)
            nc.gpsimd.memset(probs[:], 0.0).then_inc(blank, 1)
            for b in range(BATCH):
                pool.wait_ge(k_inverse, b + 1)
                k = stage[:, b % 2].rearrange("p t (h d) -> p (t h) d", d=HD)
                nc.gpsimd.tensor_tensor(k, k, ss[:, b % 2].unsqueeze(2).to_broadcast([P, QT * MEM_HEADS, HD]),
                                        ALU.mult).then_inc(k_scaled, 1)

        @block.tensor
        def _(pe):
            pe.wait_ge(q_placed, BATCH)

            def turn(b):
                pe.wait_ge(k_scaled, b + 1)
                wait(pe, k_copied, b - 1)
                for h in range(MEM_HEADS):
                    for t in range(QT):
                        mm = nc.tensor.transpose(k_ps[:, b % 2, h // 2, (h % 2 * QT + t) * P:(h % 2 * QT + t + 1) * P],
                                                 stage[:, b % 2, t, h * HD:(h + 1) * HD], g.ident[:])
                mm.then_inc(k_turned, 1)

            turn(0)
            for b in range(BATCH):
                if b + 1 < BATCH:
                    turn(b + 1)
                pe.wait_ge(k_copied, b + 1)
                for h in range(MEM_HEADS):
                    mm = nc.tensor.matmul(s_ps[32 * h:32 * h + 32, 0:MEM_LEN], q[:, h, b], turned_k[:, b % 2, h],
                                          start=(b == 0), stop=(b == BATCH - 1), skip_group_check=True)
                mm.then_inc(scored, 1)
            pe.wait_ge(scaled, 1)
            for t in range(QT):
                mm = nc.tensor.transpose(t_ps[:, t * P:(t + 1) * P], s[:, t * P:(t + 1) * P], g.ident[:])
            mm.then_inc(turned, 1)
            pe.wait_ge(placed, BATCH)
            pe.wait_ge(values_loaded, 16 * BATCH)
            for b in range(BATCH):
                for t in range(QT):
                    for h in range(MEM_HEADS):
                        mm = nc.tensor.matmul(o_ps[32 * h:32 * h + 32, 0:HD], probs[:, t, h, b],
                                              values[:, b, t, h * HD:(h + 1) * HD], start=(b == 0 and t == 0),
                                              stop=(b == BATCH - 1 and t == QT - 1), skip_group_check=True)
            mm.then_inc(multiplied, 1)
            pe.wait_ge(o_taken, 1)
            nc.tensor.transpose(t_ps[:, 384:512], o[:], g.ident[:]).then_inc(o_turned, 1)

        @block.scalar
        def _(act):
            def square(b):
                act.wait_ge(loaded[b % 2], 16 * (b // 2 + 1))
                wait(act, k_mean, b - 1)
                nc.scalar.activation(squares[:, b % 2], stage[:, b % 2].rearrange("p t n -> p (t n)"), ACT.Square
                                     ).then_inc(k_squared, 1)
            square(0)
            for b in range(BATCH):
                act.wait_ge(k_mean, b + 1)
                nc.scalar.activation(ss[:, b % 2], ss[:, b % 2], ACT.Sqrt).then_inc(k_root, 1)
                if b + 1 < BATCH:
                    square(b + 1)
                act.wait_ge(k_turned, b + 1)
                wait(act, scored, b - 1)
                gk = VEC["g_mem_k"] + layer
                nc.scalar.activation(turned_k[:, b % 2].rearrange("p (u h) k -> p u (h k)", u=2), k_ps[:, b % 2],
                                     ACT.Copy, scale=g.vec[:, gk:gk + 1]).then_inc(k_copied, 1)
            act.wait_ge(negated, 1)
            nc.scalar.activation(s[:], s_ps[:, 0:MEM_LEN], ACT.Exp, bias=stat[:, 0:1], accum_out=stat[:, 1:2]
                                 ).then_inc(exped, 1)

        @block.vector
        def _(dve):
            linked = Chain(dve, link)
            dve.wait_ge(blank, 2)
            for b in range(BATCH):
                cols = slice(b * STEP, (b + 1) * STEP)
                nc.vector.tensor_copy(q[:, :, b, cols], query[:, :, cols]).then_inc(q_placed, 1)
            for b in range(BATCH):
                dve.wait_ge(k_squared, b + 1)
                wait(dve, k_scaled, b - 1)
                linked(nc.vector.tensor_reduce(ss[:, b % 2], squares[:, b % 2].rearrange("p (c d) -> p c d", d=HD),
                                               AX_X, ALU.add))
                nc.vector.tensor_scalar(ss[:, b % 2], ss[:, b % 2], 1.0 / HD, EPS, ALU.mult, ALU.add
                                        ).then_inc(k_mean, 1)
                dve.wait_ge(k_root, b + 1)
                nc.vector.reciprocal(ss[:, b % 2], ss[:, b % 2]).then_inc(k_inverse, 1)
            dve.wait_ge(scored, BATCH)
            linked(nc.vector.tensor_reduce(stat[:, 0:1], s_ps[:, 0:MEM_LEN], AX_X, ALU.max))
            nc.vector.tensor_scalar(stat[:, 0:1], stat[:, 0:1], -1.0, None, ALU.mult).then_inc(negated, 1)
            dve.wait_ge(exped, 1)
            linked(nc.vector.reciprocal(stat[:, 2:3], stat[:, 1:2]))
            nc.vector.tensor_scalar(s[:], s[:], stat[:, 2:3], None, ALU.mult).then_inc(scaled, 1)
            dve.wait_ge(turned, 1)
            for b in range(BATCH):
                cols = slice(b * STEP, (b + 1) * STEP)
                nc.vector.tensor_copy(probs[:, :, :, b, cols], t_ps[:, 0:QT * P].rearrange(
                    "p (t h n) -> p t h n", t=QT, h=MEM_HEADS)[:, :, :, cols]).then_inc(placed, 1)
            dve.wait_ge(multiplied, 1)
            nc.vector.tensor_copy(o[:], o_ps[:, 0:HD]).then_inc(o_taken, 1)
            dve.wait_ge(o_turned, 1)
            nc.vector.tensor_copy(out, t_ps[:, 384:512].rearrange("p (h n) -> p h n", h=MEM_HEADS))


Q_TILE, K_TILE, V_TILE, R_TILE, GLA_MEM_Q = 0, GLA_KT, 2 * GLA_KT, 4 * GLA_KT, 6 * GLA_KT
ET = GLA_DV // P
V_TILES = GLA_HEADS * ET
LAST = SEQ - 1


def head_pieces(h):
    first, last = h * GLA_DK, (h + 1) * GLA_DK
    return [(t, slice(max(first - t * P, 0), min(last - t * P, P)))
            for t in range(first // P, -(-last // P))]


def by_batch(ap):
    return ap.rearrange("p k (b l) -> p k b l", l=STEP)


def prepare_linear(nc, g, a):
    with ExitStack() as ctx:
        sb = lambda n, s: ctx.enter_context(nc.sbuf_tensor(f"lin_{n}", s, F32))
        sem = counters(nc, ctx, "lin_")
        w_a2 = sb("w_a2", [GATE_RANK, GLA_KW])
        keep = sb("keep", [P, GLA_KT, TOKENS])
        z, neg, expo = g.h[:, 0:GLA_KT], g.h[:, GLA_KT:2 * GLA_KT], sb("expo", [P, GLA_KT, TOKENS])
        to_end, k_end = g.p[:, V_TILE:V_TILE + GLA_KT], g.p[:, V_TILE + GLA_KT:V_TILE + 2 * GLA_KT]
        z_ps = ctx.enter_context(nc.psum_tensor("lin_z_ps", [P, GLA_KT, 512], F32))
        rows_ps = ctx.enter_context(nc.psum_tensor("lin_rows_ps", [P, 2, 512], F32))
        loaded, blank, z_done, turned, rows_copied, neg_done, exped, plus_one, logged, link, end_diff, end_exped, \
            start_exped, k_done, pool_link = map(sem, (
                "loaded", "blank", "z_done", "turned", "rows_copied", "neg_done", "exped", "plus_one", "logged",
                "link", "end_diff", "end_exped", "start_exped", "k_done", "pool_link"))
        block = ctx.enter_context(nc.Block())
        width = lambda tok: P if tok < QT else SAMPLED
        v_sets = [(V_TILE + 4 * s, 4, tok, g.v_rows, s * 512) for s in range(V_TILES // 4) for tok in range(QT + 1)]
        k_sets = [(V_TILE + GLA_KT + first, n, tok, g.k_rows, first * P) for first, n in ((0, 4), (4, 2))
                  for tok in range(QT + 1)]
        decay = g.decay

        @block.sync
        def _(sp):
            sp.dma_start(w_a2[:], a.gla_w_a2[0]).then_inc(loaded, 16)
            sp.dma_start(g.linear_masks[:], a.linear_masks).then_inc(loaded, 16)
            sp.wait_ge(loaded, 32)

        @block.gpsimd
        def _(pool):
            linked = Chain(pool, pool_link)
            linked(nc.gpsimd.memset(keep[:], 1.0))
            nc.gpsimd.memset(keep[:, :, 0:1], 0.0)
            nc.gpsimd.memset(keep[:, :, SEQ:TOKENS:STEP], 0.0).then_inc(blank, 1)
            queries = g.p[:, Q_TILE:Q_TILE + GLA_KT]
            linked(nc.gpsimd.tensor_scalar(queries, queries, GLA_DK ** -0.5, None, ALU.mult))
            pool.wait_ge(start_exped, 1)
            nc.gpsimd.tensor_tensor(g.q_start[:], g.from_start[:], queries[:, :, SEQ:TOKENS], ALU.mult)

        @block.tensor
        def _(pe):
            pe.wait_ge(loaded, 32)
            for t in range(GLA_KT):
                mm = nc.tensor.matmul(z_ps[:, t, 0:TOKENS], w_a2[:, t * P:(t + 1) * P], g.gates[0:GATE_RANK],
                                      start=True, stop=True)
            mm.then_inc(z_done, 1)
            for n, (tile, count, tok, _, _) in enumerate(v_sets + k_sets):
                if n == len(v_sets):
                    pe.wait_ge(k_done, 1)
                wait(pe, rows_copied, n - 1)
                for o in range(count):
                    mm = nc.tensor.transpose(rows_ps[0:width(tok), n % 2, o * P:(o + 1) * P],
                                             g.p[:, tile + o, tok * P:tok * P + width(tok)], g.ident[:])
                mm.then_inc(turned, 1)

        @block.scalar
        def _(act):
            def copy(n):
                _, count, tok, rows, col = (v_sets + k_sets)[n]
                act.wait_ge(turned, n + 1)
                nc.scalar.activation(rows[0:width(tok), tok, col:col + count * P],
                                     rows_ps[0:width(tok), n % 2, 0:count * P], ACT.Copy).then_inc(rows_copied, 1)

            for n in range(3):
                copy(n)
            act.wait_ge(neg_done, 1)
            nc.scalar.activation(expo[:], expo[:], ACT.Exp).then_inc(exped, 1)
            for n in range(3, 6):
                copy(n)
            act.wait_ge(plus_one, 1)
            nc.scalar.activation(expo[:], expo[:], ACT.Ln).then_inc(logged, 1)
            for n in range(6, len(v_sets)):
                copy(n)
            act.wait_ge(end_diff, 1)
            nc.scalar.activation(to_end, to_end, ACT.Exp, scale=1.0 / GATE_TAU).then_inc(end_exped, 1)
            nc.scalar.activation(g.from_start[:], decay[:, :, SEQ:TOKENS], ACT.Exp, scale=1.0 / GATE_TAU
                                 ).then_inc(start_exped, 1)
            for n in range(len(v_sets), len(v_sets) + len(k_sets)):
                copy(n)

        @block.vector
        def _(dve):
            linked = Chain(dve, link)
            dve.wait_ge(z_done, 1)
            for t in range(GLA_KT):
                col = g.vec[:, VEC["gla_b_a"] + t:VEC["gla_b_a"] + t + 1]
                last = nc.vector.tensor_scalar(z[:, t], z_ps[:, t, 0:TOKENS], col, None, ALU.add)
            linked(last)
            linked(nc.vector.tensor_scalar(neg, z, 0.0, None, ALU.min))
            nc.vector.scalar_tensor_tensor(expo[:], neg, 2.0, z, ALU.mult, ALU.subtract).then_inc(neg_done, 1)
            dve.wait_ge(exped, 1)
            nc.vector.tensor_scalar(expo[:], expo[:], 1.0, None, ALU.add).then_inc(plus_one, 1)
            dve.wait_ge(logged, 1)
            linked(nc.vector.tensor_tensor(expo[:], neg, expo[:], ALU.subtract))
            dve.wait_ge(blank, 1)
            flat = lambda t: t.rearrange("p k n -> p (k n)")
            linked(nc.vector.tensor_tensor_scan(flat(decay[:]), flat(keep[:]), flat(expo[:]), 0.0, ALU.mult, ALU.add))
            dve.wait_ge(turned, len(v_sets))
            nc.vector.tensor_tensor(to_end[:, :, 0:SEQ], decay[:, :, LAST:SEQ].to_broadcast([P, GLA_KT, SEQ]),
                                    decay[:, :, 0:SEQ], ALU.subtract)
            sampled = by_batch(decay[:, :, SEQ:TOKENS])
            nc.vector.tensor_tensor(by_batch(to_end[:, :, SEQ:TOKENS]),
                                    sampled[:, :, :, STEP - 1:STEP].to_broadcast([P, GLA_KT, BATCH, STEP]),
                                    sampled, ALU.subtract).then_inc(end_diff, 1)
            dve.wait_ge(end_exped, 1)
            nc.vector.tensor_tensor(k_end, to_end, g.p[:, K_TILE:K_TILE + GLA_KT], ALU.mult).then_inc(k_done, 1)


def score_levels(nc, g):
    CROSS = LEVELS
    with ExitStack() as ctx:
        sb = lambda n, s: ctx.enter_context(nc.sbuf_tensor(f"lev_{n}", s, F32))
        sem = counters(nc, ctx, "lev_")
        own = sb("decayed", [P, 2, GLA_KT, TOKENS])
        decayed_q = [g.h[:, 0:GLA_KT], own[:, 0]]
        decayed_k = [g.h[:, GLA_KT:2 * GLA_KT], own[:, 1]]
        factor = [g.p[:, V_TILE:V_TILE + GLA_KT], g.p[:, V_TILE + GLA_KT:V_TILE + 2 * GLA_KT]]
        masked_to = [g.mem_k[:, 0].rearrange("p h (t i) -> p h t i", t=QT),
                     g.mem_v[:, 0].rearrange("p t n -> p (t n)").rearrange("p (h t i) -> p h t i", h=GLA_HEADS, t=QT)]
        few = sb("few", [SAMPLED, 2, GLA_HEADS, SAMPLED])
        ps = ctx.enter_context(nc.psum_tensor("lev_ps", [P, 2, GLA_HEADS, 512], F32))
        diffed, distanced, exped, q_decayed, k_decayed, scored, masked, added = map(sem, (
            "diffed", "distanced", "exped", "q_decayed", "k_decayed", "scored", "masked", "added"))
        block = ctx.enter_context(nc.Block())
        q, k = g.p[:, Q_TILE:Q_TILE + GLA_KT], g.p[:, K_TILE:K_TILE + GLA_KT]
        few_levels = [0, 1, 2]

        def span(level):
            return TOKENS if level in few_levels else SEQ

        def blocked(ap, level):
            return ap.rearrange("p k (n c) -> p k n c", c=2 ** level)

        @block.vector
        def _(dve):
            def diff(level):
                w, c = span(level), 2 ** level
                wait(dve, k_decayed, level - 2)
                d = blocked(g.decay[:, :, 0:w], level)
                nc.vector.tensor_tensor(
                    blocked(factor[level % 2][:, :, 0:w], level), d,
                    d[:, :, :, c // 2 - 1:c // 2].to_broadcast([P, GLA_KT, w // c, c]),
                    ALU.subtract).then_inc(diffed, 1)

            def queries(level):
                w = span(level)
                dve.wait_ge(exped, level)
                wait(dve, scored, level - 1)
                nc.vector.tensor_tensor(decayed_q[level % 2][:, :, 0:w], q[:, :, 0:w], factor[level % 2][:, :, 0:w],
                                        ALU.mult).then_inc(q_decayed, 1)

            def mask(level):
                dve.wait_ge(scored, level + 1)
                src = ps[:, level % 2]
                if level == CROSS:
                    nc.vector.tensor_copy(g.att[:, :, 1], src[:, :, 0:P]).then_inc(masked, 1)
                    return
                wait(dve, added, level - 2)
                m = g.linear_masks[:, level * P:(level + 1) * P]
                last = nc.vector.tensor_tensor(
                    g.att[:, :, 0:3:2] if level == 0 else masked_to[level % 2],
                    src[:, :, 0:SEQ].rearrange("p h (t i) -> p h t i", t=QT),
                    m.unsqueeze(1).unsqueeze(1).to_broadcast([P, GLA_HEADS, QT, P]), ALU.mult)
                if level in few_levels:
                    last = nc.vector.tensor_tensor(
                        g.att[0:SAMPLED, :, 3, 0:SAMPLED] if level == 0 else few[:, level % 2],
                        src[0:SAMPLED, :, SEQ:TOKENS],
                        m[0:SAMPLED, 0:SAMPLED].unsqueeze(1).to_broadcast([SAMPLED, GLA_HEADS, SAMPLED]), ALU.mult)
                last.then_inc(masked, 1)

            diff(1)
            diff(2)
            for level in range(CROSS + 1):
                if level + 1 <= CROSS:
                    queries(level + 1)
                if level + 3 <= CROSS:
                    diff(level + 3)
                mask(level)

        @block.scalar
        def _(act):
            for level in range(1, CROSS + 1):
                f = factor[level % 2][:, :, 0:span(level)]
                act.wait_ge(diffed, level)
                nc.scalar.activation(f, f, ACT.Abs).then_inc(distanced, 1)
                act.wait_ge(distanced, level)
                nc.scalar.activation(f, f, ACT.Exp, scale=-1.0 / GATE_TAU).then_inc(exped, 1)

        @block.gpsimd
        def _(pool):
            def keys(level):
                w = span(level)
                pool.wait_ge(exped, level)
                wait(pool, scored, level - 1)
                pool.wait_ge(q_decayed, level)
                nc.gpsimd.tensor_tensor(decayed_k[level % 2][:, :, 0:w], k[:, :, 0:w], factor[level % 2][:, :, 0:w],
                                        ALU.mult).then_inc(k_decayed, 1)

            def add(level):
                pool.wait_ge(masked, level + 1)
                wait(pool, added, level - 1)
                to = g.att[:, :, 0:3:2]
                last = nc.gpsimd.tensor_tensor(to, to, masked_to[level % 2], ALU.add)
                if level in few_levels:
                    to = g.att[0:SAMPLED, :, 3, 0:SAMPLED]
                    last = nc.gpsimd.tensor_tensor(to, to, few[:, level % 2], ALU.add)
                last.then_inc(added, 1)

            for level in range(1, CROSS + 1):
                keys(level)
                if level >= 2:
                    add(level - 1)

        @block.tensor
        def _(pe):
            for level in range(CROSS + 1):
                lq, lk = (q, k) if level == 0 else (decayed_q[level % 2], decayed_k[level % 2])
                wait(pe, k_decayed, level)
                wait(pe, masked, level - 1)
                spans = [(slice(0, P), slice(P, SEQ), 0)] if level == CROSS else \
                    [(slice(t * P, (t + 1) * P), slice(t * P, (t + 1) * P), t * P) for t in range(QT)]
                if level in few_levels:
                    spans.append((slice(SEQ, TOKENS), slice(SEQ, TOKENS), SEQ))
                for h in range(GLA_HEADS):
                    for keys, queries, col in spans:
                        n = keys.stop - keys.start
                        pieces = head_pieces(h)
                        for e, (t, rows) in enumerate(pieces):
                            mm = nc.tensor.matmul(ps[0:n, level % 2, h, col:col + n], lk[rows, t, keys],
                                                  lq[rows, t, queries], start=(e == 0), stop=(e == len(pieces) - 1))
                mm.then_inc(scored, 1)


def linear_outputs(nc, g, a):
    with ExitStack() as ctx:
        sb = lambda n, s: ctx.enter_context(nc.sbuf_tensor(f"linout_{n}", s, F32))
        ps = lambda n, s: ctx.enter_context(nc.psum_tensor(f"linout_{n}", s, F32))
        sem = counters(nc, ctx, "linout_")
        size = GLA_KT * GLA_DV
        before = g.ring[:].rearrange("p b k n -> p (b k n)")[:, 0:2 * size].rearrange(
            "p (b t e) -> p b t e", b=2, t=GLA_KT)
        after = g.p[:, Q_TILE:R_TILE].rearrange("p k n -> p (k n)")[:, 0:3 * size].rearrange(
            "p (b t e) -> p b t e", b=3, t=GLA_KT)
        own_q = sb("own_q", [P, 2, GLA_KT, SAMPLED])
        own_k = sb("own_k", [SAMPLED, 2, GLA_KW])
        o_rows = sb("o_rows", [P, GLA_DV])
        o_ps = ps("o_ps", [P, 2, 512])
        state_ps = ps("state_ps", [P, 2, 512])
        few_ps = ps("few_ps", [P, 512])
        turn_ps = ps("turn_ps", [P, 512])
        loaded = [sem(f"loaded{b}") for b in range(2)]
        own_done, o_done, o_copied, state_done, state_taken, few_done, few_copied, few_turned, \
            prompt_stored = map(sem, (
            "own_done", "o_done", "o_copied", "state_done", "state_taken", "few_done", "few_copied", "few_turned",
                "prompt_stored"))
        stored = [sem(f"stored{b}") for b in range(2)]
        block = ctx.enter_context(nc.Block())
        states = a.state_gla[0].rearrange("b h k v -> b (h k) v").rearrange("b (t p) v -> b p t v", p=P)
        new_states = a.gla_sample[0].rearrange("b h k v -> b (h k) v").rearrange("b (t p) v -> b p t v", p=P)
        prompt_state = a.gla_prompt[0, 0].rearrange("h k v -> (h k) v").rearrange("(t p) v -> p t v", p=P)
        v = lambda tok, h, rows: g.v_rows[rows, tok, h * GLA_DV:(h + 1) * GLA_DV]
        owners = [[(h, rows) for h in range(GLA_HEADS) for tile, rows in head_pieces(h) if tile == t]
                  for t in range(GLA_KT)]

        def twos(eng, body):
            body(0, False)
            with eng.Fori(1, BATCH // 2 - 1) as m:
                body(m, False)
            body(BATCH // 2 - 1, True)

        @block.sync
        def _(sp):
            for b in range(2):
                sp.dma_start(before[:, b], states[b]).then_inc(loaded[b], 16)
            sp.wait_ge(state_taken, GLA_KT)
            sp.dma_start(prompt_state, after[:, 2]).then_inc(prompt_stored, 16)

            def body(m, last):
                for half in range(2):
                    sp.wait_ge(state_taken, m * (2 * GLA_KT) + GLA_KT * (half + 2))
                    sp.dma_start(new_states[bass.ds(m * 2 + half, 1)].squeeze(0), after[:, half]
                                 ).then_inc(stored[half], 16)
                    if not last:
                        sp.dma_start(before[:, half], states[bass.ds(m * 2 + (half + 2), 1)].squeeze(0)
                                     ).then_inc(loaded[half], 16)
            twos(sp, body)
            sp.wait_ge(prompt_stored, 16)
            for half in range(2):
                sp.wait_ge(stored[half], 16 * (BATCH // 2))

        @block.gpsimd
        def _(pool):
            tokens_of = g.linear_masks[:, LIN_TOKENS:LIN_TOKENS + BATCH * SAMPLED]
            rows_of = g.linear_masks[0:SAMPLED, LIN_ROWS:LIN_ROWS + BATCH]

            def body(m, last):
                for half in range(2):
                    wait(pool, state_done, m * (2 * GLA_KT) + GLA_KT * half)
                    nc.gpsimd.tensor_tensor(
                        own_q[:, half], g.q_start[:],
                        tokens_of[:, bass.ds(m * (2 * SAMPLED) + half * SAMPLED, SAMPLED)].unsqueeze(1).to_broadcast(
                            [P, GLA_KT, SAMPLED]), ALU.mult)
                    nc.gpsimd.tensor_tensor(
                        own_k[:, half], g.k_rows[0:SAMPLED, QT],
                        rows_of[:, bass.ds(m * 2 + half, 1)].to_broadcast([SAMPLED, GLA_KW]), ALU.mult
                    ).then_inc(own_done, 1)
            twos(pool, body)

        @block.tensor
        def _(pe):
            for n in range(V_TILES):
                wait(pe, o_copied, n - 1)
                h = n // ET
                at = g.att[:, h].rearrange("p t i -> p (t i)")
                nc.tensor.matmul(o_ps[:, n % 2, 0:SEQ], g.v_rows[:, 0, n * P:(n + 1) * P], at[:, 0:SEQ], start=True,
                                 stop=False, skip_group_check=True)
                nc.tensor.matmul(o_ps[:, n % 2, P:SEQ], g.v_rows[:, 1, n * P:(n + 1) * P], at[:, SEQ:SEQ + P],
                                 start=False, stop=True, skip_group_check=True).then_inc(o_done, 1)
            for t in range(GLA_KT):
                wait(pe, state_taken, t - 1)
                for h, rows in owners[t]:
                    for tok in range(QT):
                        mm = nc.tensor.matmul(state_ps[rows, t % 2, 0:GLA_DV],
                                              g.k_rows[:, tok, t * P + rows.start:t * P + rows.stop],
                                              v(tok, h, slice(0, P)), start=(tok == 0), stop=(tok == QT - 1),
                                              skip_group_check=True)
                mm.then_inc(state_done, 1)
            for h in range(GLA_HEADS):
                nc.tensor.matmul(few_ps[32 * h:32 * h + 32, 0:GLA_DV], g.att[0:SAMPLED, h, 3, 0:SAMPLED],
                                 v(QT, h, slice(0, SAMPLED)), start=True, stop=False, skip_group_check=True)

            def body(m, last):
                for half in range(2):
                    pe.wait_ge(own_done, m * 2 + (half + 1))
                    pe.wait_ge(loaded[half], m * 16 + 16)
                    for e in range(2):
                        for h in range(GLA_HEADS):
                            t, rows = head_pieces(h)[e]
                            mm = nc.tensor.matmul(few_ps[32 * h:32 * h + 32, 0:GLA_DV], own_q[rows, half, t],
                                                  before[rows, half, t], start=False,
                                                  stop=(last and half == 1 and e == 1), skip_group_check=True)
                    if last and half == 1:
                        mm.then_inc(few_done, 1)
                    for t in range(GLA_KT):
                        pe.wait_ge(state_taken, m * (2 * GLA_KT) + (GLA_KT * (half + 1) + t - 1))
                        for h, rows in owners[t]:
                            mm = nc.tensor.matmul(state_ps[rows, t % 2, 0:GLA_DV],
                                                  own_k[:, half, t * P + rows.start:t * P + rows.stop],
                                                  v(QT, h, slice(0, SAMPLED)), start=True, stop=True,
                                                  skip_group_check=True)
                        mm.then_inc(state_done, 1)
            twos(pe, body)
            pe.wait_ge(few_copied, 1)
            for e in range(ET):
                mm = nc.tensor.transpose(turn_ps[:, e * P:(e + 1) * P], o_rows[:, e * P:(e + 1) * P], g.ident[:])
            mm.then_inc(few_turned, 1)

        @block.scalar
        def _(act):
            for n in range(V_TILES):
                act.wait_ge(o_done, n + 1)
                nc.scalar.activation(g.h[:, n, 0:SEQ], o_ps[:, n % 2, 0:SEQ], ACT.Copy).then_inc(o_copied, 1)
            act.wait_ge(few_done, 1)
            nc.scalar.activation(o_rows[:], few_ps[:, 0:GLA_DV], ACT.Copy).then_inc(few_copied, 1)
            act.wait_ge(few_turned, 1)
            for h in range(GLA_HEADS):
                nc.scalar.activation(
                    g.h[:, h * ET:(h + 1) * ET, SEQ:TOKENS],
                    turn_ps[:, 0:ET * P].rearrange("p (e n) -> p e n", e=ET)[:, :, h * SAMPLED:(h + 1) * SAMPLED],
                    ACT.Copy)

        @block.vector
        def _(dve):
            for t in range(GLA_KT):
                dve.wait_ge(state_done, t + 1)
                nc.vector.tensor_copy(after[:, 2, t], state_ps[:, t % 2, 0:GLA_DV]).then_inc(state_taken, 1)

            def body(m, last):
                for half in range(2):
                    wait(dve, stored[half], m * 16)
                    for t in range(GLA_KT):
                        dve.wait_ge(state_done, m * (2 * GLA_KT) + (GLA_KT * (half + 1) + t + 1))
                        col = g.from_start[:, t, bass.ds(m * (2 * STEP) + (half * STEP + STEP - 1), 1)]
                        nc.vector.scalar_tensor_tensor(after[:, half, t], before[:, half, t], col,
                                                       state_ps[:, t % 2, 0:GLA_DV], ALU.mult, ALU.add
                                                       ).then_inc(state_taken, 1)
            twos(dve, body)


def finish_linear(nc, g, next_chunks, base):
    with ExitStack() as ctx:
        sb = lambda n, s: ctx.enter_context(nc.sbuf_tensor(f"fin_{n}", s, F32))
        sem = counters(nc, ctx, "fin_")
        squares = g.p[:, V_TILE:V_TILE + V_TILES]
        swish = sb("swish", [P, V_TILES, TOKENS])
        rstd = sb("rstd", [P, GLA_HEADS, TOKENS])
        ps = ctx.enter_context(nc.psum_tensor("fin_ps", [P, GLA_HEADS, 512], F32))
        squared, summed, mean, root, exped, silu_link, silu_done, link = map(sem, (
            "squared", "summed", "mean", "root", "exped", "silu_link", "silu_done", "link"))
        block = ctx.enter_context(nc.Block())
        tiles = lambda h: slice(h * ET, (h + 1) * ET)
        r = g.p[:, R_TILE:R_TILE + V_TILES]

        @block.sync
        def _(sp):
            load_first_chunks(sp, g, next_chunks, base)

        @block.gpsimd
        def _(pool):
            for h in range(GLA_HEADS):
                pool.wait_ge(exped, h + 1)
                s = swish[:, tiles(h)]
                nc.gpsimd.tensor_scalar(s, s, 1.0, None, ALU.add).then_inc(silu_link, 1)

        @block.tensor
        def _(pe):
            for h in range(GLA_HEADS):
                pe.wait_ge(squared, h + 1)
                for e in range(ET):
                    mm = nc.tensor.matmul(ps[:, h, 0:TOKENS], g.ones[:], squares[:, h * ET + e], start=(e == 0),
                                          stop=(e == ET - 1))
                mm.then_inc(summed, 1)

        @block.scalar
        def _(act):
            for h in range(GLA_HEADS):
                nc.scalar.activation(squares[:, tiles(h)], g.h[:, tiles(h)], ACT.Square).then_inc(squared, 1)
            for h in range(GLA_HEADS):
                nc.scalar.activation(swish[:, tiles(h)], r[:, tiles(h)], ACT.Exp, scale=-1.0).then_inc(exped, 1)
            act.wait_ge(mean, 1)
            nc.scalar.activation(rstd[:], rstd[:], ACT.Sqrt).then_inc(root, 1)

        @block.vector
        def _(dve):
            linked = Chain(dve, link)
            dve.wait_ge(summed, GLA_HEADS)
            nc.vector.tensor_scalar(rstd[:], ps[:, :, 0:TOKENS], 1.0 / GLA_DV, EPS, ALU.mult, ALU.add
                                    ).then_inc(mean, 1)
            for h in range(GLA_HEADS):
                dve.wait_ge(silu_link, h + 1)
                s = swish[:, tiles(h)]
                linked(nc.vector.reciprocal(s, s))
                nc.vector.tensor_tensor(s, s, r[:, tiles(h)], ALU.mult).then_inc(silu_done, 1)
            dve.wait_ge(root, 1)
            linked(nc.vector.reciprocal(rstd[:], rstd[:]))
            for h in range(GLA_HEADS):
                for e in range(ET):
                    gain = VEC["gla_g_o"] + e
                    last = nc.vector.scalar_tensor_tensor(g.h[:, h * ET + e], g.h[:, h * ET + e],
                                                          g.vec[:, gain:gain + 1], rstd[:, h], ALU.mult, ALU.mult)
                linked(last)
                dve.wait_ge(silu_done, h + 1)
                nc.vector.tensor_tensor(g.h[:, tiles(h)], g.h[:, tiles(h)], swish[:, tiles(h)], ALU.mult)


def normalize_queries(nc, g, layer, first):
    with ExitStack() as ctx:
        sem = counters(nc, ctx, f"qnorm{layer}_")
        squares = ctx.enter_context(nc.sbuf_tensor(f"qnorm{layer}_squares", [P, MEM_HEADS, TOKENS], F32))
        gain = ctx.enter_context(nc.sbuf_tensor(f"qnorm{layer}_gain", [P, 1], F32))
        ps = ctx.enter_context(nc.psum_tensor(f"qnorm{layer}_ps", [P, MEM_HEADS, 512], F32))
        squared, summed, mean, root, link = map(sem, ("squared", "summed", "mean", "root", "link"))
        block = ctx.enter_context(nc.Block())
        q = g.p[:, first:first + MEM_HEADS]

        @block.tensor
        def _(pe):
            pe.wait_ge(squared, 1)
            for h in range(MEM_HEADS):
                mm = nc.tensor.matmul(ps[:, h, 0:TOKENS], g.ones[:], squares[:, h], start=True, stop=True)
            mm.then_inc(summed, 1)

        @block.scalar
        def _(act):
            act.wait_ge(mean, 1)
            nc.scalar.activation(squares[:], squares[:], ACT.Sqrt).then_inc(root, 1)

        @block.vector
        def _(dve):
            linked = Chain(dve, link)
            gq = VEC["g_mem_q"] + layer
            linked(nc.vector.tensor_scalar(gain[:], g.vec[:, gq:gq + 1], SCALE, None, ALU.mult))
            nc.vector.tensor_tensor(squares[:], q, q, ALU.mult).then_inc(squared, 1)
            dve.wait_ge(summed, 1)
            nc.vector.tensor_scalar(squares[:], ps[:, :, 0:TOKENS], 1.0 / HD, EPS, ALU.mult, ALU.add
                                    ).then_inc(mean, 1)
            dve.wait_ge(root, 1)
            linked(nc.vector.reciprocal(squares[:], squares[:]))
            nc.vector.scalar_tensor_tensor(q, q, gain[:], squares[:], ALU.mult, ALU.mult)


def attend_memory_prompt(nc, g, layer, p, first):
    branch = dict(width=lambda i: MEM_LEN, keys=lambda m, k: g.mem_k[:, layer, k], bias=None,
                  values=lambda k, c: g.mem_v[:, layer, c, k * HD:(k + 1) * HD])
    attend_prompt(nc, g, f"memory{layer}", 1, MEM_HEADS, lambda m, k: p[:, first + k, 0:SEQ], [branch], None,
                  lambda m, k, i: g.h[:, HEADS + k, i * P:(i + 1) * P])


def sparse_layer(nc, g, a, base):
    GATE_COL = HEADS * HD + 6 * GROUPS * HD
    gates = BRANCHES * HEADS
    normalize(nc, g, "mix0", VEC["g_mix"], (a.nsa_w_in[0], GATE_COL, gates, g.gates))
    with ExitStack() as ctx:
        sb = lambda n, s: ctx.enter_context(nc.sbuf_tensor(n, s, F32))
        g.cmp_k = sb("cmp_k", [P, PAIRS, CMP_COLS])
        g.cmp_k_prompt = sb("cmp_k_prompt", [P, GROUPS, CMP_PROMPT])
        g.cmp_v = sb("cmp_v", [P, BATCH, HD])
        g.cmp_v_prompt = sb("cmp_v_prompt", [CMP_PROMPT, GROUPS, HD])
        with nc.sbuf_tensor(
                "projected", [P, HEADS + ROW_TILES + MEM_HEADS, TOKENS], F32, side="right") as p:
            g.p = p
            base = project(nc, g, base, 7, KT, g.h, chunks_of(a.nsa_w_in[0]), ("copy", p), None,
                           (1, chunks_of(a.nsa_w_in[0], gates)))
            compress(nc, g, a, 0)
            compress(nc, g, a, 1)
            g.rows_sampled = sb("rows_sampled", [SAMPLED, ROW_TILES * P])
            g.q_sampled = sb("q_sampled", [P, PAIRS, P])
            g.new_k = sb("new_k", [P, 2 * GROUPS, SAMPLED])
            g.gates_sampled = sb("gates_sampled", [P, PAIRS, BRANCHES])
            g.bias_near = sb("bias_near", [P, 132])
            g.bias_far = sb("bias_far", [P, 1])
            g.sparse_masks = sb("sparse_masks", [P, SP_COLS])
            with nc.sbuf_tensor("rows", [P, QT, ROW_TILES * P], F32) as rows, \
                    nc.sbuf_tensor("near", [P, HEADS, T_COLS], F32) as near, \
                    nc.sbuf_tensor("gates_prompt", [P, QT, gates], F32) as gates_prompt:
                g.rows, g.near, g.gates_prompt = rows, near, gates_prompt
                prepare_sparse(nc, g, a)
                for h in range(GROUPS):
                    head = lambda m, k: m * 2 + (h * HPG + k)
                    branches = [
                        dict(width=lambda i: CMP_PROMPT, keys=lambda m, k: g.cmp_k_prompt[:, h],
                             values=lambda k, c: g.cmp_v_prompt[:, h],
                             bias=lambda m, k, i: near[:, bass.ds(head(m, k), 1), P + 31 - P * i:P + 31 - P * i + 225:CMP_LEN].squeeze(1))]
                    for k_tile, v_tile in ((SEL_K, SEL_V), (WIN_K, WIN_V)):
                        branches.append(dict(
                            width=lambda i: P * (i + 1), keys=lambda m, k, t=k_tile: p[:, t + h, 0:SEQ],
                            values=lambda k, c, t=v_tile: rows[:, c, (t - HEADS + h) * HD:(t - HEADS + h + 1) * HD],
                            bias=lambda m, k, i: near[:, bass.ds(head(m, k), 1), P - P * i:2 * P].squeeze(1)))
                    attend_prompt(nc, g, f"sparse{h}", HPG // 2, 2,
                                  lambda m, k: p[:, bass.ds(head(m, k), 1), 0:SEQ].squeeze(1), branches,
                                  lambda m, k, i: gates_prompt[:, i, bass.ds(head(m, k), BRANCHES, step=HEADS)],
                                  lambda m, k, i: g.h[:, bass.ds(head(m, k), 1), i * P:(i + 1) * P].squeeze(1))
            attend_memory_prompt(nc, g, 0, p, MEM_Q)
            attend_memory_sampled(nc, g, a, 0, p[:, MEM_Q:MEM_Q + MEM_HEADS, SEQ:TOKENS],
                                  g.h[:, HEADS:KT, SEQ:TOKENS])
        attend_sampled(nc, g, a, base, chunks_of(a.w_out[0]))
    return base


def linear_layer(nc, g, a, base):
    gate_col = 2 * GLA_KW + GLA_VW
    normalize(nc, g, "mix1", VEC["g_mix"] + KT, (a.gla_w_in[0], gate_col, GATE_RANK, g.gates))
    with ExitStack() as ctx:
        sb = lambda n, s: ctx.enter_context(nc.sbuf_tensor(f"gla_{n}", s, F32))
        g.p = sb("projected", [P, 6 * GLA_KT + MEM_HEADS, TOKENS])
        w_in = a.gla_w_in[0]
        base = project(nc, g, base, 10, KT, g.h, chunks_of(w_in), ("copy", g.p), None,
                       (4, chunks_of(w_in, GATE_RANK)))
        with ExitStack() as inner:
            sb = lambda n, s: inner.enter_context(nc.sbuf_tensor(f"gla_{n}", s, F32))
            g.linear_masks = sb("masks", [P, LIN_COLS])
            g.decay = sb("decay", [P, GLA_KT, TOKENS])
            g.v_rows = sb("v_rows", [P, QT + 1, GLA_VW])
            g.k_rows = sb("k_rows", [P, QT + 1, GLA_KW])
            g.from_start = sb("from_start", [P, GLA_KT, SAMPLED])
            g.q_start = sb("q_start", [P, GLA_KT, SAMPLED])
            prepare_linear(nc, g, a)
            g.att = sb("att", [P, GLA_HEADS, 4, P])
            score_levels(nc, g)
            linear_outputs(nc, g, a)
        normalize_queries(nc, g, 1, GLA_MEM_Q)
        attend_memory_prompt(nc, g, 1, g.p, GLA_MEM_Q)
        attend_memory_sampled(nc, g, a, 1, g.p[:, GLA_MEM_Q:GLA_MEM_Q + MEM_HEADS, SEQ:TOKENS],
                              g.h[:, HEADS:KT, SEQ:TOKENS])
        finish_linear(nc, g, chunks_of(a.w_out[1]), base)
    return base


def feed_forward(nc, g, a, base, layer, next_chunks):
    base = project(nc, g, base, 4, KT, g.h, chunks_of(a.w_out[layer]), ("add", g.x), chunks_of(a.w_up[layer]))
    normalize(nc, g, f"mlp{layer}", VEC["g_mlp"] + layer * KT)
    with nc.sbuf_tensor(f"up{layer}", [P, FT, TOKENS], F32) as up:
        base = project(nc, g, base, FT // 4, KT, g.h, chunks_of(a.w_up[layer]), ("square relu", up),
                       chunks_of(a.w_down[layer]))
        base = project(nc, g, base, 4, FT, up, chunks_of(a.w_down[layer]), ("add", g.x), next_chunks)
    return base


def layers(nc, g, a, base):
    base = sparse_layer(nc, g, a, base)
    base = feed_forward(nc, g, a, base, 0, chunks_of(a.gla_w_in[0]))
    base = linear_layer(nc, g, a, base)
    return feed_forward(nc, g, a, base, 1, None)


def build(nc, a):
    HELD.clear()
    with ExitStack() as ctx:
        sb = lambda n, s: ctx.enter_context(nc.sbuf_tensor(n, s, F32))
        g = Names()
        g.x = sb("x", [P, KT, TOKENS])
        g.h = sb("h", [P, KT, TOKENS])
        g.ring = sb("ring", [P, RING, WTILES, WCOLS])
        g.ident = sb("ident", [P, P])
        g.ones = sb("ones", [P, P])
        g.vec = sb("vec", [P, VECS])
        g.cmp_pe = sb("cmp_pe", [P, 2 * CMP_LEN])
        g.gate_bias = sb("gate_bias", [BRANCHES * HEADS, 1])
        g.mem_k = sb("mem_k", [P, 2, MEM_HEADS, MEM_LEN])
        g.mem_v = sb("mem_v", [P, 2, QT, MEM_WIDTH])
        g.gates = sb("gates", [BRANCHES * HEADS, TOKENS])
        g.pages = ctx.enter_context(nc.sbuf_tensor("pages", [1, BATCH * PAGES], I32))
        g.bias_dram = nc.dram_tensor("bias_by_distance_dram", [HEADS, DISTS], F32, kind="Internal").ap()
        g.weights_loaded = [ctx.enter_context(nc.semaphore(f"weights_loaded{b}")) for b in range(RING)]
        g.weights_used = ctx.enter_context(nc.semaphore("weights_used"))

        base = 0
        with nc.sbuf_tensor("mem", [P, KT, MEM_LEN], F32) as mem:
            g.mem = mem
            load_tokens(nc, g, a)
            base = memory_keys_values(nc, g, a, base, 0, chunks_of(a.w_mem_kv[1]))
            base = memory_keys_values(nc, g, a, base, 1, chunks_of(a.nsa_w_in[0]))
        base = layers(nc, g, a, base)
        store_tokens(nc, g, a)


_INS = ['x_prompt', 'x_sample', 'cache_nsa_kv', 'state_nsa_win', 'state_gla', 'cache_mem_kv', 'page_table',
        'mem_prompt', 'rel_bias', 'g_mix', 'g_mlp', 'g_mem', 'w_mem_kv', 'g_mem_q', 'g_mem_k', 'w_out', 'w_up',
        'w_down', 'nsa_w_in', 'nsa_gate_b', 'nsa_g_q', 'nsa_g_k', 'nsa_cmp_pe', 'nsa_cmp_w1', 'nsa_cmp_b1',
        'nsa_cmp_w2', 'gla_w_in', 'gla_w_a2', 'gla_b_a', 'gla_g_o']
_OUTS = [('y_prompt', (1, SEQ, D_MODEL)), ('y_sample', (BATCH, STEP, D_MODEL)),
         ('nsa_kv_prompt', (1, 1, SEQ, 4, GROUPS, HD)), ('nsa_win_prompt', (1, 1, SEQ, 2, GROUPS, HD)),
         ('gla_prompt', (1, 1, GLA_HEADS, GLA_DK, GLA_DV)), ('mem_kv_prompt', (2, 1, MEM_LEN, 2, MEM_HEADS, HD)),
         ('nsa_kv_sample', (1, BATCH, STEP, 4, GROUPS, HD)), ('nsa_win_sample', (1, BATCH, WINDOW, 2, GROUPS, HD)),
         ('gla_sample', (1, BATCH, GLA_HEADS, GLA_DK, GLA_DV))]


def kernel(**inputs):
    import concourse.bacc as _bacc
    from concourse.bass_utils import run_bass_kernel_spmd as _run

    nc = _bacc.Bacc("TRN2", target_bir_lowering=False, num_devices=1)
    a, arrays = Names(), {}
    named = [(name, inputs[name]) for name in _INS]
    named += list(zip(('bucket_onehot', 'sparse_masks', 'gate_rows', 'linear_masks'), shape_constants()))
    for name, value in named:
        value = np.ascontiguousarray(value)
        arrays[f"in_{name}_dram"] = value
        a.__dict__[name] = nc.dram_tensor(f"in_{name}_dram", value.shape, mybir.dt.from_np(value.dtype),
                                          kind="ExternalInput").ap()
    for name, shape in _OUTS:
        a.__dict__[name] = nc.dram_tensor(f"out_{name}_dram", shape, F32, kind="ExternalOutput").ap()
    build(nc, a)
    r = _run(nc, [arrays], core_ids=[0])
    return tuple(r.results[0][f"out_{name}_dram"] for name, _ in _OUTS)
```

```python
from contextlib import ExitStack

import numpy as np

import concourse.bass as bass
from concourse import mybir

F32 = mybir.dt.float32
F32R = mybir.dt.float32r
I32 = mybir.dt.int32
ALU = mybir.AluOpType
ACT = mybir.ActivationFunctionType
AX_X = mybir.AxisListType.X

P = 128
D_MODEL = 2048
KT = D_MODEL // P
SEQ = 256
QT = SEQ // P
BATCH = 8
STEP = 4
SAMPLED = BATCH * STEP
TOKENS = SEQ + SAMPLED
PAST = 2048
PAGE = 128
PAGES = PAST // PAGE
HD = 128
HEADS = 12
GROUPS = 2
HPG = HEADS // GROUPS
MEM_HEADS = 4
MEM_LEN = 256
MEM_WIDTH = MEM_HEADS * HD
WINDOW = 512
CMP_LEN = 32
CMP_PER_PAGE = PAGE // CMP_LEN
CMP_BLOCKS = PAST // CMP_LEN
CMP_PROMPT = SEQ // CMP_LEN
CMP_HIDDEN = 256
SEL_LEN = 64
SEL_BLOCKS = PAST // SEL_LEN + 1
BRANCHES = 3
BUCKETS = 32
D_FF = 8192
FT = D_FF // P
GLA_HEADS = 4
GLA_DK = 192
GLA_DV = 384
GLA_KW = GLA_HEADS * GLA_DK
GLA_KT = GLA_KW // P
GLA_VW = GLA_HEADS * GLA_DV
GATE_RANK = 16
GATE_TAU = 16.0
EPS = 1e-6
MASKED = -1e30
SCALE = HD ** -0.5

RING = 4
WCOLS = 512
WTILES = 4
PAIRS = BATCH // 2

VEC = {}
_at = 0
for _name, _rows in (("g_mix", 2 * KT), ("g_mlp", 2 * KT), ("g_mem", 2 * KT), ("g_mem_q", 2), ("g_mem_k", 2),
                     ("nsa_g_q", 1), ("nsa_g_k", 3), ("cmp_b1", 4), ("gla_b_a", GLA_KT), ("gla_g_o", 3)):
    VEC[_name] = _at
    _at += _rows
VECS = _at

DIST0 = 255
DISTS = 512


def shape_constants():
    dist = DIST0 - np.arange(DISTS)
    n = np.maximum(dist, 0)
    large = 16 + (np.log(np.maximum(n, 1) / 16.0) / np.log(8.0) * 16).astype(np.int64)
    bucket = np.where(n < 16, n, np.minimum(large, BUCKETS - 1))
    onehot = np.zeros((BUCKETS + 1, DISTS), np.float32)
    onehot[bucket[dist >= 0], np.arange(DISTS)[dist >= 0]] = 1.0
    onehot[BUCKETS, dist < 0] = MASKED

    row = np.arange(P)
    block, hh, pos = row // 32, row % 32 // STEP, row % STEP
    same = ((block[:, None] == block[None]) & (pos[:, None] == pos[None])
            & (hh[:, None] < HPG) & (hh[None] < HPG)).astype(np.float32)
    wrong_group = np.where(block[:, None] % 2 == np.arange(P)[None] // CMP_BLOCKS, 0.0, MASKED)
    too_old = np.where(np.arange(32)[None] <= pos[:, None], MASKED, 0.0)
    token_of = np.arange(SAMPLED) // STEP
    other = np.stack([np.where(token_of[None] == 2 * t + (block // 2)[:, None], 0.0, MASKED)
                      for t in range(PAIRS)], 1).reshape(P, -1)
    own = (np.arange(2 * STEP)[None] == (block // 2 * STEP + pos)[:, None]) & (hh < HPG)[:, None]
    at = pos[:, None] == np.arange(STEP)[None]
    flip = np.eye(P)[::-1]
    sparse = np.concatenate([same, wrong_group, too_old, other, own, at, flip], 1).astype(np.float32)
    head = block % 2 * HPG + hh
    gate_rows = np.concatenate([np.arange(BRANCHES * HEADS)[:, None] == (r * HEADS + head)[None]
                                for r in range(BRANCHES)], 1) & np.tile(hh < HPG, BRANCHES)[None]

    i = np.arange(P)
    level = [(i[:, None] == i[None])]
    s = 1
    while s < P:
        level.append((i[:, None] // (2 * s) == i[None] // (2 * s)) & (i[:, None] // s % 2 == 0)
                     & (i[None] // s % 2 == 1))
        s *= 2
    batch_rows = i[:, None] // STEP == np.arange(BATCH)[None]
    batch_tokens = np.repeat(np.eye(BATCH), STEP, 1).reshape(1, -1) * np.ones((P, 1))
    linear = np.concatenate(level + [batch_rows, batch_tokens], 1).astype(np.float32)
    return onehot, sparse, gate_rows.astype(np.float32), linear


LEVELS = 8
SP_SAME, SP_GROUP, SP_OLD, SP_OTHER = 0, P, 2 * P, 2 * P + 32
SP_OWN = SP_OTHER + PAIRS * SAMPLED
SP_AT = SP_OWN + 2 * STEP
SP_FLIP = SP_AT + STEP
SP_COLS = SP_FLIP + P
LIN_ROWS = LEVELS * P
LIN_TOKENS = LIN_ROWS + BATCH
LIN_COLS = LIN_TOKENS + BATCH * SAMPLED


class Names:
    pass


class Chain:

    def __init__(self, eng, sem, base=0):
        self.eng, self.sem, self.base, self.n = eng, sem, base, 0

    def __call__(self, ins):
        self.n += 1
        ins.then_inc(self.sem, 1)
        self.eng.wait_ge(self.sem, self.base + self.n)


def wait(eng, sem, value):
    if not isinstance(value, int) or value > 0:
        eng.wait_ge(sem, value)


HELD = []


def counters(nc, ctx, tag):
    used = []

    def clear():
        numbers = [s.num for s in used]
        nc.clear_and_free_semaphores(used)
        for held in HELD:
            nc.release_semaphore(held)
        HELD[:] = [nc.alloc_semaphore(f"held_{tag}{n}", num=n) for n in numbers]

    ctx.callback(clear)

    def sem(name):
        used.append(nc.alloc_semaphore(tag + name))
        return used[-1]
    return sem



def chunks_of(w, first_col=0):
    tiled = w.rearrange("(c k p) n -> c p k n", k=WTILES, p=P)
    return lambda n, c: tiled[c][:, :, bass.ds(n * WCOLS + first_col, WCOLS)]


def load_first_chunks(sp, g, src, base):
    for b in range(RING):
        if base:
            sp.wait_ge(g.weights_used, base + b - RING + 1)
        sp.dma_start(g.ring[:, b], src(0, b)).then_inc(g.weights_loaded[b], 16)


def load_other_chunks(sp, g, src, base, groups, chunks, late=(0, None)):
    for c in range(RING, chunks):
        sp.wait_ge(g.weights_used, base + c - RING + 1)
        sp.dma_start(g.ring[:, c % RING], src(0, c)).then_inc(g.weights_loaded[c % RING], 16)
    late, late_source = late

    def group(n, source):
        for c in range(chunks):
            sp.wait_ge(g.weights_used, n * chunks + (base + c - RING + 1))
            sp.dma_start(g.ring[:, c % RING], source(n, c)).then_inc(g.weights_loaded[c % RING], 16)

    if groups - late > 1:
        with sp.Fori(1, groups - late) as n:
            group(n, src)
    if late > 1:
        with sp.Fori(groups - late, groups) as n:
            group(n, late_source)
    elif late:
        group(groups - 1, late_source)


def project(nc, g, base, groups, k_tiles, src, then, moving=None, parts=None, next_chunks=None, late=(0, None)):
    chunks = k_tiles // WTILES
    loads = chunks // RING
    kind, out = then
    with ExitStack() as ctx:
        banks = ctx.enter_context(nc.psum_tensor(f"project{base}_banks", [P, 2, 4, 512], F32))
        positive = ctx.enter_context(nc.sbuf_tensor(f"project{base}_positive", [P, 4, TOKENS], F32)) \
            if kind == "square relu" else None
        if parts is None:
            parts = [ctx.enter_context(nc.sbuf_tensor(f"project{base}_{name}", [P, k_tiles, TOKENS], F32R))
                     for name in ("high", "low")]
        moving_high, moving_low = parts
        weights_high, weights_low = (ctx.enter_context(nc.sbuf_tensor(
            f"project{base}_weights_{name}", [P, 2, WTILES, WCOLS], F32R)) for name in ("high", "low"))
        banks_free, squared, square_rounded, rounded, moving_rounded, split, first_rounded, first_split = map(
            counters(nc, ctx, f"project{base}_"), (
                "banks_free", "squared", "square_rounded", "rounded", "moving_rounded", "split", "first_rounded",
                "first_split"))
        block = ctx.enter_context(nc.Block())

        def over_groups(eng, group):
            group(0, 0)
            group(1, 1)
            with eng.Fori(1, groups // 2) as m:
                group(m * 2, 0)
                group(m * 2 + 1, 1)
            if groups % 2:
                group(groups - 1, 0)

        def tiles_of(c):
            return slice(c * WTILES, (c + 1) * WTILES)

        def is_first(n, c=0):
            return isinstance(n, int) and n == 0 and c == 0

        @block.sync
        def _(sp):
            load_other_chunks(sp, g, src, base, groups, chunks, late)
            if next_chunks is not None:
                load_first_chunks(sp, g, next_chunks, base + groups * chunks)

        @block.tensor
        def _(pe):
            def group(n, half):
                wait(pe, banks_free, n - 1)
                for c in range(chunks):
                    if not is_first(n, c):
                        pe.wait_ge(split, n * chunks + c)
                    for k in range(WTILES):
                        if is_first(n, c):
                            pe.wait_ge(first_split, k + 1)
                        kt = c * WTILES + k
                        for o in range(4):
                            w_high = weights_high[:, c % 2, k, o * P:(o + 1) * P]
                            w_low = weights_low[:, c % 2, k, o * P:(o + 1) * P]
                            bank = banks[:, half, o, 0:TOKENS]
                            nc.tensor.matmul(bank, w_high, moving_high[:, kt], start=(kt == 0), stop=False)
                            nc.tensor.matmul(bank, w_high, moving_low[:, kt], start=False, stop=False)
                            mm = nc.tensor.matmul(bank, w_low, moving_high[:, kt], start=False,
                                                  stop=(kt == k_tiles - 1))
                    mm.then_inc(g.weights_used, 1)
            over_groups(pe, group)

        @block.scalar
        def _(act):
            def leave(n, half):
                if kind == "add":
                    return
                act.wait_ge(g.weights_used, n * chunks + (base + chunks))
                if kind == "copy":
                    nc.scalar.activation(out[:, bass.ds(n * 4, 4)], banks[:, half, :, 0:TOKENS],
                                         ACT.Copy).then_inc(banks_free, 1)
                else:
                    wait(act, squared, n * 2)
                    nc.scalar.activation(positive[:], banks[:, half, :, 0:TOKENS], ACT.Relu).then_inc(banks_free, 1)
                    act.wait_ge(squared, n * 2 + 1)
                    nc.scalar.activation(out[0][:, bass.ds(n * 4, 4)], positive[:], ACT.Copy
                                         ).then_inc(square_rounded, 1)

            def group(n, half):
                for c in range(chunks):
                    if is_first(n, c):
                        act.wait_ge(g.weights_loaded[0], 16 * (base // RING + 1))
                        for k in range(WTILES):
                            if moving is not None:
                                nc.scalar.activation(moving_high[:, k], moving[:, k], ACT.Copy)
                            nc.scalar.activation(weights_high[:, 0, k], g.ring[:, 0, k], ACT.Copy
                                                 ).then_inc(first_rounded, 1)
                        continue
                    if is_first(n) and moving is not None:
                        nc.scalar.activation(moving_high[:, tiles_of(c)], moving[:, tiles_of(c)], ACT.Copy
                                             ).then_inc(moving_rounded, 1)
                    act.wait_ge(g.weights_loaded[c % RING],
                                n * (16 * loads) + 16 * (base // RING + c // RING + 1))
                    wait(act, g.weights_used, n * chunks + (base + c - 1))
                    nc.scalar.activation(weights_high[:, c % 2], g.ring[:, c % RING], ACT.Copy).then_inc(rounded, 1)
                    if c == 1 and not is_first(n):
                        leave(n - 1, 1 - half)

            over_groups(act, group)
            leave(groups - 1, (groups - 1) % 2)

        @block.vector
        def _(dve):
            def leave(n, half):
                if kind == "copy":
                    return
                if kind == "add":
                    dst = out[:, bass.ds(n * 4, 4)]
                    dve.wait_ge(g.weights_used, n * chunks + (base + chunks))
                    nc.vector.tensor_tensor(dst, banks[:, half, :, 0:TOKENS], dst, ALU.add).then_inc(banks_free, 1)
                else:
                    dve.wait_ge(banks_free, n + 1)
                    nc.vector.tensor_tensor(positive[:], positive[:], positive[:], ALU.mult).then_inc(squared, 1)
                    dve.wait_ge(square_rounded, n + 1)
                    nc.vector.tensor_tensor(out[1][:, bass.ds(n * 4, 4)], positive[:],
                                            out[0][:, bass.ds(n * 4, 4)].bitcast(F32), ALU.subtract
                                            ).then_inc(squared, 1)

            def group(n, half):
                for c in range(chunks):
                    if is_first(n, c):
                        for k in range(WTILES):
                            dve.wait_ge(first_rounded, k + 1)
                            if moving is not None:
                                nc.vector.tensor_tensor(moving_low[:, k], moving[:, k], moving_high[:, k].bitcast(F32),
                                                        ALU.subtract)
                            nc.vector.tensor_tensor(weights_low[:, 0, k], g.ring[:, 0, k],
                                                    weights_high[:, 0, k].bitcast(F32), ALU.subtract
                                                    ).then_inc(first_split, 1)
                        continue
                    if is_first(n) and moving is not None:
                        dve.wait_ge(moving_rounded, c)
                        nc.vector.tensor_tensor(moving_low[:, tiles_of(c)], moving[:, tiles_of(c)],
                                                moving_high[:, tiles_of(c)].bitcast(F32), ALU.subtract)
                    dve.wait_ge(rounded, n * chunks + c)
                    nc.vector.tensor_tensor(weights_low[:, c % 2], g.ring[:, c % RING],
                                            weights_high[:, c % 2].bitcast(F32), ALU.subtract).then_inc(split, 1)
                    if c == 1 and not is_first(n):
                        leave(n - 1, 1 - half)

            over_groups(dve, group)
            leave(groups - 1, (groups - 1) % 2)
    return base + groups * chunks


def normalize(nc, g, tag, gain, narrow=None, parts=None):
    with ExitStack() as ctx:
        squares = ctx.enter_context(nc.sbuf_tensor(f"norm{tag}_squares", [P, KT, TOKENS], F32))
        rstd = ctx.enter_context(nc.sbuf_tensor(f"norm{tag}_rstd", [P, TOKENS], F32))
        sums = ctx.enter_context(nc.psum_tensor(f"norm{tag}_sums", [P, TOKENS], F32))
        few = ctx.enter_context(nc.psum_tensor(f"norm{tag}_few", [P, 512], F32))
        columns = narrow[2] if narrow else 1
        w_few = ctx.enter_context(nc.sbuf_tensor(f"norm{tag}_w", [P, KT, columns], F32))
        sem = counters(nc, ctx, f"norm{tag}_")
        squared, summed, mean, root, ready, few_loaded, few_done, few_out, rounded = map(sem, (
            "squared", "summed", "mean", "root", "ready", "few_loaded", "few_done", "few_out", "rounded"))
        normed = g.h if parts is None else squares
        block = ctx.enter_context(nc.Block())

        @block.sync
        def _(sp):
            if narrow:
                w, col, n, _ = narrow
                sp.dma_start(w_few[:], w.rearrange("(k p) n -> p k n", p=P)[:, :, col:col + n]
                             ).then_inc(few_loaded, 16)

        @block.gpsimd
        def _(pool):
            for t in range(KT):
                if t % 4 == 3:
                    nc.gpsimd.tensor_tensor(squares[:, t], g.x[:, t], g.x[:, t], ALU.mult).then_inc(squared, 1)
            if parts:
                for t in range(KT):
                    pool.wait_ge(rounded, t + 1)
                    nc.gpsimd.tensor_tensor(parts[1][:, t], normed[:, t], parts[0][:, t].bitcast(F32), ALU.subtract)

        @block.scalar
        def _(act):
            for t in range(KT):
                if t % 4 in (1, 2):
                    nc.scalar.activation(squares[:, t], g.x[:, t], ACT.Square).then_inc(squared, 1)
            act.wait_ge(mean, 1)
            nc.scalar.activation(rstd[:], rstd[:], ACT.Sqrt).then_inc(root, 1)
            if parts:
                for t in range(KT):
                    act.wait_ge(ready, t + 1)
                    nc.scalar.activation(parts[0][:, t], normed[:, t], ACT.Copy).then_inc(rounded, 1)
            if narrow:
                act.wait_ge(few_done, 1)
                nc.scalar.activation(narrow[3][0:narrow[2]], few[0:narrow[2], 0:TOKENS], ACT.Copy).then_inc(few_out, 1)

        @block.tensor
        def _(pe):
            pe.wait_ge(squared, KT)
            for t in range(KT):
                mm = nc.tensor.matmul(sums[:], g.ones[:], squares[:, t], start=(t == 0), stop=(t == KT - 1))
            mm.then_inc(summed, 1)
            if narrow:
                pe.wait_ge(few_loaded, 16)
                for t in range(KT):
                    pe.wait_ge(ready, t + 1)
                    mm = nc.tensor.matmul(few[0:columns, 0:TOKENS], w_few[:, t], g.h[:, t],
                                          start=(t == 0), stop=(t == KT - 1))
                mm.then_inc(few_done, 1)

        @block.vector
        def _(dve):
            for t in range(0, KT, 4):
                nc.vector.tensor_tensor(squares[:, t], g.x[:, t], g.x[:, t], ALU.mult).then_inc(squared, 1)
            dve.wait_ge(summed, 1)
            nc.vector.tensor_scalar(rstd[:], sums[:], 1.0 / D_MODEL, EPS, ALU.mult, ALU.add).then_inc(mean, 1)
            dve.wait_ge(root, 1)
            nc.vector.reciprocal(rstd[:], rstd[:]).then_inc(root, 1)
            dve.wait_ge(root, 2)
            for t in range(KT):
                nc.vector.scalar_tensor_tensor(normed[:, t], g.x[:, t], g.vec[:, gain + t:gain + t + 1], rstd[:],
                                               ALU.mult, ALU.mult).then_inc(ready, 1)


def load_tokens(nc, g, a):
    with ExitStack() as ctx:
        sb = lambda n, s: ctx.enter_context(nc.sbuf_tensor(n, s, F32))
        sem = counters(nc, ctx, "start_")
        rows = sb("token_rows", [P, QT, D_MODEL])
        sampled = sb("sampled_rows", [SAMPLED, D_MODEL])
        memory = sb("memory_rows", [P, QT, D_MODEL])
        vec_rows = sb("vec_rows", [VECS, P])
        pe_rows = sb("pe_rows", [2 * CMP_LEN, P])
        table = sb("bias_table", [BUCKETS + 1, HEADS])
        onehot = sb("bucket_onehot", [BUCKETS + 1, DISTS])
        bias = sb("bias_by_distance", [HEADS, DISTS])
        scratch = sb("memory_squares", [P, D_MODEL])
        ss = sb("memory_sums", [P, QT])
        banks = ctx.enter_context(nc.psum_tensor("turn_banks", [P, 8, 512], F32))
        ident_cleared, consts, params_loaded, tokens_loaded, memory_loaded, row_ones, turned, copied, mem_copied, \
            mem_squared, mem_mean, mem_root, mem_scaled, bias_stored = map(sem, (
                "ident_cleared", "consts", "params_loaded", "tokens_loaded", "memory_loaded", "row_ones", "turned",
                "copied", "mem_copied", "mem_squared", "mem_mean", "mem_root", "mem_scaled", "bias_stored"))
        block = ctx.enter_context(nc.Block())
        params = [(a.g_mix, "g_mix"), (a.g_mlp, "g_mlp"), (a.g_mem, "g_mem"), (a.g_mem_q, "g_mem_q"),
                  (a.g_mem_k, "g_mem_k"), (a.nsa_g_q, "nsa_g_q"), (a.nsa_g_k, "nsa_g_k"), (a.nsa_cmp_b1, "cmp_b1"),
                  (a.gla_b_a, "gla_b_a"), (a.gla_g_o, "gla_g_o")]

        @block.sync
        def _(sp):
            for ap, name in params:
                names = "abc"[:len(ap.shape)]
                flat = ap.rearrange(f"{' '.join(names)} -> ({' '.join(names)})").rearrange("(r p) -> r p", p=P)
                sp.dma_start(vec_rows[VEC[name]:VEC[name] + flat.shape[0]], flat).then_inc(params_loaded, 16)
            sp.dma_start(pe_rows[:], a.nsa_cmp_pe[0].rearrange("k l d -> (k l) d")).then_inc(params_loaded, 16)
            sp.dma_start(table[0:BUCKETS], a.rel_bias).then_inc(params_loaded, 16)
            sp.dma_start(onehot[:], a.bucket_onehot).then_inc(params_loaded, 16)
            sp.dma_start(g.gate_bias[:], a.nsa_gate_b.rearrange("a n -> n a")).then_inc(params_loaded, 16)
            sp.dma_start(g.pages[:], a.page_table.rearrange("b n -> (b n)").unsqueeze(0)).then_inc(params_loaded, 16)
            load_first_chunks(sp, g, chunks_of(a.w_mem_kv[0]), 0)
            sp.wait_ge(copied, 3)
            sp.dma_start(g.bias_dram, bias[:]).then_inc(bias_stored, 16)
            sp.wait_ge(bias_stored, 16)

        @block.scalar
        def _(act):
            for t in range(QT):
                act.dma_start(memory[:, t], a.mem_prompt[0, t * P:(t + 1) * P]).then_inc(memory_loaded, 16)
            for t in range(QT):
                act.dma_start(rows[:, t], a.x_prompt[0, t * P:(t + 1) * P]).then_inc(tokens_loaded, 16)
            act.dma_start(sampled[:], a.x_sample.rearrange("b l d -> (b l) d")).then_inc(tokens_loaded, 16)
            act.wait_ge(memory_loaded, 16 * QT)
            for t in range(QT):
                nc.scalar.activation(scratch[:], memory[:, t], ACT.Square,
                                     accum_out=ss[:, t:t + 1]).then_inc(mem_squared, 1)
                act.wait_ge(mem_squared, t + 1)
            act.wait_ge(mem_mean, 1)
            nc.scalar.activation(ss[:], ss[:], ACT.Sqrt).then_inc(mem_root, 1)
            for s in range(KT // 4):
                act.wait_ge(turned, 3 + KT // 4 + s + 1)
                nc.scalar.activation(g.mem[:, 4 * s:4 * s + 4], banks[:, 4 * (s % 2):4 * (s % 2) + 4, 0:MEM_LEN],
                                     ACT.Copy).then_inc(mem_copied, 1)

        @block.gpsimd
        def _(pool):
            nc.gpsimd.memset(g.ident[:], 0.0).then_inc(ident_cleared, 1)
            nc.gpsimd.memset(g.ones[:], 1.0).then_inc(consts, 1)
            pool.wait_ge(ident_cleared, 1)
            nc.gpsimd.affine_select(out=g.ident[:], in_=g.ident[:], compare_op=ALU.not_equal, fill=1.0, base=0,
                                    pattern=[[-1, P]], channel_multiplier=1).then_inc(consts, 1)

        @block.tensor
        def _(pe):
            pe.wait_ge(consts, 2)
            pe.wait_ge(params_loaded, 16 * (len(params) + 5))
            nc.tensor.transpose(banks[:, 0, 0:VECS], vec_rows[:], g.ident[0:VECS, 0:VECS]).then_inc(turned, 1)
            nc.tensor.transpose(banks[:, 1, 0:2 * CMP_LEN], pe_rows[:],
                                g.ident[0:2 * CMP_LEN, 0:2 * CMP_LEN]).then_inc(turned, 1)
            pe.wait_ge(row_ones, 1)
            nc.tensor.matmul(banks[0:HEADS, 2, :], table[:], onehot[:], start=True, stop=True).then_inc(turned, 1)
            pe.wait_ge(tokens_loaded, 16 * (QT + 1))
            pe.wait_ge(copied, 3)
            for s in range(KT // 4):
                if s >= 2:
                    pe.wait_ge(copied, 3 + s - 1)
                for o in range(4):
                    t = 4 * s + o
                    bank = banks[:, 4 * (s % 2) + o]
                    for q in range(QT):
                        nc.tensor.transpose(bank[:, q * P:(q + 1) * P], rows[:, q, t * P:(t + 1) * P], g.ident[:])
                    mm = nc.tensor.transpose(bank[:, SEQ:TOKENS], sampled[:, t * P:(t + 1) * P],
                                             g.ident[0:SAMPLED, 0:SAMPLED])
                mm.then_inc(turned, 1)
            pe.wait_ge(mem_scaled, QT)
            for s in range(KT // 4):
                if s < 2:
                    pe.wait_ge(copied, 3 + KT // 4 + s - 1)
                else:
                    pe.wait_ge(mem_copied, s - 1)
                for o in range(4):
                    t = 4 * s + o
                    for q in range(QT):
                        mm = nc.tensor.transpose(banks[:, 4 * (s % 2) + o, q * P:(q + 1) * P],
                                                 memory[:, q, t * P:(t + 1) * P], g.ident[:])
                mm.then_inc(turned, 1)

        @block.vector
        def _(dve):
            nc.vector.memset(table[BUCKETS:BUCKETS + 1], 1.0).then_inc(row_ones, 1)
            for n, (dst, src) in enumerate(((g.vec[:], banks[:, 0, 0:VECS]), (g.cmp_pe[:], banks[:, 1, 0:2 * CMP_LEN]),
                                            (bias[:], banks[0:HEADS, 2, :]))):
                dve.wait_ge(turned, n + 1)
                nc.vector.tensor_copy(dst, src).then_inc(copied, 1)
            dve.wait_ge(mem_squared, QT)
            nc.vector.tensor_scalar(ss[:], ss[:], 1.0 / D_MODEL, EPS, ALU.mult, ALU.add).then_inc(mem_mean, 1)
            dve.wait_ge(mem_root, 1)
            nc.vector.reciprocal(ss[:], ss[:]).then_inc(mem_root, 1)
            dve.wait_ge(mem_root, 2)
            for t in range(QT):
                nc.vector.tensor_scalar(memory[:, t], memory[:, t], ss[:, t:t + 1], None,
                                        ALU.mult).then_inc(mem_scaled, 1)
            for s in range(KT // 4):
                dve.wait_ge(turned, 3 + s + 1)
                nc.vector.tensor_copy(g.x[:, 4 * s:4 * s + 4], banks[:, 4 * (s % 2):4 * (s % 2) + 4, 0:TOKENS]
                                      ).then_inc(copied, 1)


def store_tokens(nc, g, a):
    with ExitStack() as ctx:
        rows = ctx.enter_context(nc.sbuf_tensor("out_rows", [P, QT + 1, D_MODEL], F32))
        banks = ctx.enter_context(nc.psum_tensor("out_banks", [P, 8, 512], F32))
        turned, copied, stored = map(counters(nc, ctx, "out_"), ("turned", "copied", "stored"))
        block = ctx.enter_context(nc.Block())
        steps = [(q, s) for q in range(QT + 1) for s in range(KT // 4)]
        width = lambda q: P if q < QT else SAMPLED

        @block.tensor
        def _(pe):
            for n, (q, s) in enumerate(steps):
                if n >= 8:
                    pe.wait_ge(copied, n - 7)
                for o in range(4):
                    mm = nc.tensor.transpose(banks[0:width(q), n % 8, o * P:(o + 1) * P],
                                             g.x[:, 4 * s + o, q * P:q * P + width(q)], g.ident[:])
                mm.then_inc(turned, 1)

        @block.vector
        def _(dve):
            for n, (q, s) in enumerate(steps):
                dve.wait_ge(turned, n + 1)
                nc.vector.tensor_copy(rows[0:width(q), q, s * 512:(s + 1) * 512], banks[0:width(q), n % 8, :]
                                      ).then_inc(copied, 1)

        @block.sync
        def _(sp):
            for q in range(QT + 1):
                sp.wait_ge(copied, (q + 1) * (KT // 4))
                dst = a.y_prompt[0, q * P:(q + 1) * P] if q < QT else a.y_sample.rearrange("b l d -> (b l) d")
                sp.dma_start(dst, rows[0:width(q), q]).then_inc(stored, 16)
            sp.wait_ge(stored, 16 * (QT + 1))


def memory_keys_values(nc, g, a, base, layer, next_chunks):
    chunks = KT // WTILES
    with ExitStack() as ctx:
        sb = lambda n, s: ctx.enter_context(nc.sbuf_tensor(f"memkv{layer}_{n}", s, F32))
        sem = counters(nc, ctx, f"memkv{layer}_")
        scaled = sb("scaled", [P, KT, MEM_LEN])
        keys = sb("keys", [P, QT, MEM_WIDTH])
        squares = sb("squares", [P, QT, MEM_WIDTH])
        ss = sb("sums", [P, QT, MEM_HEADS])
        banks = ctx.enter_context(nc.psum_tensor(f"memkv{layer}_banks", [P, 8, 512], F32))
        scaled_done, copied, link, mean, root, keys_scaled, turned, stored = map(sem, (
            "scaled_done", "copied", "link", "mean", "root", "keys_scaled", "turned", "stored"))
        block = ctx.enter_context(nc.Block())
        gain = VEC["g_mem"] + layer * KT
        out = a.mem_kv_prompt[layer, 0].rearrange("m s h d -> m s (h d)")

        @block.sync
        def _(sp):
            load_other_chunks(sp, g, chunks_of(a.w_mem_kv[layer]), base, 2, chunks)
            for part, src in enumerate((keys, g.mem_v[layer])):
                sp.wait_ge(copied, 2 * part + 2)
                for t in range(QT):
                    sp.dma_start(out[t * P:(t + 1) * P, part], src[:, t]).then_inc(stored, 16)
            sp.wait_ge(stored, 16 * 2 * QT)
            load_first_chunks(sp, g, next_chunks, base + 2 * chunks)

        @block.tensor
        def _(pe):
            for part in range(2):
                for c in range(chunks):
                    pe.wait_ge(g.weights_loaded[c % RING], 16 * (base // RING + part * chunks // RING + c // RING + 1))
                    for k in range(WTILES):
                        kt = c * WTILES + k
                        if part == 0:
                            pe.wait_ge(scaled_done, kt + 1)
                        for t in range(QT):
                            mm = nc.tensor.matmul(banks[:, 2 * part + t, :], scaled[:, kt, t * P:(t + 1) * P],
                                                  g.ring[:, c % RING, k, :], start=(kt == 0), stop=(kt == KT - 1))
                    mm.then_inc(g.weights_used, 1)
            pe.wait_ge(keys_scaled, 1)
            for h in range(MEM_HEADS):
                for t in range(QT):
                    mm = nc.tensor.transpose(banks[:, 4 + h, t * P:(t + 1) * P], squares[:, t, h * HD:(h + 1) * HD],
                                             g.ident[:])
            mm.then_inc(turned, 1)

        @block.scalar
        def _(act):
            for part in range(2):
                act.wait_ge(g.weights_used, base + (part + 1) * chunks)
                for t in range(QT):
                    dst = (keys if part == 0 else g.mem_v[layer])[:, t]
                    nc.scalar.activation(dst, banks[:, 2 * part + t, :], ACT.Copy).then_inc(copied, 1)
                if part == 0:
                    act.wait_ge(mean, 1)
                    nc.scalar.activation(ss[:], ss[:], ACT.Sqrt).then_inc(root, 1)

        @block.vector
        def _(dve):
            for t in range(KT):
                nc.vector.tensor_scalar(scaled[:, t], g.mem[:, t], g.vec[:, gain + t:gain + t + 1], None,
                                        ALU.mult).then_inc(scaled_done, 1)
            dve.wait_ge(copied, 2)
            nc.vector.tensor_tensor(squares[:], keys[:], keys[:], ALU.mult).then_inc(link, 1)
            dve.wait_ge(link, 1)
            nc.vector.tensor_reduce(ss[:], squares[:].rearrange("p t (h d) -> p t h d", d=HD), AX_X, ALU.add
                                    ).then_inc(link, 1)
            dve.wait_ge(link, 2)
            nc.vector.tensor_scalar(ss[:], ss[:], 1.0 / HD, EPS, ALU.mult, ALU.add).then_inc(mean, 1)
            dve.wait_ge(root, 1)
            nc.vector.reciprocal(ss[:], ss[:]).then_inc(link, 1)
            dve.wait_ge(link, 3)
            for t in range(QT):
                mm = nc.vector.tensor_tensor(squares[:, t].rearrange("p (h d) -> p h d", d=HD),
                                             keys[:, t].rearrange("p (h d) -> p h d", d=HD),
                                             ss[:, t].unsqueeze(2).to_broadcast([P, MEM_HEADS, HD]), ALU.mult)
            mm.then_inc(keys_scaled, 1)
            dve.wait_ge(turned, 1)
            gk = VEC["g_mem_k"] + layer
            nc.vector.tensor_scalar(g.mem_k[layer], banks[:, 4:8, 0:MEM_LEN], g.vec[:, gk:gk + 1], None, ALU.mult)
    return base + 2 * chunks
CHUNK_PAGES = 4
CHUNKS = PAGES // CHUNK_PAGES
PAIR_COLS = 2 * GROUPS * CMP_BLOCKS
OWN_COLS = GROUPS * CMP_PROMPT // PAIRS
CMP_COLS = PAIR_COLS + OWN_COLS


def compress(nc, g, a, kind):
    with ExitStack() as ctx:
        tag = "cmp_kv"[4 + kind]
        sb = lambda n, s: ctx.enter_context(nc.sbuf_tensor(f"cmp_{tag}_{n}", s, F32))
        ps = lambda n, s: ctx.enter_context(nc.psum_tensor(f"cmp_{tag}_{n}", s, F32))
        sem = counters(nc, ctx, f"cmp_{tag}_")
        stage = g.h[:].rearrange("p k n -> p (k n)")[:, 0:4 * CHUNK_PAGES * GROUPS * HD].rearrange(
            "p (b q n) -> p b q n", b=4, q=CHUNK_PAGES)
        blocks = sb("blocks", [P, 2, CMP_LEN, CMP_COLS])
        w1 = g.ring[:].rearrange("p b k n -> p (b k n)").rearrange("p (j m) -> p j m", m=CMP_HIDDEN)
        w2 = sb("w2", [P, 2, HD])
        neg_b1 = sb("neg_b1", [P, 2])
        e = sb("exp", [P, 2, CMP_COLS])
        hidden = sb("hidden", [P, 2, CMP_COLS])
        own_hidden = sb("own_hidden", [P, 2, GROUPS, CMP_PROMPT])
        squares = blocks[:, 0].rearrange("p j n -> p (j n)")[:, 0:PAIRS * CMP_COLS]
        rows_ps = ps("rows_ps", [P, 2, 512])
        hid_ps = ps("hid_ps", [P, 2, 2, 512])
        out_ps = ps("out_ps", [P, 2, 512])
        stage_loaded = g.pages_loaded
        w1_loaded = [sem(f"w1_loaded{q}") for q in range(4)]
        w2_loaded, turned, placed, own_placed, own_hidden_placed, hid_done, exp_done, link, hidden_done, \
            out_done, out_copied, b1_neg, squared, summed, mean, root = map(sem, (
                "w2_loaded", "turned", "placed", "own_placed", "own_hidden_placed", "hid_done", "exp_done",
                "link", "hidden_done", "out_done", "out_copied", "b1_neg", "squared", "summed", "mean", "root"))
        block = ctx.enter_context(nc.Block())
        per_pair = 2 * CHUNKS
        total = PAIRS * per_pair
        pages = a.cache_nsa_kv[0].rearrange("n r k g d -> n r k (g d)")
        b1 = VEC["cmp_b1"] + 2 * kind
        quarter = CMP_LEN // 4
        thirds = [(s, min(512, PAIRS * CMP_COLS - s)) for s in range(0, PAIRS * CMP_COLS, 512)]

        @block.sync
        def _(sp):
            def chunk(n, b, units=0, part=kind):
                numbers = [sp.value_load(g.pages[0:1, bass.ds(n * CHUNK_PAGES + q, 1)], min_val=0,
                                         max_val=pages.shape[0] - 1) for q in range(CHUNK_PAGES)]
                wait(sp, turned, units)
                for q, page in enumerate(numbers):
                    sp.dma_start(stage[:, b, q], pages[bass.ds(page, 1), :, part].squeeze(0)
                                 ).then_inc(stage_loaded[b], 16)

            sp.dma_start(w2[:], a.nsa_cmp_w2[0, kind].rearrange("(k p) n -> p k n", p=P)).then_inc(w2_loaded, 16)
            if kind == 0:
                for b in range(4):
                    chunk(b, b)
            with sp.Fori(1, total // 4) as m:
                for b in range(4):
                    chunk(m * 4 + b, b, m * (4 * GROUPS) + (b - 3) * GROUPS)
            if kind == 0:
                for b in range(4):
                    chunk(b, b, (total + b - 3) * GROUPS, 1)

        @block.gpsimd
        def _(pool):
            nc.gpsimd.tensor_scalar(neg_b1[:], g.vec[:, b1:b1 + 2], -1.0, None, ALU.mult).then_inc(b1_neg, 1)

        @block.scalar
        def _(act):
            act.wait_ge(turned, 1)
            for q in range(4):
                act.dma_start(w1[:, q * quarter:(q + 1) * quarter],
                              a.nsa_cmp_w1[0, kind].rearrange("(j p) m -> p j m", p=P)[:, q * quarter:(q + 1) * quarter]
                              ).then_inc(w1_loaded[q], 16)
            act.wait_ge(b1_neg, 1)
            for t in range(PAIRS):
                act.wait_ge(hid_done, t + 1)
                if t:
                    act.wait_ge(hidden_done, 2 * t)
                for m in range(2):
                    nc.scalar.activation(e[:, m], hid_ps[:, t % 2, m, 0:CMP_COLS], ACT.Exp, bias=neg_b1[:, m:m + 1],
                                         scale=-1.0).then_inc(exp_done, 1)
                act.wait_ge(out_done, t + 1)
                if kind == 0:
                    nc.scalar.activation(g.cmp_k[:, t], out_ps[:, 0, 0:CMP_COLS], ACT.Copy).then_inc(out_copied, 1)
                else:
                    nc.scalar.activation(g.cmp_v[:, 2 * t:2 * t + 2], out_ps[:, 0, 0:2 * HD].rearrange(
                        "p (b d) -> p b d", b=2), ACT.Copy).then_inc(out_copied, 1)
            if kind == 0:
                act.wait_ge(mean, 1)
                nc.scalar.activation(squares, squares, ACT.Sqrt).then_inc(root, 1)
            else:
                act.wait_ge(out_done, PAIRS + 1)
                nc.scalar.activation(g.cmp_v_prompt[0:CMP_PROMPT], out_ps[0:CMP_PROMPT, 1, 0:GROUPS * HD].rearrange(
                    "p (g d) -> p g d", g=GROUPS), ACT.Copy)

        @block.tensor
        def _(pe):
            def turn_chunk(n):
                b = n % 4
                pe.wait_ge(stage_loaded[b], 16 * CHUNK_PAGES * ((kind * total + n) // 4 + 1))
                for h in range(GROUPS):
                    wait(pe, placed, n * GROUPS + h - 1)
                    for q in range(CHUNK_PAGES):
                        mm = nc.tensor.transpose(rows_ps[:, h, q * PAGE:(q + 1) * PAGE],
                                                 stage[:, b, q, h * HD:(h + 1) * HD], g.ident[:])
                    mm.then_inc(turned, 1)

            def hide(t, i):
                if i == 0:
                    pe.wait_ge(placed, per_pair * GROUPS * (t + 1))
                    pe.wait_ge(own_placed, t + 1)
                    wait(pe, hidden_done, 2 * (t - 1))
                step = CMP_LEN // per_pair
                for j in range(i * step, (i + 1) * step):
                    if t == 0 and j % quarter == 0:
                        pe.wait_ge(w1_loaded[j // quarter], 16)
                    for m in range(2):
                        mm = nc.tensor.matmul(hid_ps[:, t % 2, m, 0:CMP_COLS], w1[:, j, m * P:(m + 1) * P],
                                              blocks[:, t % 2, j], start=(j == 0), stop=(j == CMP_LEN - 1))
                if i == per_pair - 1:
                    mm.then_inc(hid_done, 1)

            def second_layer(t):
                pe.wait_ge(hidden_done, 2 * t + 2)
                if t == 0:
                    pe.wait_ge(w2_loaded, 16)
                else:
                    pe.wait_ge(out_copied, t)
                if kind == 0:
                    for m in range(2):
                        mm = nc.tensor.matmul(out_ps[:, 0, 0:CMP_COLS], w2[:, m], hidden[:, m], start=(m == 0),
                                              stop=(m == 1))
                else:
                    for b in range(2):
                        for m in range(2):
                            mm = nc.tensor.matmul(out_ps[:, 0, b * HD:(b + 1) * HD], hidden[:, m, b * P:(b + 1) * P],
                                                  w2[:, m], start=(m == 0), stop=(m == 1))
                mm.then_inc(out_done, 1)

            for n in range(per_pair):
                turn_chunk(n)
            for t in range(PAIRS):
                for i in range(per_pair):
                    hide(t, i)
                    if t + 1 < PAIRS:
                        turn_chunk((t + 1) * per_pair + i)
                    if i == 2 and t:
                        second_layer(t - 1)
            second_layer(PAIRS - 1)
            if kind == 0:
                pe.wait_ge(squared, 1)
                for n, (s, w) in enumerate(thirds):
                    mm = nc.tensor.matmul((hid_ps[:, 0, n] if n < 2 else out_ps[:, 1])[:, 0:w], g.ones[:],
                                          squares[:, s:s + w], start=True, stop=True)
                mm.then_inc(summed, 1)
            else:
                pe.wait_ge(own_hidden_placed, PAIRS)
                for h in range(GROUPS):
                    for m in range(2):
                        mm = nc.tensor.matmul(out_ps[0:CMP_PROMPT, 1, h * HD:(h + 1) * HD], own_hidden[:, m, h],
                                              w2[:, m], start=(m == 0), stop=(m == 1))
                mm.then_inc(out_done, 1)

        @block.vector
        def _(dve):
            pe_cols = g.cmp_pe[:, kind * CMP_LEN:(kind + 1) * CMP_LEN]
            linked = Chain(dve, link)

            def place(n):
                t, c = divmod(n, per_pair)
                b, c = divmod(c, CHUNKS)
                if t >= 2 and n % per_pair == 0:
                    dve.wait_ge(hid_done, t - 1)
                for h in range(GROUPS):
                    dve.wait_ge(turned, n * GROUPS + h + 1)
                    col = b * P + h * CMP_BLOCKS + c * CHUNK_PAGES * CMP_PER_PAGE
                    width = CHUNK_PAGES * CMP_PER_PAGE
                    nc.vector.tensor_tensor(
                        blocks[:, t % 2, :, col:col + width].rearrange("p j n -> p n j"),
                        rows_ps[:, h].rearrange("p (n j) -> p n j", j=CMP_LEN),
                        pe_cols.unsqueeze(1).to_broadcast([P, width, CMP_LEN]), ALU.add).then_inc(placed, 1)

            def place_own(t):
                for h in range(GROUPS):
                    col = PAIR_COLS + 2 * h
                    own = g.p[:, HEADS + kind * GROUPS + h, 2 * t * CMP_LEN:2 * (t + 1) * CMP_LEN]
                    last = nc.vector.tensor_tensor(
                        blocks[:, t % 2, :, col:col + 2].rearrange("p j n -> p n j"),
                        own.rearrange("p (n j) -> p n j", j=CMP_LEN),
                        pe_cols.unsqueeze(1).to_broadcast([P, 2, CMP_LEN]), ALU.add)
                last.then_inc(own_placed, 1)

            def silu(t):
                dve.wait_ge(exp_done, 2 * t + 2)
                linked(nc.vector.tensor_scalar(e[:], e[:], 1.0, None, ALU.add))
                linked(nc.vector.reciprocal(e[:], e[:]))
                if t:
                    dve.wait_ge(out_done, t)
                for m in range(2):
                    nc.vector.scalar_tensor_tensor(hidden[:, m], hid_ps[:, t % 2, m, 0:CMP_COLS],
                                                   g.vec[:, b1 + m:b1 + m + 1], e[:, m], ALU.add,
                                                   ALU.mult).then_inc(hidden_done, 1)
                if kind == 1:
                    dve.wait_ge(hidden_done, 2 * t + 2)
                    nc.vector.tensor_copy(
                        own_hidden[:, :, :, 2 * t:2 * t + 2],
                        hidden[:, :, PAIR_COLS:CMP_COLS].rearrange("p m (h c) -> p m h c", h=GROUPS)
                    ).then_inc(own_hidden_placed, 1)

            for n in range(per_pair):
                place(n)
            place_own(0)
            for t in range(PAIRS):
                for i in range(per_pair):
                    if t + 1 < PAIRS:
                        place((t + 1) * per_pair + i)
                    if i == 0 and t:
                        silu(t - 1)
                if t + 1 < PAIRS:
                    place_own(t + 1)
            silu(PAIRS - 1)
            if kind == 0:
                flat = g.cmp_k[:].rearrange("p t n -> p (t n)")
                dve.wait_ge(out_copied, PAIRS)
                nc.vector.tensor_tensor(squares, flat, flat, ALU.mult).then_inc(squared, 1)
                dve.wait_ge(summed, 1)
                for n, (s, w) in enumerate(thirds):
                    last = nc.vector.tensor_scalar(squares[:, s:s + w],
                                                   (hid_ps[:, 0, n] if n < 2 else out_ps[:, 1])[:, 0:w],
                                                   1.0 / HD, EPS, ALU.mult, ALU.add)
                last.then_inc(mean, 1)
                dve.wait_ge(root, 1)
                linked(nc.vector.reciprocal(squares, squares))
                gk = VEC["nsa_g_k"]
                linked(nc.vector.scalar_tensor_tensor(flat, flat, g.vec[:, gk:gk + 1], squares, ALU.mult, ALU.mult))
                nc.vector.tensor_copy(g.cmp_k_prompt[:].rearrange("p h (t c) -> p h t c", c=2),
                                      g.cmp_k[:, :, PAIR_COLS:CMP_COLS].rearrange("p t (h c) -> p h t c", c=2))


SEL_K, SEL_V, WIN_K, WIN_V = HEADS + 4, HEADS + 6, HEADS + 8, HEADS + 10
MEM_Q = HEADS + 12
ROW_TILES = 12
T_COLS = 384


def prepare_sparse(nc, g, a):
    with ExitStack() as ctx:
        sb = lambda n, s: ctx.enter_context(nc.sbuf_tensor(f"prep_{n}", s, F32))
        sem = counters(nc, ctx, f"prep_")
        gq, gk, gm = VEC["nsa_g_q"], VEC["nsa_g_k"], VEC["g_mem_q"]
        normed = [(t, gq, SCALE) for t in range(HEADS)] \
            + [(t, gk + 1, 1.0) for t in (SEL_K, SEL_K + 1)] + [(t, gk + 2, 1.0) for t in (WIN_K, WIN_K + 1)] \
            + [(t, gm, SCALE) for t in range(MEM_Q, MEM_Q + MEM_HEADS)]
        BATCHED = 4
        squares = sb("squares", [P, 2, BATCHED, TOKENS])
        inverse_rms = sb("inverse_rms", [P, 2, TOKENS])
        spread = sb("spread", [P, BATCHED, P])
        scaled_gain = sb("scaled_gain", [P, 2])
        neg_bias = sb("neg_bias", [BRANCHES * HEADS, 1])
        gate_rows = sb("gate_rows", [BRANCHES * HEADS, BRANCHES * P])
        own_gates = sb("own_gates", [P, BRANCHES * SAMPLED])
        bias = sb("bias", [HEADS, DISTS])
        rows_ps = ctx.enter_context(nc.psum_tensor("prep_rows_ps", [P, 4, 512], F32))
        sums_ps = ctx.enter_context(nc.psum_tensor("prep_sums_ps", [P, BATCHED, 512], F32))
        turned, rows_copied, squared, summed, mean, root, inverse, spread_done, scaled, link, neg_done, gate_exp, gates_done, \
            loaded, stored, blank = map(sem, (
                "turned", "rows_copied", "squared", "summed", "mean", "root", "inverse", "spread_done", "scaled", "link",
                "neg_done", "gate_exp", "gates_done", "loaded", "stored", "blank"))
        flipped, flip_copied = sem("flipped"), sem("flip_copied")
        FLIP_BANKS = 3
        FLIPS = HEADS * T_COLS // (512 * FLIP_BANKS)
        block = ctx.enter_context(nc.Block())
        sets = [(s, tok) for tok in range(QT + 1) for s in range(ROW_TILES // 4)]
        width = lambda tok: P if tok < QT else SAMPLED
        rounds = len(normed) // BATCHED
        u = g.bias_dram.tensor

        @block.sync
        def _(sp):
            sp.dma_start(g.near[:], bass.AP(u, 0, [[1, P], [DISTS, HEADS], [1, T_COLS]])).then_inc(loaded, 16)
            sp.dma_start(bias[:], g.bias_dram).then_inc(loaded, 16)
            sp.dma_start(g.sparse_masks[:], a.sparse_masks).then_inc(loaded, 16)
            sp.dma_start(gate_rows[:], a.gate_rows).then_inc(loaded, 16)
            kv, win = 4 * GROUPS * HD, 2 * GROUPS * HD
            for tok in range(QT + 1):
                sp.wait_ge(rows_copied, 3 * (tok + 1))
                src = g.rows[:, tok] if tok < QT else g.rows_sampled[:]
                if tok < QT:
                    dst = a.nsa_kv_prompt[0, 0, tok * P:(tok + 1) * P].rearrange("r k g d -> r (k g d)")
                    dst_win = a.nsa_win_prompt[0, 0, tok * P:(tok + 1) * P].rearrange("r k g d -> r (k g d)")
                    sp.dma_start(dst_win, src[:, kv:kv + win]).then_inc(stored, 16)
                else:
                    dst = a.nsa_kv_sample[0].rearrange("b l k g d -> (b l) (k g d)")
                    for b in range(BATCH):
                        sp.dma_start(a.nsa_win_sample[0, b, WINDOW - STEP:WINDOW].rearrange("r k g d -> r (k g d)"),
                                     src[b * STEP:(b + 1) * STEP, kv:kv + win]).then_inc(stored, 16)
                sp.dma_start(dst, src[:, 0:kv]).then_inc(stored, 16)
            for b in range(BATCH):
                sp.dma_start(a.nsa_win_sample[0, b, 0:WINDOW - STEP], a.state_nsa_win[0, b, STEP:WINDOW]
                             ).then_inc(stored, 16)
            sp.wait_ge(stored, 16 * (QT * 2 + 1 + 2 * BATCH))
            sp.wait_ge(loaded, 16 * 4)

        @block.gpsimd
        def _(pool):
            nc.gpsimd.tensor_copy(spread[:], g.ident[:, 0:P:P // BATCHED].unsqueeze(2).to_broadcast([P, BATCHED, P]))
            nc.gpsimd.memset(g.q_sampled[:], 0.0).then_inc(blank, 1)

        @block.tensor
        def _(pe):
            for n, (s, tok) in enumerate(sets):
                if n >= 4:
                    pe.wait_ge(rows_copied, n - 3)
                for o in range(4):
                    mm = nc.tensor.transpose(rows_ps[0:width(tok), n % 4, o * P:(o + 1) * P],
                                             g.p[:, HEADS + 4 * s + o, tok * P:tok * P + width(tok)], g.ident[:])
                mm.then_inc(turned, 1)
            pe.wait_ge(gates_done, 1)
            pe.wait_ge(rows_copied, len(sets))
            for tok in range(QT):
                mm = nc.tensor.transpose(rows_ps[:, tok, 0:BRANCHES * HEADS], g.gates[:, tok * P:(tok + 1) * P],
                                         g.ident[0:BRANCHES * HEADS, 0:BRANCHES * HEADS])
            pe.wait_ge(loaded, 16 * 4)
            for r in range(BRANCHES):
                mm = nc.tensor.matmul(rows_ps[:, 2, r * SAMPLED:(r + 1) * SAMPLED], gate_rows[:, r * P:(r + 1) * P],
                                      g.gates[:, SEQ:TOKENS], start=True, stop=True)
            mm.then_inc(turned, 1)
            nc.tensor.matmul(rows_ps[:, 3, :], gate_rows[0:HEADS, 0:P], bias[:], start=True, stop=True
                             ).then_inc(turned, 1)
            flat = g.near[:].rearrange("p h c -> p (h c)")
            for n in range(FLIPS):
                wait(pe, flip_copied, n)
                for o in range(FLIP_BANKS):
                    at = (n * FLIP_BANKS + o) * 512
                    mm = nc.tensor.matmul(sums_ps[:, o], g.sparse_masks[:, SP_FLIP:SP_FLIP + P], flat[:, at:at + 512],
                                          start=True, stop=True)
                mm.then_inc(flipped, 1)
            pe.wait_ge(flip_copied, FLIPS)
            pe.wait_ge(blank, 1)

            def sum_squares(r):
                pe.wait_ge(squared, r + 1)
                wait(pe, mean, r - 1)
                for o in range(BATCHED):
                    mm = nc.tensor.matmul(rows_ps[32 * o:32 * o + 32, r % 2, 0:TOKENS], g.ones[:, 0:32],
                                          squares[:, r % 2, o], start=True, stop=True, skip_group_check=True)
                mm.then_inc(summed, 1)

            sum_squares(0)
            for r in range(rounds):
                if r + 1 < rounds:
                    sum_squares(r + 1)
                pe.wait_ge(inverse, r + 1)
                wait(pe, scaled, r)
                for o in range(BATCHED):
                    mm = nc.tensor.matmul(sums_ps[:, o, 0:TOKENS], spread[:, o], inverse_rms[:, r % 2], start=True,
                                          stop=True)
                mm.then_inc(spread_done, 1)

        @block.scalar
        def _(act):
            act.wait_ge(neg_done, 1)
            nc.scalar.activation(g.gates[:], g.gates[:], ACT.Exp, bias=neg_bias[:], scale=-1.0
                                 ).then_inc(gate_exp, 1)
            for n, (s, tok) in enumerate(sets):
                act.wait_ge(turned, n + 1)
                dst = g.rows[:, tok, s * 512:(s + 1) * 512] if tok < QT else g.rows_sampled[:, s * 512:(s + 1) * 512]
                nc.scalar.activation(dst, rows_ps[0:width(tok), n % 4, :], ACT.Copy).then_inc(rows_copied, 1)
            for n in range(FLIPS):
                act.wait_ge(flipped, n + 1)
                nc.scalar.activation(
                    g.near[:].rearrange("p h c -> p (h c)").rearrange("p (n b c) -> p n b c", b=FLIP_BANKS, c=512)[:, n],
                    sums_ps[:, 0:FLIP_BANKS], ACT.Copy).then_inc(flip_copied, 1)
            for r in range(rounds):
                act.wait_ge(mean, r + 1)
                nc.scalar.activation(inverse_rms[:, r % 2], inverse_rms[:, r % 2], ACT.Sqrt).then_inc(root, 1)

        @block.vector
        def _(dve):
            linked = Chain(dve, link)
            nc.vector.tensor_scalar(neg_bias[:], g.gate_bias[:], -1.0, None, ALU.mult).then_inc(neg_done, 1)
            linked(nc.vector.tensor_scalar(scaled_gain[:, 0:1], g.vec[:, gq:gq + 1], SCALE, None, ALU.mult))
            linked(nc.vector.tensor_scalar(scaled_gain[:, 1:2], g.vec[:, gm:gm + 1], SCALE, None, ALU.mult))
            dve.wait_ge(gate_exp, 1)
            linked(nc.vector.tensor_scalar(g.gates[:], g.gates[:], 1.0, None, ALU.add))
            nc.vector.reciprocal(g.gates[:], g.gates[:]).then_inc(gates_done, 1)
            dve.wait_ge(turned, len(sets) + 1)
            nc.vector.tensor_copy(g.gates_prompt[:], rows_ps[:, 0:QT, 0:BRANCHES * HEADS])
            own = g.sparse_masks[:, SP_OWN:SP_OWN + 2 * STEP]
            linked(nc.vector.tensor_tensor(
                own_gates[:].rearrange("p (n c) -> p n c", c=2 * STEP),
                rows_ps[:, 2, 0:BRANCHES * SAMPLED].rearrange("p (n c) -> p n c", c=2 * STEP),
                own.unsqueeze(1).to_broadcast([P, BRANCHES * PAIRS, 2 * STEP]), ALU.mult))
            nc.vector.tensor_reduce(g.gates_sampled[:], own_gates[:].rearrange(
                "p (r t c) -> p t r c", t=PAIRS, c=2 * STEP), AX_X, ALU.add)

            dve.wait_ge(turned, len(sets) + 2)
            nc.vector.tensor_copy(g.bias_far[:], rows_ps[:, 3, 0:1])
            for l in range(STEP):
                near = rows_ps[:, 3, P - 1 - l:P - 1 - l + 132]
                at = g.sparse_masks[:, SP_AT + l:SP_AT + l + 1]
                if l == 0:
                    linked(nc.vector.tensor_scalar(g.bias_near[:], near, at, None, ALU.mult))
                else:
                    linked(nc.vector.scalar_tensor_tensor(g.bias_near[:], near, at, g.bias_near[:], ALU.mult, ALU.add))

            def square(r):
                for o in range(BATCHED):
                    t = normed[r * BATCHED + o][0]
                    last = nc.vector.tensor_tensor(squares[:, r % 2, o], g.p[:, t], g.p[:, t], ALU.mult)
                last.then_inc(squared, 1)

            def mean_square(r):
                dve.wait_ge(summed, r + 1)
                wait(dve, spread_done, r - 1)
                nc.vector.tensor_scalar(inverse_rms[:, r % 2], rows_ps[:, r % 2, 0:TOKENS], 1.0 / HD, EPS, ALU.mult,
                                        ALU.add).then_inc(mean, 1)

            square(0)
            square(1)
            mean_square(0)
            for r in range(rounds):
                dve.wait_ge(root, r + 1)
                nc.vector.reciprocal(inverse_rms[:, r % 2], inverse_rms[:, r % 2]).then_inc(inverse, 1)
                if r + 1 < rounds:
                    mean_square(r + 1)
                if r + 2 < rounds:
                    square(r + 2)
                dve.wait_ge(spread_done, r + 1)
                for o in range(BATCHED):
                    t, gain, scale = normed[r * BATCHED + o]
                    col = g.vec[:, gain:gain + 1] if scale == 1.0 else scaled_gain[:, int(gain == gm):int(gain == gm) + 1]
                    if o == 0:
                        dve.wait_ge(turned, len(sets))
                    last = nc.vector.scalar_tensor_tensor(g.p[:, t], g.p[:, t], col, sums_ps[:, o, 0:TOKENS], ALU.mult,
                                                          ALU.mult)
                last.then_inc(scaled, 1)
            dve.wait_ge(scaled, rounds)
            dve.wait_ge(blank, 1)
            for j in range(4):
                h0, b = (j % 2) * HPG, j // 2
                src = g.p[:, h0:h0 + HPG, SEQ:TOKENS].rearrange("p h (t b l) -> p b t h l", b=2, l=STEP)[:, b]
                for t in range(PAIRS):
                    nc.vector.tensor_copy(g.q_sampled[:, t, 32 * j:32 * j + HPG * STEP].rearrange(
                        "p (h l) -> p h l", l=STEP), src[:, t])
            nc.vector.tensor_copy(g.new_k[:, 0:2], g.p[:, SEL_K:SEL_K + 2, SEQ:TOKENS])
            nc.vector.tensor_copy(g.new_k[:, 2:4], g.p[:, WIN_K:WIN_K + 2, SEQ:TOKENS])


def attend_prompt(nc, g, tag, bodies, heads, query, branches, gate, out):
    units = [(k, i) for k in range(heads) for i in range(QT)]
    NB = len(branches)
    biased = gate is not None
    widest = [b["width"](QT - 1) for b in branches]
    starts = [sum(widest[:n]) for n in range(NB)]
    cols = sum(widest)
    with ExitStack() as ctx:
        sb = lambda n, s: ctx.enter_context(nc.sbuf_tensor(f"{tag}_{n}", s, F32))
        sem = counters(nc, ctx, f"{tag}_")
        q = sb("q", [P, 2, SEQ])
        s = sb("scores", [P, 2, cols])
        probs = sb("probs", [P, 2, cols])
        maxima = sb("maxima", [P, 2, NB])
        sums = sb("sums", [P, 2, NB])
        coef = sb("coef", [P, 2, NB])
        turned = sb("turned", [P, 5, P])
        s_ps = ctx.enter_context(nc.psum_tensor(f"{tag}_s_ps", [P, 2, 2, 512], F32))
        t_ps = ctx.enter_context(nc.psum_tensor(f"{tag}_t_ps", [P, 2, 512], F32))
        o_ps = ctx.enter_context(nc.psum_tensor(f"{tag}_o_ps", [P, 2, 512], F32))
        q_ready, scored, biased_done, negated, exped, scaled, turns_done, turns_copied, out_done, \
            out_copied, link = map(sem, (
                "q_ready", "scored", "biased_done", "negated", "exped", "scaled",
                "turns_done", "turns_copied", "out_done", "out_copied", "link"))
        block = ctx.enter_context(nc.Block())

        def place(n):
            return (0, starts[n] - (starts[1] if NB == 3 else 0)) if (NB == 1 or n > 0) else (1, 0)

        def pieces(i):
            return [(n, c, min(P, b["width"](i) - c * P)) for n, b in enumerate(branches)
                    for c in range(-(-b["width"](i) // P))]

        U = len(units)

        def score_psum(n, unit):
            bank, col = place(n)
            return s_ps[:, unit % 2, bank, col:col + branches[n]["width"](units[unit][1])]

        def loop(eng, body):
            body(0)
            if bodies > 1:
                with eng.Fori(1, bodies) as m:
                    body(m)

        @block.gpsimd
        def _(pool):
            def body(m):
                for k in range(heads):
                    wait(pool, scored, m * U + QT * (k - 1))
                    nc.gpsimd.tensor_copy(q[:, k % 2], query(m, k)).then_inc(q_ready, 1)
            loop(pool, body)

        @block.tensor
        def _(pe):
            def scores(m, u):
                k, i = units[u]
                if i == 0:
                    pe.wait_ge(q_ready, m * heads + (k + 1))
                wait(pe, biased_done if biased else exped, m * U + (u - 1))
                for n, b in enumerate(branches):
                    mm = nc.tensor.matmul(score_psum(n, u), q[:, k % 2, i * P:(i + 1) * P],
                                          b["keys"](m, k)[:, 0:b["width"](i)], start=True, stop=True,
                                          skip_group_check=True)
                mm.then_inc(scored, 1)

            def turn(m, u):
                k, i = units[u]
                pe.wait_ge(scaled, m * U + (u + 1))
                wait(pe, turns_copied, m * U + u)
                for e, (n, c, w) in enumerate(pieces(i)):
                    mm = nc.tensor.transpose(t_ps[0:w, e // 4, (e % 4) * P:(e % 4 + 1) * P],
                                             probs[:, u % 2, starts[n] + c * P:starts[n] + c * P + w], g.ident[:])
                mm.then_inc(turns_done, 1)

            def multiply(m, u):
                k, i = units[u]
                pe.wait_ge(turns_copied, m * U + (u + 1))
                wait(pe, out_copied, m * U + (u - 1))
                for e, (n, c, w) in enumerate(pieces(i)):
                    mm = nc.tensor.matmul(o_ps[:, u % 2, 0:P], branches[n]["values"](k, c)[0:w], turned[0:w, e],
                                          start=(e == 0), stop=(e == len(pieces(i)) - 1))
                mm.then_inc(out_done, 1)

            def body(m):
                scores(m, 0)
                scores(m, 1)
                for u in range(U):
                    turn(m, u)
                    if u + 2 < U:
                        scores(m, u + 2)
                    multiply(m, u)
            loop(pe, body)

        @block.vector
        def _(dve):
            def front(m, u, linked):
                k, i = units[u]
                dve.wait_ge(scored, m * U + (u + 1))
                for n, b in enumerate(branches):
                    w = b["width"](i)
                    if biased:
                        last = nc.vector.tensor_tensor(s[:, u % 2, starts[n]:starts[n] + w], score_psum(n, u), b["bias"](m, k, i), ALU.add)
                if biased:
                    last.then_inc(biased_done, 1)
                    dve.wait_ge(biased_done, m * U + (u + 1))
                for n, b in enumerate(branches):
                    w = b["width"](i)
                    src = s[:, u % 2, starts[n]:starts[n] + w] if biased else score_psum(n, u)
                    last = nc.vector.tensor_reduce(maxima[:, u % 2, n:n + 1], src, AX_X, ALU.max)
                linked(last)
                nc.vector.tensor_scalar(maxima[:, u % 2], maxima[:, u % 2], 0.1 * MASKED, -1.0, ALU.max, ALU.mult
                                        ).then_inc(negated, 1)

            def back(m, u, linked):
                k, i = units[u]
                dve.wait_ge(exped, m * U + (u + 1))
                linked(nc.vector.tensor_scalar(sums[:, u % 2], sums[:, u % 2], 1e-30, None, ALU.max))
                linked(nc.vector.reciprocal(coef[:, u % 2], sums[:, u % 2]))
                if biased:
                    linked(nc.vector.tensor_tensor(coef[:, u % 2], coef[:, u % 2], gate(m, k, i), ALU.mult))
                for n, b in enumerate(branches):
                    at = slice(starts[n], starts[n] + b["width"](i))
                    last = nc.vector.tensor_scalar(probs[:, u % 2, at], probs[:, u % 2, at],
                                                   coef[:, u % 2, n:n + 1], None, ALU.mult)
                last.then_inc(scaled, 1)

            def take(m, u):
                dve.wait_ge(out_done, m * U + (u + 1))
                k, i = units[u]
                nc.vector.tensor_copy(out(m, k, i), o_ps[:, u % 2, 0:P]).then_inc(out_copied, 1)

            def body(m):
                links = U * (4 if biased else 3)
                linked = Chain(dve, link, m * links)
                front(m, 0, linked)
                for u in range(U):
                    if u + 1 < U:
                        front(m, u + 1, linked)
                    back(m, u, linked)
                    if u >= 1:
                        take(m, u - 1)
                take(m, U - 1)
                assert linked.n == links
            loop(dve, body)

        @block.scalar
        def _(act):
            def exps(m, u):
                k, i = units[u]
                act.wait_ge(negated, m * U + (u + 1))
                for n, b in enumerate(branches):
                    at = slice(starts[n], starts[n] + b["width"](i))
                    src = s[:, u % 2, at] if biased else score_psum(n, u)
                    last = nc.scalar.activation(probs[:, u % 2, at], src, ACT.Exp, bias=maxima[:, u % 2, n:n + 1],
                                                accum_out=sums[:, u % 2, n:n + 1])
                last.then_inc(exped, 1)

            def copies(m, u):
                k, i = units[u]
                act.wait_ge(turns_done, m * U + (u + 1))
                wait(act, out_done, m * U + u)
                e = pieces(i)
                for b in range(-(-len(e) // 4)):
                    part = e[4 * b:4 * b + 4]
                    few = [(x, y) for x, y in enumerate(part) if y[2] < P]
                    first = 1 if few else 0
                    if few:
                        w = few[0][1][2]
                        nc.scalar.activation(turned[0:w, 4 * b], t_ps[0:w, b, 0:P], ACT.Copy)
                    last = nc.scalar.activation(turned[:, 4 * b + first:4 * b + len(part)],
                                                t_ps[:, b, first * P:len(part) * P].rearrange("p (c q) -> p c q", q=P),
                                                ACT.Copy)
                last.then_inc(turns_copied, 1)

            def body(m):
                exps(m, 0)
                for u in range(U):
                    if u + 1 < U:
                        exps(m, u + 1)
                    copies(m, u)
            loop(act, body)


NEW = SAMPLED
S_CMP, S_SEL = 0, 2 * CMP_BLOCKS
S_SEL_NEW = S_SEL + PAST
S_WIN = S_SEL_NEW + NEW
S_WIN_NEW = S_WIN + WINDOW
S_COLS = S_WIN_NEW + NEW
HALVES = 2 * (CHUNKS + 1)
TOP_ROUNDS = 2
FORCED = 1e4
P_CHUNKS = [(S_CMP, P)] + [(S_SEL + c * P, P) for c in range(PAGES)] + [(S_SEL_NEW, NEW)] \
    + [(S_WIN + c * P, P) for c in range(WINDOW // P)] + [(S_WIN_NEW, NEW)]


def attend_sampled(nc, g, a, base, next_chunks):
    with ExitStack() as ctx:
        sb = lambda n, s: ctx.enter_context(nc.sbuf_tensor(f"sp_{n}", s, F32))
        ps = lambda n, s: ctx.enter_context(nc.psum_tensor(f"sp_{n}", s, F32))
        sem = counters(nc, ctx, "sp_")
        q = sb("q", [P, P])
        cmp_k = sb("cmp_k", [P, 2, GROUPS * CMP_BLOCKS])
        cmp_v = sb("cmp_v", [P, 2, HD])
        in_ring = g.ring[:].rearrange("p b k n -> p (b k n)").rearrange("p (b k q n) -> p b k q n", b=4, k=2,
                                                                         q=CHUNK_PAGES)
        rest = sb("keys_values", [P, HALVES - 4, 2, CHUNK_PAGES, GROUPS * HD])
        keys_values = [in_ring[:, n] if n < 4 else rest[:, n - 4] for n in range(HALVES)]
        stage, values = ([kv[:, part] for kv in keys_values] for part in range(2))
        squares = [g.mem_k[0][:].rearrange("p h k -> p (h k)"), g.mem_v[0][:].rearrange("p t n -> p (t n)")]
        ss = sb("ss", [P, HALVES, CHUNK_PAGES * GROUPS])
        turned_k = sb("turned_k", [P, 2, GROUPS, 512])
        s = sb("s", [P, S_COLS])
        probs = sb("probs", [P, len(P_CHUNKS), P])
        cmp_bias = sb("cmp_bias", [P, 2 * CMP_BLOCKS])
        win_bias = sb("win_bias", [P, WINDOW])
        new_bias = sb("new_bias", [P, NEW])
        near_bias = sb("near_bias", [P, P])
        block_score = sb("block_score", [P, SEL_BLOCKS])
        pair_score = sb("pair_score", [P, 2 * GROUPS * CMP_BLOCKS // 4])
        unselected = sb("unselected", [P, SEL_BLOCKS])
        sel_bias = sb("sel_bias", [P, SEL_BLOCKS])
        top = sb("top", [P, TOP_ROUNDS, 8])
        spare = sb("spare", [P, 1])
        neg_max = sb("neg_max", [P, BRANCHES])
        sums = sb("sums", [P, BRANCHES])
        coef = sb("coef", [P, BRANCHES])
        o = sb("o", [P, HD])
        k_ps = ps("k_ps", [P, 2, GROUPS, 512])
        s_ps = ps("s_ps", [P, 2, 512])
        small_ps = ps("small_ps", [P, 512])
        o_ps = ps("o_ps", [P, 512])
        stage_loaded = [sem(f"stage_loaded{n}") for n in range(HALVES)]
        q_ready, small_scored, cmp_negated, cmp_exped, cmp_ready, group_summed, k_squared, k_mean, k_root, k_inverse, \
            k_scaled, k_turned, k_copied, half_scored, s_taken, negated, exped, scaled, p_turned, p_copied, multiplied, \
            o_taken, o_turned, link = map(sem, (
                "q_ready", "small_scored", "cmp_negated", "cmp_exped", "cmp_ready", "group_summed", "k_squared",
                "k_mean", "k_root", "k_inverse", "k_scaled", "k_turned", "k_copied", "half_scored", "s_taken",
                "negated", "exped", "scaled", "p_turned", "p_copied", "multiplied", "o_taken", "o_turned",
                "link"))
        block = ctx.enter_context(nc.Block())
        pages = a.cache_nsa_kv[0].rearrange("n r k g d -> n r k (g d)")
        window = a.state_nsa_win[0].rearrange("b (c p) k g d -> b p c k (g d)", p=P)
        CH = CHUNKS + 1
        sets = [list(range(n, min(n + 8, len(P_CHUNKS)))) for n in range(0, len(P_CHUNKS), 8)]

        def values_of(col):
            c = (col - S_SEL) // P if col < S_WIN else PAGES + (col - S_WIN) // P
            return 2 * (c // CHUNK_PAGES), c % CHUNK_PAGES

        def sets_with(n):
            return 1 + max(i for i, chunks in enumerate(sets) for x in chunks
                           if P_CHUNKS[x][1] == P and x and values_of(P_CHUNKS[x][0])[0] == n // 2 * 2)

        def turns(eng, body):
            body(0)
            with eng.Fori(1, PAIRS) as t:
                body(t)

        @block.sync
        def _(sp):
            def body(t):
                for n in range(HALVES):
                    c, b = divmod(n, 2)
                    first = t * (2 * PAGES) + (b * PAGES + c * CHUNK_PAGES)
                    numbers = [sp.value_load(g.pages[0:1, bass.ds(first + quarter, 1)], min_val=0,
                                             max_val=pages.shape[0] - 1)
                               for quarter in range(CHUNK_PAGES if c < CHUNKS else 0)]
                    wait(sp, multiplied, (t - 1) * len(sets) + sets_with(n))
                    for quarter, page in enumerate(numbers):
                        sp.dma_start(keys_values[n][:, :, quarter], pages[bass.ds(page, 1), :, 2:4].squeeze(0)
                                     ).then_inc(stage_loaded[n], 16)
                    for part in range(0 if numbers else 2):
                        sp.dma_start(keys_values[n][:, part], window[bass.ds(t * 2 + b, 1), :, :, part].squeeze(0)
                                     ).then_inc(stage_loaded[n], 16)

            body(0)
            with sp.Fori(1, PAIRS) as t:
                body(t)
            sp.wait_ge(multiplied, PAIRS * len(sets))
            load_first_chunks(sp, g, next_chunks, base)

        @block.gpsimd
        def _(pool):
            def body(t):
                for n in range(HALVES):
                    pool.wait_ge(k_inverse, t * HALVES + (n + 1))
                    k = stage[n].rearrange("p q (g d) -> p (q g) d", g=GROUPS)
                    nc.gpsimd.tensor_tensor(k, k, ss[:, n].unsqueeze(2).to_broadcast(
                        [P, CHUNK_PAGES * GROUPS, HD]), ALU.mult).then_inc(k_scaled, 1)
            turns(pool, body)

        @block.tensor
        def _(pe):
            def turn_keys(t, n):
                pe.wait_ge(k_scaled, t * HALVES + (n + 1))
                wait(pe, k_copied, t * HALVES + (n - 1))
                if n < 2:
                    wait(pe, p_copied, t * len(sets))
                for h in range(GROUPS):
                    for q_ in range(CHUNK_PAGES):
                        mm = nc.tensor.transpose(k_ps[:, n % 2, h, q_ * P:(q_ + 1) * P],
                                                 stage[n][:, q_, h * HD:(h + 1) * HD], g.ident[:])
                mm.then_inc(k_turned, 1)

            def score(t, n):
                c, b = divmod(n, 2)
                pe.wait_ge(k_copied, t * HALVES + (n + 1))
                wait(pe, s_taken, t * CH + (c - 1 if c else 0))
                for h in range(GROUPS):
                    j = 2 * b + h
                    mm = nc.tensor.matmul(s_ps[32 * j:32 * j + 32, c % 2], q[:, 32 * j:32 * j + 32],
                                          turned_k[:, n % 2, h], start=True, stop=True)
                mm.then_inc(half_scored, 1)

            def body(t):
                pe.wait_ge(q_ready, t + 1)
                for j in range(4):
                    rows = slice(32 * j, 32 * j + 32)
                    nc.tensor.matmul(small_ps[rows, 0:P], q[:, rows], cmp_k[:, j // 2], start=True, stop=True, skip_group_check=True)
                for j in range(4):
                    rows = slice(32 * j, 32 * j + 32)
                    for w in range(2):
                        mm = nc.tensor.matmul(small_ps[rows, P + w * NEW:P + (w + 1) * NEW], q[:, rows],
                                              g.new_k[:, 2 * w + j % 2], start=True, stop=True,
                                              skip_group_check=True)
                mm.then_inc(small_scored, 1)
                turn_keys(t, 0)
                turn_keys(t, 1)
                pe.wait_ge(cmp_ready, t + 1)
                nc.tensor.matmul(small_ps[:, 256:256 + P], g.sparse_masks[:, SP_SAME:SP_SAME + P], s[:, 0:P],
                                 start=True, stop=True, skip_group_check=True).then_inc(group_summed, 1)
                for n in range(HALVES):
                    score(t, n)
                    if n + 2 < HALVES:
                        turn_keys(t, n + 2)
                pe.wait_ge(scaled, t + 1)
                for i, chunks in enumerate(sets):
                    pe.wait_ge(k_copied, (t + 1) * HALVES)
                    if i >= 2:
                        pe.wait_ge(p_copied, t * len(sets) + (i - 1))
                    for e, x in enumerate(chunks):
                        col, w = P_CHUNKS[x]
                        mm = nc.tensor.transpose(k_ps[0:w, i % 2, e // 4, e % 4 * P:(e % 4 + 1) * P], s[:, col:col + w],
                                                 g.ident[:])
                    mm.then_inc(p_turned, 1)
                wait(pe, o_taken, t)
                for i, chunks in enumerate(sets):
                    pe.wait_ge(p_copied, t * len(sets) + (i + 1))
                    for x in chunks:
                        col, w = P_CHUNKS[x]
                        for j in range(4):
                            b, h = divmod(j, 2)
                            if x == 0:
                                v = cmp_v[:, b]
                            elif w == NEW:
                                tile = (SEL_V if col == S_SEL_NEW else WIN_V) - HEADS + h
                                v = g.rows_sampled[:, tile * HD:(tile + 1) * HD]
                            else:
                                first, quarter = values_of(col)
                                v = values[first + b][:, quarter, h * HD:(h + 1) * HD]
                            mm = nc.tensor.matmul(o_ps[32 * j:32 * j + 32, 0:HD], probs[0:w, x, 32 * j:32 * j + 32], v,
                                                  start=(x == 0), stop=(x == len(P_CHUNKS) - 1))
                    mm.then_inc(multiplied, 1)
                pe.wait_ge(o_taken, t + 1)
                nc.tensor.transpose(small_ps[:, 384:512], o[:], g.ident[:]).then_inc(o_turned, 1)
            turns(pe, body)

        @block.scalar
        def _(act):
            def body(t):
                def square(n):
                    loads = 16 * (CHUNK_PAGES if n < 2 * CHUNKS else 2)
                    act.wait_ge(stage_loaded[n], t * loads + loads)
                    wait(act, k_mean, t * HALVES + (n - 1))
                    nc.scalar.activation(squares[n % 2], stage[n].rearrange("p q n -> p (q n)"), ACT.Square
                                         ).then_inc(k_squared, 1)

                def root(n):
                    act.wait_ge(k_mean, t * HALVES + (n + 1))
                    nc.scalar.activation(ss[:, n], ss[:, n], ACT.Sqrt).then_inc(k_root, 1)

                for n in range(3):
                    square(n)
                root(0)
                root(1)
                act.wait_ge(cmp_negated, t + 1)
                nc.scalar.activation(s[:, 0:P], s[:, 0:P], ACT.Exp, bias=neg_max[:, 0:1],
                                     accum_out=sums[:, 0:1]).then_inc(cmp_exped, 1)
                for n in range(HALVES):
                    if n + 2 < HALVES:
                        root(n + 2)
                    if n + 3 < HALVES:
                        square(n + 3)
                    act.wait_ge(k_turned, t * HALVES + (n + 1))
                    wait(act, half_scored, t * HALVES + (n - 1))
                    gk = VEC["nsa_g_k"] + (1 if n < 2 * CHUNKS else 2)
                    nc.scalar.activation(turned_k[:, n % 2], k_ps[:, n % 2], ACT.Copy, scale=g.vec[:, gk:gk + 1]
                                         ).then_inc(k_copied, 1)
                act.wait_ge(negated, t + 1)
                for r, (c0, c1) in ((1, (S_SEL, S_WIN)), (2, (S_WIN, S_COLS))):
                    nc.scalar.activation(s[:, c0:c1], s[:, c0:c1], ACT.Exp, bias=neg_max[:, r:r + 1],
                                         accum_out=sums[:, r:r + 1]).then_inc(exped, 1)
                for i, chunks in enumerate(sets):
                    act.wait_ge(p_turned, t * len(sets) + (i + 1))
                    wait(act, multiplied, t * len(sets))
                    for h in range(2):
                        part = chunks[4 * h:4 * h + 4]
                        whole = [x for x in part if P_CHUNKS[x][1] == P]
                        runs = []
                        for x in whole:
                            if runs and runs[-1][-1] == x - 1:
                                runs[-1].append(x)
                            else:
                                runs.append([x])
                        for x in part:
                            if x not in whole:
                                e = x - part[0]
                                last = nc.scalar.activation(probs[0:NEW, x], k_ps[0:NEW, i % 2, h, e * P:(e + 1) * P],
                                                            ACT.Copy)
                        for run in runs:
                            e = run[0] - part[0]
                            last = nc.scalar.activation(
                                probs[:, run[0]:run[-1] + 1],
                                k_ps[:, i % 2, h, e * P:(e + len(run)) * P].rearrange("p (c n) -> p c n", n=P), ACT.Copy)
                    last.then_inc(p_copied, 1)
            turns(act, body)

        @block.vector
        def _(dve):
            mask = g.sparse_masks
            far = g.bias_far[:, 0:1]
            linked = Chain(dve, link)
            linked(nc.vector.tensor_scalar(cmp_bias[:], mask[:, SP_GROUP:SP_GROUP + P], far, None, ALU.add))
            for h in range(GROUPS):
                cols = slice(h * CMP_BLOCKS + CMP_BLOCKS - 4, (h + 1) * CMP_BLOCKS)
                linked(nc.vector.tensor_tensor(
                    cmp_bias[:, cols], mask[:, SP_GROUP + cols.start:SP_GROUP + cols.stop],
                    g.bias_near[:, CMP_LEN - 1:P:CMP_LEN], ALU.add))
            linked(nc.vector.memset(win_bias[:], 0.0))
            linked(nc.vector.tensor_scalar(win_bias[:], win_bias[:], far, None, ALU.add))
            linked(nc.vector.tensor_tensor(win_bias[:, 0:32], win_bias[:, 0:32], mask[:, SP_OLD:SP_OLD + 32], ALU.add))
            linked(nc.vector.tensor_copy(win_bias[:, WINDOW - P:WINDOW], g.bias_near[:, 0:P]))
            setup = linked.n

            def sum_squares(t, n, linked):
                dve.wait_ge(k_squared, t * HALVES + (n + 1))
                wait(dve, k_scaled, t * HALVES + (n + 1 - HALVES))
                linked(nc.vector.tensor_reduce(ss[:, n], squares[n % 2].rearrange("p (c d) -> p c d", d=HD),
                                               AX_X, ALU.add))
                nc.vector.tensor_scalar(ss[:, n], ss[:, n], 1.0 / HD, EPS, ALU.mult, ALU.add).then_inc(k_mean, 1)

            def invert(t, n):
                dve.wait_ge(k_root, t * HALVES + (n + 1))
                nc.vector.reciprocal(ss[:, n], ss[:, n]).then_inc(k_inverse, 1)

            def take_scores(t, c):
                dve.wait_ge(half_scored, t * HALVES + (2 * c + 2))
                if c == CHUNKS:
                    last = nc.vector.tensor_tensor(s[:, S_WIN:S_WIN + 512], s_ps[:, c % 2], win_bias[:], ALU.add)
                else:
                    wide = 8 if c < CHUNKS - 1 else 6
                    last = nc.vector.tensor_tensor(
                        s[:, S_SEL + c * 512:S_SEL + c * 512 + wide * SEL_LEN].rearrange("p (n k) -> p n k", k=SEL_LEN),
                        s_ps[:, c % 2, 0:wide * SEL_LEN].rearrange("p (n k) -> p n k", k=SEL_LEN),
                        sel_bias[:, c * 8:c * 8 + wide].unsqueeze(2).to_broadcast([P, wide, SEL_LEN]), ALU.add)
                    if wide < 8:
                        last = nc.vector.tensor_tensor(s[:, S_SEL_NEW - P:S_SEL_NEW], s_ps[:, c % 2, 512 - P:512],
                                                       near_bias[:], ALU.add)
                last.then_inc(s_taken, 1)

            def body(t, base):
                linked = Chain(dve, link, base)
                wait(dve, multiplied, t * len(sets))
                nc.vector.tensor_copy(cmp_v[:], g.cmp_v[:, bass.ds(t * 2, 2)])
                nc.vector.tensor_copy(cmp_k[:].rearrange("p b n -> p (b n)"),
                                      g.cmp_k[:, bass.ds(t, 1), 0:PAIR_COLS].squeeze(1))
                nc.vector.tensor_copy(q[:], g.q_sampled[:, bass.ds(t, 1)].squeeze(1)).then_inc(q_ready, 1)
                linked(nc.vector.tensor_tensor(
                    new_bias[:].rearrange("p (b l) -> p b l", l=STEP),
                    mask[:, bass.ds(t * SAMPLED + SP_OTHER, SAMPLED)].rearrange("p (b l) -> p b l", l=STEP),
                    g.bias_near[:, P:P + STEP].unsqueeze(1).to_broadcast([P, BATCH, STEP]), ALU.add))
                for n in range(3):
                    sum_squares(t, n, linked)
                invert(t, 0)
                invert(t, 1)
                dve.wait_ge(small_scored, t + 1)
                wait(dve, p_turned, t * len(sets))
                nc.vector.tensor_tensor(s[:, S_SEL_NEW:S_WIN], small_ps[:, P:P + NEW], new_bias[:], ALU.add)
                nc.vector.tensor_tensor(s[:, S_WIN_NEW:S_COLS], small_ps[:, P + NEW:P + 2 * NEW], new_bias[:], ALU.add)
                linked(nc.vector.tensor_tensor(s[:, 0:P], small_ps[:, 0:P], cmp_bias[:], ALU.add))
                linked(nc.vector.tensor_reduce(neg_max[:, 0:1], s[:, 0:P], AX_X, ALU.max))
                nc.vector.tensor_scalar(neg_max[:, 0:1], neg_max[:, 0:1], 0.1 * MASKED, -1.0, ALU.max, ALU.mult
                                        ).then_inc(cmp_negated, 1)
                dve.wait_ge(cmp_exped, t + 1)
                linked(nc.vector.tensor_scalar(sums[:, 0:1], sums[:, 0:1], 1e-30, None, ALU.max))
                linked(nc.vector.reciprocal(coef[:, 0:1], sums[:, 0:1]))
                nc.vector.tensor_scalar(s[:, 0:P], s[:, 0:P], coef[:, 0:1], None, ALU.mult).then_inc(cmp_ready, 1)
                sum_squares(t, 3, linked)
                invert(t, 2)
                dve.wait_ge(group_summed, t + 1)
                linked(nc.vector.tensor_reduce(pair_score[:], small_ps[:, 256:256 + P].rearrange(
                    "p (n c) -> p n c", c=2), AX_X, ALU.add))
                half = SEL_BLOCKS - 1
                linked(nc.vector.tensor_tensor(block_score[:, 0:half], pair_score[:, 0:half],
                                               pair_score[:, half:2 * half], ALU.add))
                linked(nc.vector.memset(block_score[:, 0:1], FORCED))
                linked(nc.vector.memset(block_score[:, half - 1:half + 1], FORCED))
                for r in range(TOP_ROUNDS):
                    nc.vector.memset(spare[:], 0.0)
                    linked(nc.vector.max(top[:, r], block_score[:]))
                    nc.vector.memset(spare[:], 0.0)
                    linked(nc.vector.match_replace(block_score[:], top[:, r], block_score[:], MASKED))
                linked(nc.vector.tensor_scalar(unselected[:], block_score[:], 0.0, MASKED, ALU.is_ge, ALU.mult))
                linked(nc.vector.tensor_scalar(sel_bias[:], unselected[:], far, None, ALU.add))
                linked(nc.vector.tensor_tensor(
                    near_bias[:].rearrange("p (n k) -> p n k", k=SEL_LEN),
                    g.bias_near[:, 0:P].rearrange("p (n k) -> p n k", k=SEL_LEN),
                    unselected[:, half - 2:half].unsqueeze(2).to_broadcast([P, 2, SEL_LEN]), ALU.add))
                for n in range(1, HALVES):
                    if n + 3 < HALVES:
                        sum_squares(t, n + 3, linked)
                    if n + 2 < HALVES:
                        invert(t, n + 2)
                    if n % 2 == 1:
                        take_scores(t, n // 2)
                dve.wait_ge(s_taken, t * CH + CH)
                nc.vector.tensor_reduce(neg_max[:, 1:2], s[:, S_SEL:S_WIN], AX_X, ALU.max)
                linked(nc.vector.tensor_reduce(neg_max[:, 2:3], s[:, S_WIN:S_COLS], AX_X, ALU.max))
                nc.vector.tensor_scalar(neg_max[:, 1:3], neg_max[:, 1:3], 0.1 * MASKED, -1.0, ALU.max, ALU.mult
                                        ).then_inc(negated, 1)
                dve.wait_ge(exped, t * 2 + 2)
                linked(nc.vector.tensor_scalar(sums[:, 1:3], sums[:, 1:3], 1e-30, None, ALU.max))
                linked(nc.vector.reciprocal(coef[:, 1:3], sums[:, 1:3]))
                gates = g.gates_sampled[:, bass.ds(t, 1)].squeeze(1)
                linked(nc.vector.tensor_tensor(coef[:, 1:3], coef[:, 1:3], gates[:, 1:3], ALU.mult))
                nc.vector.tensor_scalar(s[:, 0:P], s[:, 0:P], gates[:, 0:1], None, ALU.mult)
                nc.vector.tensor_scalar(s[:, S_SEL:S_WIN], s[:, S_SEL:S_WIN], coef[:, 1:2], None, ALU.mult)
                nc.vector.tensor_scalar(s[:, S_WIN:S_COLS], s[:, S_WIN:S_COLS], coef[:, 2:3], None, ALU.mult
                                        ).then_inc(scaled, 1)
                dve.wait_ge(multiplied, t * len(sets) + len(sets))
                nc.vector.tensor_copy(o[:], o_ps[:, 0:HD]).then_inc(o_taken, 1)
                dve.wait_ge(o_turned, t + 1)
                for j in range(4):
                    b, h = divmod(j, 2)
                    nc.vector.tensor_copy(
                        g.h[:, h * HPG:(h + 1) * HPG, bass.ds(t * (2 * STEP) + (SEQ + b * STEP), STEP)],
                        small_ps[:, 384 + 32 * j:384 + 32 * j + HPG * STEP].rearrange("p (h l) -> p h l", l=STEP))
                return linked.n

            per_turn = body(0, setup)
            with dve.Fori(1, PAIRS) as t:
                assert body(t, t * per_turn + setup) == per_turn


def attend_memory_sampled(nc, g, a, layer, query, out):
    with ExitStack() as ctx:
        sb = lambda n, s: ctx.enter_context(nc.sbuf_tensor(f"mem{layer}_{n}", s, F32))
        ps = lambda n, s: ctx.enter_context(nc.psum_tensor(f"mem{layer}_{n}", s, F32))
        sem = counters(nc, ctx, f"mem{layer}_")
        STAGES = 4
        q = sb("q", [P, MEM_HEADS, BATCH, SAMPLED])
        stage = sb("stage", [P, STAGES, QT, MEM_WIDTH])
        squares = sb("squares", [P, 2, QT * MEM_WIDTH])
        ss = sb("ss", [P, BATCH, QT * MEM_HEADS])
        turned_k = sb("turned_k", [P, 2, MEM_HEADS, MEM_LEN])
        values = g.ring[:].rearrange("p b k n -> p (b k) n").rearrange("p (b t) n -> p b t n", t=QT)
        s = sb("s", [P, MEM_LEN])
        probs = sb("probs", [P, QT, MEM_HEADS, BATCH, SAMPLED])
        stat = sb("stat", [P, 3])
        o = sb("o", [P, HD])
        k_ps = ps("k_ps", [P, 2, 2, 512])
        s_ps = ps("s_ps", [P, 512])
        t_ps = ps("t_ps", [P, 512])
        o_ps = ps("o_ps", [P, 512])
        blank, q_placed, k_squared, k_mean, k_root, k_inverse, k_scaled, k_turned, k_copied, scored, negated, exped, \
            scaled, turned, placed, multiplied, o_taken, o_turned, values_loaded, link = map(sem, (
                "blank", "q_placed", "k_squared", "k_mean", "k_root", "k_inverse", "k_scaled", "k_turned", "k_copied",
                "scored", "negated", "exped", "scaled", "turned", "placed", "multiplied", "o_taken", "o_turned",
                "values_loaded", "link"))
        loaded = [sem(f"loaded{b}") for b in range(STAGES)]
        block = ctx.enter_context(nc.Block())
        rows = a.cache_mem_kv[layer].rearrange("b (t p) k h d -> b p t k (h d)", p=P)

        @block.sync
        def _(sp):
            for b in range(BATCH):
                wait(sp, k_turned, b - STAGES + 1)
                sp.dma_start(stage[:, b % STAGES], rows[b, :, :, 0]).then_inc(loaded[b % STAGES], 16)
                sp.dma_start(values[:, b], rows[b, :, :, 1]).then_inc(values_loaded, 16)

        @block.gpsimd
        def _(pool):
            nc.gpsimd.memset(q[:], 0.0).then_inc(blank, 1)
            nc.gpsimd.memset(probs[:], 0.0).then_inc(blank, 1)
            for b in range(BATCH):
                pool.wait_ge(k_inverse, b + 1)
                k = stage[:, b % STAGES].rearrange("p t (h d) -> p (t h) d", d=HD)
                nc.gpsimd.tensor_tensor(k, k, ss[:, b].unsqueeze(2).to_broadcast([P, QT * MEM_HEADS, HD]),
                                        ALU.mult).then_inc(k_scaled, 1)

        @block.tensor
        def _(pe):
            pe.wait_ge(q_placed, BATCH)

            def turn(b):
                pe.wait_ge(k_scaled, b + 1)
                wait(pe, k_copied, b - 1)
                for h in range(MEM_HEADS):
                    for t in range(QT):
                        mm = nc.tensor.transpose(k_ps[:, b % 2, h // 2, (h % 2 * QT + t) * P:(h % 2 * QT + t + 1) * P],
                                                 stage[:, b % STAGES, t, h * HD:(h + 1) * HD], g.ident[:])
                mm.then_inc(k_turned, 1)

            turn(0)
            for b in range(BATCH):
                if b + 1 < BATCH:
                    turn(b + 1)
                pe.wait_ge(k_copied, b + 1)
                for h in range(MEM_HEADS):
                    mm = nc.tensor.matmul(s_ps[32 * h:32 * h + 32, 0:MEM_LEN], q[:, h, b], turned_k[:, b % 2, h],
                                          start=(b == 0), stop=(b == BATCH - 1), skip_group_check=True)
                mm.then_inc(scored, 1)
            pe.wait_ge(scaled, 1)
            for t in range(QT):
                mm = nc.tensor.transpose(t_ps[:, t * P:(t + 1) * P], s[:, t * P:(t + 1) * P], g.ident[:])
            mm.then_inc(turned, 1)
            pe.wait_ge(placed, BATCH)
            pe.wait_ge(values_loaded, 16 * BATCH)
            for b in range(BATCH):
                for t in range(QT):
                    for h in range(MEM_HEADS):
                        mm = nc.tensor.matmul(o_ps[32 * h:32 * h + 32, 0:HD], probs[:, t, h, b],
                                              values[:, b, t, h * HD:(h + 1) * HD], start=(b == 0 and t == 0),
                                              stop=(b == BATCH - 1 and t == QT - 1), skip_group_check=True)
            mm.then_inc(multiplied, 1)
            pe.wait_ge(o_taken, 1)
            nc.tensor.transpose(t_ps[:, 384:512], o[:], g.ident[:]).then_inc(o_turned, 1)

        @block.scalar
        def _(act):
            def square(b):
                act.wait_ge(loaded[b % STAGES], 16 * (b // STAGES + 1))
                wait(act, k_mean, b - 1)
                nc.scalar.activation(squares[:, b % 2], stage[:, b % STAGES].rearrange("p t n -> p (t n)"), ACT.Square
                                     ).then_inc(k_squared, 1)

            def root(b):
                act.wait_ge(k_mean, b + 1)
                nc.scalar.activation(ss[:, b], ss[:, b], ACT.Sqrt).then_inc(k_root, 1)

            square(0)
            square(1)
            root(0)
            for b in range(BATCH):
                if b + 1 < BATCH:
                    root(b + 1)
                if b + 2 < BATCH:
                    square(b + 2)
                act.wait_ge(k_turned, b + 1)
                wait(act, scored, b - 1)
                gk = VEC["g_mem_k"] + layer
                nc.scalar.activation(turned_k[:, b % 2].rearrange("p (u h) k -> p u (h k)", u=2), k_ps[:, b % 2],
                                     ACT.Copy, scale=g.vec[:, gk:gk + 1]).then_inc(k_copied, 1)
            act.wait_ge(negated, 1)
            nc.scalar.activation(s[:], s_ps[:, 0:MEM_LEN], ACT.Exp, bias=stat[:, 0:1], accum_out=stat[:, 1:2]
                                 ).then_inc(exped, 1)

        @block.vector
        def _(dve):
            linked = Chain(dve, link)
            dve.wait_ge(blank, 2)
            for b in range(BATCH):
                cols = slice(b * STEP, (b + 1) * STEP)
                nc.vector.tensor_copy(q[:, :, b, cols], query[:, :, cols]).then_inc(q_placed, 1)
            def sum_squares(b):
                dve.wait_ge(k_squared, b + 1)
                linked(nc.vector.tensor_reduce(ss[:, b], squares[:, b % 2].rearrange("p (c d) -> p c d", d=HD),
                                               AX_X, ALU.add))
                nc.vector.tensor_scalar(ss[:, b], ss[:, b], 1.0 / HD, EPS, ALU.mult, ALU.add).then_inc(k_mean, 1)

            sum_squares(0)
            for b in range(BATCH):
                if b + 1 < BATCH:
                    sum_squares(b + 1)
                dve.wait_ge(k_root, b + 1)
                nc.vector.reciprocal(ss[:, b], ss[:, b]).then_inc(k_inverse, 1)
            dve.wait_ge(scored, BATCH)
            linked(nc.vector.tensor_reduce(stat[:, 0:1], s_ps[:, 0:MEM_LEN], AX_X, ALU.max))
            nc.vector.tensor_scalar(stat[:, 0:1], stat[:, 0:1], -1.0, None, ALU.mult).then_inc(negated, 1)
            dve.wait_ge(exped, 1)
            linked(nc.vector.reciprocal(stat[:, 2:3], stat[:, 1:2]))
            nc.vector.tensor_scalar(s[:], s[:], stat[:, 2:3], None, ALU.mult).then_inc(scaled, 1)
            dve.wait_ge(turned, 1)
            for b in range(BATCH):
                cols = slice(b * STEP, (b + 1) * STEP)
                nc.vector.tensor_copy(probs[:, :, :, b, cols], t_ps[:, 0:QT * P].rearrange(
                    "p (t h n) -> p t h n", t=QT, h=MEM_HEADS)[:, :, :, cols]).then_inc(placed, 1)
            dve.wait_ge(multiplied, 1)
            nc.vector.tensor_copy(o[:], o_ps[:, 0:HD]).then_inc(o_taken, 1)
            dve.wait_ge(o_turned, 1)
            nc.vector.tensor_copy(out, t_ps[:, 384:512].rearrange("p (h n) -> p h n", h=MEM_HEADS))


Q_TILE, K_TILE, V_TILE, R_TILE, GLA_MEM_Q = 0, GLA_KT, 2 * GLA_KT, 4 * GLA_KT, 6 * GLA_KT
ET = GLA_DV // P
V_TILES = GLA_HEADS * ET
LAST = SEQ - 1


def head_pieces(h):
    first, last = h * GLA_DK, (h + 1) * GLA_DK
    return [(t, slice(max(first - t * P, 0), min(last - t * P, P)))
            for t in range(first // P, -(-last // P))]


def by_batch(ap):
    return ap.rearrange("p k (b l) -> p k b l", l=STEP)


def prepare_linear(nc, g, a):
    with ExitStack() as ctx:
        sb = lambda n, s: ctx.enter_context(nc.sbuf_tensor(f"lin_{n}", s, F32))
        sem = counters(nc, ctx, "lin_")
        w_a2 = sb("w_a2", [GATE_RANK, GLA_KW])
        keep = sb("keep", [P, GLA_KT, TOKENS])
        z, neg, expo = g.h[:, 0:GLA_KT], g.h[:, GLA_KT:2 * GLA_KT], sb("expo", [P, GLA_KT, TOKENS])
        to_end, k_end = g.p[:, V_TILE:V_TILE + GLA_KT], g.p[:, V_TILE + GLA_KT:V_TILE + 2 * GLA_KT]
        z_ps = ctx.enter_context(nc.psum_tensor("lin_z_ps", [P, GLA_KT, 512], F32))
        rows_ps = ctx.enter_context(nc.psum_tensor("lin_rows_ps", [P, 2, 512], F32))
        loaded, blank, z_done, turned, rows_copied, neg_done, exped, plus_one, logged, link, end_diff, end_exped, \
            start_exped, k_done, pool_link = map(sem, (
                "loaded", "blank", "z_done", "turned", "rows_copied", "neg_done", "exped", "plus_one", "logged",
                "link", "end_diff", "end_exped", "start_exped", "k_done", "pool_link"))
        block = ctx.enter_context(nc.Block())
        width = lambda tok: P if tok < QT else SAMPLED
        v_sets = [(V_TILE + 4 * s, 4, tok, g.v_rows, s * 512) for s in range(V_TILES // 4) for tok in range(QT + 1)]
        k_sets = [(V_TILE + GLA_KT + first, n, tok, g.k_rows, first * P) for first, n in ((0, 4), (4, 2))
                  for tok in range(QT + 1)]
        decay = g.decay

        @block.sync
        def _(sp):
            sp.dma_start(w_a2[:], a.gla_w_a2[0]).then_inc(loaded, 16)
            sp.dma_start(g.linear_masks[:], a.linear_masks).then_inc(loaded, 16)
            sp.wait_ge(loaded, 32)

        @block.gpsimd
        def _(pool):
            linked = Chain(pool, pool_link)
            linked(nc.gpsimd.memset(keep[:], 1.0))
            nc.gpsimd.memset(keep[:, :, 0:1], 0.0)
            nc.gpsimd.memset(keep[:, :, SEQ:TOKENS:STEP], 0.0).then_inc(blank, 1)
            queries = g.p[:, Q_TILE:Q_TILE + GLA_KT]
            linked(nc.gpsimd.tensor_scalar(queries, queries, GLA_DK ** -0.5, None, ALU.mult))
            pool.wait_ge(start_exped, 1)
            nc.gpsimd.tensor_tensor(g.q_start[:], g.from_start[:], queries[:, :, SEQ:TOKENS], ALU.mult)

        @block.tensor
        def _(pe):
            pe.wait_ge(loaded, 32)
            for t in range(GLA_KT):
                mm = nc.tensor.matmul(z_ps[:, t, 0:TOKENS], w_a2[:, t * P:(t + 1) * P], g.gates[0:GATE_RANK],
                                      start=True, stop=True)
            mm.then_inc(z_done, 1)
            for n, (tile, count, tok, _, _) in enumerate(v_sets + k_sets):
                if n == len(v_sets):
                    pe.wait_ge(k_done, 1)
                wait(pe, rows_copied, n - 1)
                for o in range(count):
                    mm = nc.tensor.transpose(rows_ps[0:width(tok), n % 2, o * P:(o + 1) * P],
                                             g.p[:, tile + o, tok * P:tok * P + width(tok)], g.ident[:])
                mm.then_inc(turned, 1)

        @block.scalar
        def _(act):
            def copy(n):
                _, count, tok, rows, col = (v_sets + k_sets)[n]
                act.wait_ge(turned, n + 1)
                nc.scalar.activation(rows[0:width(tok), tok, col:col + count * P],
                                     rows_ps[0:width(tok), n % 2, 0:count * P], ACT.Copy).then_inc(rows_copied, 1)

            for n in range(3):
                copy(n)
            act.wait_ge(neg_done, 1)
            nc.scalar.activation(expo[:], expo[:], ACT.Exp).then_inc(exped, 1)
            for n in range(3, 6):
                copy(n)
            act.wait_ge(plus_one, 1)
            nc.scalar.activation(expo[:], expo[:], ACT.Ln).then_inc(logged, 1)
            for n in range(6, len(v_sets)):
                copy(n)
            act.wait_ge(end_diff, 1)
            nc.scalar.activation(to_end, to_end, ACT.Exp, scale=1.0 / GATE_TAU).then_inc(end_exped, 1)
            nc.scalar.activation(g.from_start[:], decay[:, :, SEQ:TOKENS], ACT.Exp, scale=1.0 / GATE_TAU
                                 ).then_inc(start_exped, 1)
            for n in range(len(v_sets), len(v_sets) + len(k_sets)):
                copy(n)

        @block.vector
        def _(dve):
            linked = Chain(dve, link)
            dve.wait_ge(z_done, 1)
            for t in range(GLA_KT):
                col = g.vec[:, VEC["gla_b_a"] + t:VEC["gla_b_a"] + t + 1]
                last = nc.vector.tensor_scalar(z[:, t], z_ps[:, t, 0:TOKENS], col, None, ALU.add)
            linked(last)
            linked(nc.vector.tensor_scalar(neg, z, 0.0, None, ALU.min))
            nc.vector.scalar_tensor_tensor(expo[:], neg, 2.0, z, ALU.mult, ALU.subtract).then_inc(neg_done, 1)
            dve.wait_ge(exped, 1)
            nc.vector.tensor_scalar(expo[:], expo[:], 1.0, None, ALU.add).then_inc(plus_one, 1)
            dve.wait_ge(logged, 1)
            linked(nc.vector.tensor_tensor(expo[:], neg, expo[:], ALU.subtract))
            dve.wait_ge(blank, 1)
            flat = lambda t: t.rearrange("p k n -> p (k n)")
            linked(nc.vector.tensor_tensor_scan(flat(decay[:]), flat(keep[:]), flat(expo[:]), 0.0, ALU.mult, ALU.add))
            dve.wait_ge(turned, len(v_sets))
            nc.vector.tensor_tensor(to_end[:, :, 0:SEQ], decay[:, :, LAST:SEQ].to_broadcast([P, GLA_KT, SEQ]),
                                    decay[:, :, 0:SEQ], ALU.subtract)
            sampled = by_batch(decay[:, :, SEQ:TOKENS])
            nc.vector.tensor_tensor(by_batch(to_end[:, :, SEQ:TOKENS]),
                                    sampled[:, :, :, STEP - 1:STEP].to_broadcast([P, GLA_KT, BATCH, STEP]),
                                    sampled, ALU.subtract).then_inc(end_diff, 1)
            dve.wait_ge(end_exped, 1)
            nc.vector.tensor_tensor(k_end, to_end, g.p[:, K_TILE:K_TILE + GLA_KT], ALU.mult).then_inc(k_done, 1)


def score_levels(nc, g):
    CROSS = LEVELS
    with ExitStack() as ctx:
        sb = lambda n, s: ctx.enter_context(nc.sbuf_tensor(f"lev_{n}", s, F32))
        sem = counters(nc, ctx, "lev_")
        own = sb("decayed", [P, 2, GLA_KT, TOKENS])
        decayed_q = [g.h[:, 0:GLA_KT], own[:, 0]]
        decayed_k = [g.h[:, GLA_KT:2 * GLA_KT], own[:, 1]]
        factor = [g.p[:, V_TILE:V_TILE + GLA_KT], g.p[:, V_TILE + GLA_KT:V_TILE + 2 * GLA_KT]]
        masked_scores = sb("masked", [P, 2, GLA_HEADS, QT, P])
        masked_to = [masked_scores[:, n] for n in range(2)]
        few = sb("few", [SAMPLED, 2, GLA_HEADS, SAMPLED])
        ps = ctx.enter_context(nc.psum_tensor("lev_ps", [P, 2, GLA_HEADS, 512], F32))
        diffed, distanced, exped, q_decayed, k_decayed, scored, masked, added = map(sem, (
            "diffed", "distanced", "exped", "q_decayed", "k_decayed", "scored", "masked", "added"))
        block = ctx.enter_context(nc.Block())
        q, k = g.p[:, Q_TILE:Q_TILE + GLA_KT], g.p[:, K_TILE:K_TILE + GLA_KT]
        few_levels = [0, 1, 2]

        def span(level):
            return TOKENS if level in few_levels else SEQ

        def blocked(ap, level):
            return ap.rearrange("p k (n c) -> p k n c", c=2 ** level)

        @block.vector
        def _(dve):
            def diff(level):
                w, c = span(level), 2 ** level
                wait(dve, k_decayed, level - 2)
                d = blocked(g.decay[:, :, 0:w], level)
                nc.vector.tensor_tensor(
                    blocked(factor[level % 2][:, :, 0:w], level), d,
                    d[:, :, :, c // 2 - 1:c // 2].to_broadcast([P, GLA_KT, w // c, c]),
                    ALU.subtract).then_inc(diffed, 1)

            def queries(level):
                w = span(level)
                dve.wait_ge(exped, level)
                wait(dve, scored, level - 1)
                nc.vector.tensor_tensor(decayed_q[level % 2][:, :, 0:w], q[:, :, 0:w], factor[level % 2][:, :, 0:w],
                                        ALU.mult).then_inc(q_decayed, 1)

            def mask(level):
                dve.wait_ge(scored, level + 1)
                src = ps[:, level % 2]
                if level == CROSS:
                    nc.vector.tensor_copy(g.att[:, :, 1], src[:, :, 0:P]).then_inc(masked, 1)
                    return
                wait(dve, added, level - 2)
                m = g.linear_masks[:, level * P:(level + 1) * P]
                last = nc.vector.tensor_tensor(
                    g.att[:, :, 0:3:2] if level == 0 else masked_to[level % 2],
                    src[:, :, 0:SEQ].rearrange("p h (t i) -> p h t i", t=QT),
                    m.unsqueeze(1).unsqueeze(1).to_broadcast([P, GLA_HEADS, QT, P]), ALU.mult)
                if level in few_levels:
                    last = nc.vector.tensor_tensor(
                        g.att[0:SAMPLED, :, 3, 0:SAMPLED] if level == 0 else few[:, level % 2],
                        src[0:SAMPLED, :, SEQ:TOKENS],
                        m[0:SAMPLED, 0:SAMPLED].unsqueeze(1).to_broadcast([SAMPLED, GLA_HEADS, SAMPLED]), ALU.mult)
                last.then_inc(masked, 1)

            diff(1)
            diff(2)
            for level in range(CROSS + 1):
                if level + 1 <= CROSS:
                    queries(level + 1)
                if level + 3 <= CROSS:
                    diff(level + 3)
                mask(level)

        @block.scalar
        def _(act):
            for level in range(1, CROSS + 1):
                f = factor[level % 2][:, :, 0:span(level)]
                act.wait_ge(diffed, level)
                nc.scalar.activation(f, f, ACT.Abs).then_inc(distanced, 1)
                act.wait_ge(distanced, level)
                nc.scalar.activation(f, f, ACT.Exp, scale=-1.0 / GATE_TAU).then_inc(exped, 1)

        @block.gpsimd
        def _(pool):
            def keys(level):
                w = span(level)
                pool.wait_ge(exped, level)
                wait(pool, scored, level - 1)
                pool.wait_ge(q_decayed, level)
                nc.gpsimd.tensor_tensor(decayed_k[level % 2][:, :, 0:w], k[:, :, 0:w], factor[level % 2][:, :, 0:w],
                                        ALU.mult).then_inc(k_decayed, 1)

            def add(level):
                pool.wait_ge(masked, level + 1)
                wait(pool, added, level - 1)
                to = g.att[:, :, 0:3:2]
                last = nc.gpsimd.tensor_tensor(to, to, masked_to[level % 2], ALU.add)
                if level in few_levels:
                    to = g.att[0:SAMPLED, :, 3, 0:SAMPLED]
                    last = nc.gpsimd.tensor_tensor(to, to, few[:, level % 2], ALU.add)
                last.then_inc(added, 1)

            for level in range(1, CROSS + 1):
                keys(level)
                if level >= 2:
                    add(level - 1)

        @block.tensor
        def _(pe):
            for level in range(CROSS + 1):
                lq, lk = (q, k) if level == 0 else (decayed_q[level % 2], decayed_k[level % 2])
                wait(pe, k_decayed, level)
                wait(pe, masked, level - 1)
                spans = [(slice(0, P), slice(P, SEQ), 0)] if level == CROSS else \
                    [(slice(t * P, (t + 1) * P), slice(t * P, (t + 1) * P), t * P) for t in range(QT)]
                if level in few_levels:
                    spans.append((slice(SEQ, TOKENS), slice(SEQ, TOKENS), SEQ))
                for h in range(GLA_HEADS):
                    for keys, queries, col in spans:
                        n = keys.stop - keys.start
                        pieces = head_pieces(h)
                        for e, (t, rows) in enumerate(pieces):
                            mm = nc.tensor.matmul(ps[0:n, level % 2, h, col:col + n], lk[rows, t, keys],
                                                  lq[rows, t, queries], start=(e == 0), stop=(e == len(pieces) - 1))
                mm.then_inc(scored, 1)


def linear_outputs(nc, g, a):
    with ExitStack() as ctx:
        sb = lambda n, s: ctx.enter_context(nc.sbuf_tensor(f"linout_{n}", s, F32))
        ps = lambda n, s: ctx.enter_context(nc.psum_tensor(f"linout_{n}", s, F32))
        sem = counters(nc, ctx, "linout_")
        size = GLA_KT * GLA_DV
        before = g.ring[:].rearrange("p b k n -> p (b k n)")[:, 0:2 * size].rearrange(
            "p (b t e) -> p b t e", b=2, t=GLA_KT)
        after = g.p[:, Q_TILE:R_TILE].rearrange("p k n -> p (k n)")[:, 0:3 * size].rearrange(
            "p (b t e) -> p b t e", b=3, t=GLA_KT)
        swish = sb("swish", [P, V_TILES, TOKENS])
        r = g.p[:, R_TILE:R_TILE + V_TILES]
        exped, plus_one, inverse = sem("exped"), sem("plus_one"), sem("inverse")
        gate_tiles = [slice(h * ET, (h + 1) * ET) for h in range(GLA_HEADS)]
        own_q = sb("own_q", [P, 2, GLA_KT, SAMPLED])
        own_k = sb("own_k", [SAMPLED, 2, GLA_KW])
        o_rows = sb("o_rows", [P, GLA_DV])
        o_ps = ps("o_ps", [P, 2, 512])
        state_ps = ps("state_ps", [P, 2, 512])
        few_ps = ps("few_ps", [P, 512])
        turn_ps = ps("turn_ps", [P, 512])
        loaded = [sem(f"loaded{b}") for b in range(2)]
        own_done, o_done, o_copied, state_done, state_taken, few_done, few_copied, few_turned, \
            prompt_stored = map(sem, (
            "own_done", "o_done", "o_copied", "state_done", "state_taken", "few_done", "few_copied", "few_turned",
                "prompt_stored"))
        stored = [sem(f"stored{b}") for b in range(2)]
        block = ctx.enter_context(nc.Block())
        states = a.state_gla[0].rearrange("b h k v -> b (h k) v").rearrange("b (t p) v -> b p t v", p=P)
        new_states = a.gla_sample[0].rearrange("b h k v -> b (h k) v").rearrange("b (t p) v -> b p t v", p=P)
        prompt_state = a.gla_prompt[0, 0].rearrange("h k v -> (h k) v").rearrange("(t p) v -> p t v", p=P)
        v = lambda tok, h, rows: g.v_rows[rows, tok, h * GLA_DV:(h + 1) * GLA_DV]
        owners = [[(h, rows) for h in range(GLA_HEADS) for tile, rows in head_pieces(h) if tile == t]
                  for t in range(GLA_KT)]

        def twos(eng, body):
            body(0, False)
            with eng.Fori(1, BATCH // 2 - 1) as m:
                body(m, False)
            body(BATCH // 2 - 1, True)

        @block.sync
        def _(sp):
            for b in range(2):
                sp.dma_start(before[:, b], states[b]).then_inc(loaded[b], 16)
            sp.wait_ge(state_taken, GLA_KT)
            sp.dma_start(prompt_state, after[:, 2]).then_inc(prompt_stored, 16)

            def body(m, last):
                for half in range(2):
                    sp.wait_ge(state_taken, m * (2 * GLA_KT) + GLA_KT * (half + 2))
                    sp.dma_start(new_states[bass.ds(m * 2 + half, 1)].squeeze(0), after[:, half]
                                 ).then_inc(stored[half], 16)
                    if not last:
                        sp.dma_start(before[:, half], states[bass.ds(m * 2 + (half + 2), 1)].squeeze(0)
                                     ).then_inc(loaded[half], 16)
            twos(sp, body)
            sp.wait_ge(prompt_stored, 16)
            for half in range(2):
                sp.wait_ge(stored[half], 16 * (BATCH // 2))

        @block.gpsimd
        def _(pool):
            tokens_of = g.linear_masks[:, LIN_TOKENS:LIN_TOKENS + BATCH * SAMPLED]
            rows_of = g.linear_masks[0:SAMPLED, LIN_ROWS:LIN_ROWS + BATCH]
            for h, tiles in enumerate(gate_tiles):
                pool.wait_ge(exped, h + 1)
                nc.gpsimd.tensor_scalar(swish[:, tiles], swish[:, tiles], 1.0, None, ALU.add).then_inc(plus_one, 1)

            def body(m, last):
                for half in range(2):
                    wait(pool, state_done, m * (2 * GLA_KT) + GLA_KT * half)
                    nc.gpsimd.tensor_tensor(
                        own_q[:, half], g.q_start[:],
                        tokens_of[:, bass.ds(m * (2 * SAMPLED) + half * SAMPLED, SAMPLED)].unsqueeze(1).to_broadcast(
                            [P, GLA_KT, SAMPLED]), ALU.mult)
                    nc.gpsimd.tensor_tensor(
                        own_k[:, half], g.k_rows[0:SAMPLED, QT],
                        rows_of[:, bass.ds(m * 2 + half, 1)].to_broadcast([SAMPLED, GLA_KW]), ALU.mult
                    ).then_inc(own_done, 1)
            twos(pool, body)

        @block.tensor
        def _(pe):
            for n in range(V_TILES):
                wait(pe, o_copied, n - 1)
                h = n // ET
                at = g.att[:, h].rearrange("p t i -> p (t i)")
                nc.tensor.matmul(o_ps[:, n % 2, 0:SEQ], g.v_rows[:, 0, n * P:(n + 1) * P], at[:, 0:SEQ], start=True,
                                 stop=False, skip_group_check=True)
                nc.tensor.matmul(o_ps[:, n % 2, P:SEQ], g.v_rows[:, 1, n * P:(n + 1) * P], at[:, SEQ:SEQ + P],
                                 start=False, stop=True, skip_group_check=True).then_inc(o_done, 1)
            for t in range(GLA_KT):
                wait(pe, state_taken, t - 1)
                for h, rows in owners[t]:
                    for tok in range(QT):
                        mm = nc.tensor.matmul(state_ps[rows, t % 2, 0:GLA_DV],
                                              g.k_rows[:, tok, t * P + rows.start:t * P + rows.stop],
                                              v(tok, h, slice(0, P)), start=(tok == 0), stop=(tok == QT - 1),
                                              skip_group_check=True)
                mm.then_inc(state_done, 1)
            for h in range(GLA_HEADS):
                nc.tensor.matmul(few_ps[32 * h:32 * h + 32, 0:GLA_DV], g.att[0:SAMPLED, h, 3, 0:SAMPLED],
                                 v(QT, h, slice(0, SAMPLED)), start=True, stop=False, skip_group_check=True)

            def body(m, last):
                for half in range(2):
                    pe.wait_ge(own_done, m * 2 + (half + 1))
                    pe.wait_ge(loaded[half], m * 16 + 16)
                    for e in range(2):
                        for h in range(GLA_HEADS):
                            t, rows = head_pieces(h)[e]
                            mm = nc.tensor.matmul(few_ps[32 * h:32 * h + 32, 0:GLA_DV], own_q[rows, half, t],
                                                  before[rows, half, t], start=False,
                                                  stop=(last and half == 1 and e == 1), skip_group_check=True)
                    if last and half == 1:
                        mm.then_inc(few_done, 1)
                    for t in range(GLA_KT):
                        pe.wait_ge(state_taken, m * (2 * GLA_KT) + (GLA_KT * (half + 1) + t - 1))
                        for h, rows in owners[t]:
                            mm = nc.tensor.matmul(state_ps[rows, t % 2, 0:GLA_DV],
                                                  own_k[:, half, t * P + rows.start:t * P + rows.stop],
                                                  v(QT, h, slice(0, SAMPLED)), start=True, stop=True,
                                                  skip_group_check=True)
                        mm.then_inc(state_done, 1)
            twos(pe, body)
            pe.wait_ge(few_copied, 1)
            for e in range(ET):
                mm = nc.tensor.transpose(turn_ps[:, e * P:(e + 1) * P], o_rows[:, e * P:(e + 1) * P], g.ident[:])
            mm.then_inc(few_turned, 1)

        @block.scalar
        def _(act):
            for tiles in gate_tiles:
                nc.scalar.activation(swish[:, tiles], r[:, tiles], ACT.Exp, scale=-1.0).then_inc(exped, 1)
            for n in range(V_TILES):
                act.wait_ge(o_done, n + 1)
                nc.scalar.activation(g.h[:, n, 0:SEQ], o_ps[:, n % 2, 0:SEQ], ACT.Copy).then_inc(o_copied, 1)
            act.wait_ge(few_done, 1)
            nc.scalar.activation(o_rows[:], few_ps[:, 0:GLA_DV], ACT.Copy).then_inc(few_copied, 1)
            act.wait_ge(few_turned, 1)
            for h in range(GLA_HEADS):
                nc.scalar.activation(
                    g.h[:, h * ET:(h + 1) * ET, SEQ:TOKENS],
                    turn_ps[:, 0:ET * P].rearrange("p (e n) -> p e n", e=ET)[:, :, h * SAMPLED:(h + 1) * SAMPLED],
                    ACT.Copy)

        @block.vector
        def _(dve):
            def gate(n):
                at = bass.ds(n, 1)
                nc.vector.reciprocal(swish[:, at], swish[:, at]).then_inc(inverse, 1)
                dve.wait_ge(inverse, n + 1)
                nc.vector.tensor_tensor(r[:, at], r[:, at], swish[:, at], ALU.mult)

            dve.wait_ge(plus_one, GLA_HEADS)
            for n in range(V_TILES - BATCH):
                gate(n)
            for t in range(GLA_KT):
                dve.wait_ge(state_done, t + 1)
                nc.vector.tensor_copy(after[:, 2, t], state_ps[:, t % 2, 0:GLA_DV]).then_inc(state_taken, 1)

            def body(m, last):
                for half in range(2):
                    wait(dve, stored[half], m * 16)
                    for t in range(GLA_KT):
                        dve.wait_ge(state_done, m * (2 * GLA_KT) + (GLA_KT * (half + 1) + t + 1))
                        col = g.from_start[:, t, bass.ds(m * (2 * STEP) + (half * STEP + STEP - 1), 1)]
                        nc.vector.scalar_tensor_tensor(after[:, half, t], before[:, half, t], col,
                                                       state_ps[:, t % 2, 0:GLA_DV], ALU.mult, ALU.add
                                                       ).then_inc(state_taken, 1)
                    gate(m * 2 + (half + V_TILES - BATCH))
            twos(dve, body)


def finish_linear(nc, g, next_chunks, base):
    with ExitStack() as ctx:
        sb = lambda n, s: ctx.enter_context(nc.sbuf_tensor(f"fin_{n}", s, F32))
        sem = counters(nc, ctx, "fin_")
        squares = g.p[:, V_TILE:V_TILE + V_TILES]
        rstd = sb("rstd", [P, GLA_HEADS, TOKENS])
        ps = ctx.enter_context(nc.psum_tensor("fin_ps", [P, GLA_HEADS, 512], F32))
        squared, summed, mean, root, link = map(sem, ("squared", "summed", "mean", "root", "link"))
        block = ctx.enter_context(nc.Block())
        tiles = lambda h: slice(h * ET, (h + 1) * ET)
        silu = g.p[:, R_TILE:R_TILE + V_TILES]

        @block.sync
        def _(sp):
            load_first_chunks(sp, g, next_chunks, base)

        @block.tensor
        def _(pe):
            for h in range(GLA_HEADS):
                pe.wait_ge(squared, h + 1)
                for e in range(ET):
                    mm = nc.tensor.matmul(ps[:, h, 0:TOKENS], g.ones[:], squares[:, h * ET + e], start=(e == 0),
                                          stop=(e == ET - 1))
                mm.then_inc(summed, 1)

        @block.scalar
        def _(act):
            for h in range(GLA_HEADS):
                nc.scalar.activation(squares[:, tiles(h)], g.h[:, tiles(h)], ACT.Square).then_inc(squared, 1)
            for h in range(GLA_HEADS):
                act.wait_ge(mean, h + 1)
                nc.scalar.activation(rstd[:, h], rstd[:, h], ACT.Sqrt).then_inc(root, 1)

        @block.vector
        def _(dve):
            linked = Chain(dve, link)
            for h in range(GLA_HEADS):
                dve.wait_ge(summed, h + 1)
                nc.vector.tensor_scalar(rstd[:, h], ps[:, h, 0:TOKENS], 1.0 / GLA_DV, EPS, ALU.mult, ALU.add
                                        ).then_inc(mean, 1)
            for h in range(GLA_HEADS):
                dve.wait_ge(root, h + 1)
                linked(nc.vector.reciprocal(rstd[:, h], rstd[:, h]))
                for e in range(ET):
                    gain = VEC["gla_g_o"] + e
                    last = nc.vector.scalar_tensor_tensor(g.h[:, h * ET + e], g.h[:, h * ET + e],
                                                          g.vec[:, gain:gain + 1], rstd[:, h], ALU.mult, ALU.mult)
                linked(last)
                nc.vector.tensor_tensor(g.h[:, tiles(h)], g.h[:, tiles(h)], silu[:, tiles(h)], ALU.mult)


def normalize_queries(nc, g, layer, first):
    with ExitStack() as ctx:
        sem = counters(nc, ctx, f"qnorm{layer}_")
        squares = ctx.enter_context(nc.sbuf_tensor(f"qnorm{layer}_squares", [P, MEM_HEADS, TOKENS], F32))
        gain = ctx.enter_context(nc.sbuf_tensor(f"qnorm{layer}_gain", [P, 1], F32))
        ps = ctx.enter_context(nc.psum_tensor(f"qnorm{layer}_ps", [P, MEM_HEADS, 512], F32))
        squared, summed, mean, root, link = map(sem, ("squared", "summed", "mean", "root", "link"))
        block = ctx.enter_context(nc.Block())
        q = g.p[:, first:first + MEM_HEADS]

        @block.tensor
        def _(pe):
            pe.wait_ge(squared, 1)
            for h in range(MEM_HEADS):
                mm = nc.tensor.matmul(ps[:, h, 0:TOKENS], g.ones[:], squares[:, h], start=True, stop=True)
            mm.then_inc(summed, 1)

        @block.scalar
        def _(act):
            act.wait_ge(mean, 1)
            nc.scalar.activation(squares[:], squares[:], ACT.Sqrt).then_inc(root, 1)

        @block.vector
        def _(dve):
            linked = Chain(dve, link)
            gq = VEC["g_mem_q"] + layer
            linked(nc.vector.tensor_scalar(gain[:], g.vec[:, gq:gq + 1], SCALE, None, ALU.mult))
            nc.vector.tensor_tensor(squares[:], q, q, ALU.mult).then_inc(squared, 1)
            dve.wait_ge(summed, 1)
            nc.vector.tensor_scalar(squares[:], ps[:, :, 0:TOKENS], 1.0 / HD, EPS, ALU.mult, ALU.add
                                    ).then_inc(mean, 1)
            dve.wait_ge(root, 1)
            linked(nc.vector.reciprocal(squares[:], squares[:]))
            nc.vector.scalar_tensor_tensor(q, q, gain[:], squares[:], ALU.mult, ALU.mult)


def attend_memory_prompt(nc, g, layer, p, first):
    branch = dict(width=lambda i: MEM_LEN, keys=lambda m, k: g.mem_k[layer][:, k], bias=None,
                  values=lambda k, c: g.mem_v[layer][:, c, k * HD:(k + 1) * HD])
    attend_prompt(nc, g, f"memory{layer}", 1, MEM_HEADS, lambda m, k: p[:, first + k, 0:SEQ], [branch], None,
                  lambda m, k, i: g.h[:, HEADS + k, i * P:(i + 1) * P])


def sparse_layer(nc, g, a, base):
    GATE_COL = HEADS * HD + 6 * GROUPS * HD
    gates = BRANCHES * HEADS
    normalize(nc, g, "mix0", VEC["g_mix"], (a.nsa_w_in[0], GATE_COL, gates, g.gates))
    with ExitStack() as ctx:
        sb = lambda n, s: ctx.enter_context(nc.sbuf_tensor(n, s, F32))
        g.cmp_k = sb("cmp_k", [P, PAIRS, CMP_COLS])
        g.cmp_k_prompt = sb("cmp_k_prompt", [P, GROUPS, CMP_PROMPT])
        g.cmp_v = sb("cmp_v", [P, BATCH, HD])
        g.cmp_v_prompt = sb("cmp_v_prompt", [CMP_PROMPT, GROUPS, HD])
        with nc.sbuf_tensor(
                "projected", [P, HEADS + ROW_TILES + MEM_HEADS, TOKENS], F32, side="right") as p:
            g.p = p
            base = project(nc, g, base, 7, KT, chunks_of(a.nsa_w_in[0]), ("copy", p), moving=g.h,
                           late=(1, chunks_of(a.nsa_w_in[0], gates)))
            compress(nc, g, a, 0)
            compress(nc, g, a, 1)
            g.rows_sampled = sb("rows_sampled", [SAMPLED, ROW_TILES * P])
            g.q_sampled = sb("q_sampled", [P, PAIRS, P])
            g.new_k = sb("new_k", [P, 2 * GROUPS, SAMPLED])
            g.gates_sampled = sb("gates_sampled", [P, PAIRS, BRANCHES])
            g.bias_near = sb("bias_near", [P, 132])
            g.bias_far = sb("bias_far", [P, 1])
            g.sparse_masks = sb("sparse_masks", [P, SP_COLS])
            with nc.sbuf_tensor("rows", [P, QT, ROW_TILES * P], F32) as rows, \
                    nc.sbuf_tensor("near", [P, HEADS, T_COLS], F32) as near, \
                    nc.sbuf_tensor("gates_prompt", [P, QT, gates], F32) as gates_prompt:
                g.rows, g.near, g.gates_prompt = rows, near, gates_prompt
                prepare_sparse(nc, g, a)
                for h in range(GROUPS):
                    head = lambda m, k: m * 2 + (h * HPG + k)
                    branches = [
                        dict(width=lambda i: CMP_PROMPT, keys=lambda m, k: g.cmp_k_prompt[:, h],
                             values=lambda k, c: g.cmp_v_prompt[:, h],
                             bias=lambda m, k, i: near[:, bass.ds(head(m, k), 1), P + 31 - P * i:P + 31 - P * i + 225:CMP_LEN].squeeze(1))]
                    for k_tile, v_tile in ((SEL_K, SEL_V), (WIN_K, WIN_V)):
                        branches.append(dict(
                            width=lambda i: P * (i + 1), keys=lambda m, k, t=k_tile: p[:, t + h, 0:SEQ],
                            values=lambda k, c, t=v_tile: rows[:, c, (t - HEADS + h) * HD:(t - HEADS + h + 1) * HD],
                            bias=lambda m, k, i: near[:, bass.ds(head(m, k), 1), P - P * i:2 * P].squeeze(1)))
                    attend_prompt(nc, g, f"sparse{h}", HPG // 2, 2,
                                  lambda m, k: p[:, bass.ds(head(m, k), 1), 0:SEQ].squeeze(1), branches,
                                  lambda m, k, i: gates_prompt[:, i, bass.ds(head(m, k), BRANCHES, step=HEADS)],
                                  lambda m, k, i: g.h[:, bass.ds(head(m, k), 1), i * P:(i + 1) * P].squeeze(1))
            attend_memory_prompt(nc, g, 0, p, MEM_Q)
            attend_memory_sampled(nc, g, a, 0, p[:, MEM_Q:MEM_Q + MEM_HEADS, SEQ:TOKENS],
                                  g.h[:, HEADS:KT, SEQ:TOKENS])
        attend_sampled(nc, g, a, base, chunks_of(a.w_out[0]))
    return base


def linear_layer(nc, g, a, base):
    gate_col = 2 * GLA_KW + GLA_VW
    normalize(nc, g, "mix1", VEC["g_mix"] + KT, (a.gla_w_in[0], gate_col, GATE_RANK, g.gates))
    with ExitStack() as ctx:
        sb = lambda n, s: ctx.enter_context(nc.sbuf_tensor(f"gla_{n}", s, F32))
        g.p = sb("projected", [P, 6 * GLA_KT + MEM_HEADS, TOKENS])
        w_in = a.gla_w_in[0]
        base = project(nc, g, base, 10, KT, chunks_of(w_in), ("copy", g.p), moving=g.h,
                       late=(4, chunks_of(w_in, GATE_RANK)))
        with ExitStack() as inner:
            sb = lambda n, s: inner.enter_context(nc.sbuf_tensor(f"gla_{n}", s, F32))
            g.linear_masks = sb("masks", [P, LIN_COLS])
            g.decay = sb("decay", [P, GLA_KT, TOKENS])
            g.v_rows = sb("v_rows", [P, QT + 1, GLA_VW])
            g.k_rows = sb("k_rows", [P, QT + 1, GLA_KW])
            g.from_start = sb("from_start", [P, GLA_KT, SAMPLED])
            g.q_start = sb("q_start", [P, GLA_KT, SAMPLED])
            prepare_linear(nc, g, a)
            g.att = sb("att", [P, GLA_HEADS, 4, P])
            score_levels(nc, g)
            linear_outputs(nc, g, a)
        normalize_queries(nc, g, 1, GLA_MEM_Q)
        attend_memory_prompt(nc, g, 1, g.p, GLA_MEM_Q)
        attend_memory_sampled(nc, g, a, 1, g.p[:, GLA_MEM_Q:GLA_MEM_Q + MEM_HEADS, SEQ:TOKENS],
                              g.h[:, HEADS:KT, SEQ:TOKENS])
        finish_linear(nc, g, chunks_of(a.w_out[1]), base)
    return base


def feed_forward(nc, g, a, base, layer, next_chunks, mixer):
    half = FT // 2
    w_up, w_down = a.w_up[layer], a.w_down[layer]
    up_chunks = [chunks_of(w_up, n * half * P) for n in range(2)]
    down_chunks = [chunks_of(w_down[n * half * P:(n + 1) * half * P]) for n in range(2)]
    with ExitStack() as ctx:
        sb = lambda n, tiles: ctx.enter_context(nc.sbuf_tensor(n, [P, tiles, TOKENS], F32R, side="right"))
        parts = [sb(f"{name}{layer}", KT) for name in ("high", "low")]
        base = project(nc, g, base, 4, KT, chunks_of(a.w_out[layer]), ("add", g.x), moving=g.h, parts=parts,
                       next_chunks=up_chunks[0])
        mixer.close()
        normalize(nc, g, f"mlp{layer}", VEC["g_mlp"] + layer * KT, parts=parts)
        up = [sb(f"up_{name}{layer}", half) for name in ("high", "low")]
        for n in range(2):
            base = project(nc, g, base, half // 4, KT, up_chunks[n], ("square relu", up), parts=parts,
                           next_chunks=down_chunks[n])
            base = project(nc, g, base, 4, half, down_chunks[n], ("add", g.x), parts=up,
                           next_chunks=up_chunks[1] if n == 0 else next_chunks)
    return base


def layers(nc, g, a, mixer):
    base = sparse_layer(nc, g, a, g.base)
    base = feed_forward(nc, g, a, base, 0, chunks_of(a.gla_w_in[0]), mixer)
    with ExitStack() as mixer:
        g.h = mixer.enter_context(nc.sbuf_tensor("h1", [P, KT, TOKENS], F32))
        base = linear_layer(nc, g, a, base)
        feed_forward(nc, g, a, base, 1, None, mixer)


def memory_tensors(nc, ctx, layer):
    return (ctx.enter_context(nc.sbuf_tensor(f"mem_k{layer}", [P, MEM_HEADS, MEM_LEN], F32))[:],
            ctx.enter_context(nc.sbuf_tensor(f"mem_v{layer}", [P, QT, MEM_WIDTH], F32))[:])


def build(nc, a):
    HELD.clear()
    with ExitStack() as ctx:
        sb = lambda n, s: ctx.enter_context(nc.sbuf_tensor(n, s, F32))
        g = Names()
        g.x = sb("x", [P, KT, TOKENS])
        g.ring = sb("ring", [P, RING, WTILES, WCOLS])
        g.ident = sb("ident", [P, P])
        g.ones = sb("ones", [P, P])
        g.vec = sb("vec", [P, VECS])
        g.cmp_pe = sb("cmp_pe", [P, 2 * CMP_LEN])
        g.gate_bias = sb("gate_bias", [BRANCHES * HEADS, 1])
        g.gates = sb("gates", [BRANCHES * HEADS, TOKENS])
        g.pages = ctx.enter_context(nc.sbuf_tensor("pages", [1, BATCH * PAGES], I32))
        g.bias_dram = nc.dram_tensor("bias_by_distance_dram", [HEADS, DISTS], F32, kind="Internal").ap()
        g.weights_loaded = [ctx.enter_context(nc.semaphore(f"weights_loaded{b}")) for b in range(RING)]
        g.pages_loaded = [ctx.enter_context(nc.semaphore(f"pages_loaded{b}")) for b in range(4)]
        g.weights_used = ctx.enter_context(nc.semaphore("weights_used"))

        with ExitStack() as mixer:
            second = memory_tensors(nc, ctx, 1)
            first = memory_tensors(nc, mixer, 0)
            g.mem_k, g.mem_v = zip(first, second)
            g.h = mixer.enter_context(nc.sbuf_tensor("h0", [P, KT, TOKENS], F32))
            with nc.sbuf_tensor("mem", [P, KT, MEM_LEN], F32) as mem:
                g.mem = mem
                load_tokens(nc, g, a)
                base = memory_keys_values(nc, g, a, 0, 0, chunks_of(a.w_mem_kv[1]))
                g.base = memory_keys_values(nc, g, a, base, 1, chunks_of(a.nsa_w_in[0]))
            layers(nc, g, a, mixer)
        store_tokens(nc, g, a)


_INS = ['x_prompt', 'x_sample', 'cache_nsa_kv', 'state_nsa_win', 'state_gla', 'cache_mem_kv', 'page_table',
        'mem_prompt', 'rel_bias', 'g_mix', 'g_mlp', 'g_mem', 'w_mem_kv', 'g_mem_q', 'g_mem_k', 'w_out', 'w_up',
        'w_down', 'nsa_w_in', 'nsa_gate_b', 'nsa_g_q', 'nsa_g_k', 'nsa_cmp_pe', 'nsa_cmp_w1', 'nsa_cmp_b1',
        'nsa_cmp_w2', 'gla_w_in', 'gla_w_a2', 'gla_b_a', 'gla_g_o']
_OUTS = [('y_prompt', (1, SEQ, D_MODEL)), ('y_sample', (BATCH, STEP, D_MODEL)),
         ('nsa_kv_prompt', (1, 1, SEQ, 4, GROUPS, HD)), ('nsa_win_prompt', (1, 1, SEQ, 2, GROUPS, HD)),
         ('gla_prompt', (1, 1, GLA_HEADS, GLA_DK, GLA_DV)), ('mem_kv_prompt', (2, 1, MEM_LEN, 2, MEM_HEADS, HD)),
         ('nsa_kv_sample', (1, BATCH, STEP, 4, GROUPS, HD)), ('nsa_win_sample', (1, BATCH, WINDOW, 2, GROUPS, HD)),
         ('gla_sample', (1, BATCH, GLA_HEADS, GLA_DK, GLA_DV))]


def kernel(**inputs):
    import concourse.bacc as _bacc
    from concourse.bass_utils import run_bass_kernel_spmd as _run

    nc = _bacc.Bacc("TRN2", target_bir_lowering=False, num_devices=1)
    a, arrays = Names(), {}
    named = [(name, inputs[name]) for name in _INS]
    named += list(zip(('bucket_onehot', 'sparse_masks', 'gate_rows', 'linear_masks'), shape_constants()))
    for name, value in named:
        value = np.ascontiguousarray(value)
        arrays[f"in_{name}_dram"] = value
        a.__dict__[name] = nc.dram_tensor(f"in_{name}_dram", value.shape, mybir.dt.from_np(value.dtype),
                                          kind="ExternalInput").ap()
    for name, shape in _OUTS:
        a.__dict__[name] = nc.dram_tensor(f"out_{name}_dram", shape, F32, kind="ExternalOutput").ap()
    build(nc, a)
    r = _run(nc, [arrays], core_ids=[0])
    return tuple(r.results[0][f"out_{name}_dram"] for name, _ in _OUTS)
```
